# Optimizing a Trainium2 kernel written in Bass

```python
import jax, jax.numpy as jnp
from jax import lax
import numpy as np
import math

D_MODEL = 1024
BATCH = 1
SEQ = 512
DEPTH = 2

HEAD_DIM = 64
N_GROUP_HEADS = 4
GROUP_WIDTH = N_GROUP_HEADS * HEAD_DIM
MIX_WIDTH = 4 * GROUP_WIDTH
MLA_Q_RANK = 256
MLA_KV_RANK = 128
MLA_NOPE = 64
MLA_ROPE = 32
MLA_V = 64
SWA_KV_HEADS = 2
SWA_WINDOW = 128
IDX_HEADS = 8
IDX_DIM = 32
DSA_TOPK = 256
FOX_HEADS = 4
D_FF = 4 * D_MODEL
ROPE_THETA = 10000.0
Q_BLOCK = 128
EPS = 1e-6

IN_SPLITS = (
    MLA_Q_RANK, MLA_KV_RANK, MLA_ROPE,
    GROUP_WIDTH, SWA_KV_HEADS * HEAD_DIM, SWA_KV_HEADS * HEAD_DIM,
    GROUP_WIDTH, GROUP_WIDTH, GROUP_WIDTH, IDX_HEADS * IDX_DIM, IDX_DIM, IDX_HEADS,
    GROUP_WIDTH, GROUP_WIDTH, GROUP_WIDTH, FOX_HEADS,
)
IN_WIDTH = sum(IN_SPLITS)


def rms_norm(x, g):
    xf = x.astype(jnp.float32)
    y = xf * lax.rsqrt(jnp.mean(xf * xf, axis=-1, keepdims=True) + EPS)
    return (y * g.astype(jnp.float32)).astype(x.dtype)

def rope(x, pos):
    d = x.shape[-1]
    half = d // 2
    inv_freq = 1.0 / (ROPE_THETA ** (jnp.arange(0, half, dtype=jnp.float32) * 2.0 / d))
    ang = pos[:, None] * inv_freq[None, :]
    cos = jnp.cos(ang)[:, None, :]
    sin = jnp.sin(ang)[:, None, :]
    xf = x.astype(jnp.float32)
    x1, x2 = xf[..., :half], xf[..., half:]
    out = jnp.concatenate([x1 * cos - x2 * sin, x2 * cos + x1 * sin], axis=-1)
    return out.astype(x.dtype)

def split_cols(proj):
    offs, acc = [], 0
    for n in IN_SPLITS[:-1]:
        acc += n
        offs.append(acc)
    return jnp.split(proj, offs, axis=-1)

def causal_block_attention(q, k, v, scale, log_f_cum=None):
    B, S, H, dk = q.shape
    dv = v.shape[-1]
    nb = S // Q_BLOCK
    q_blocks = q.reshape(B, nb, Q_BLOCK, H, dk).swapaxes(0, 1)
    starts = jnp.arange(nb, dtype=jnp.int32) * Q_BLOCK
    key_pos = jnp.arange(S, dtype=jnp.int32)
    if log_f_cum is None:
        xs = (q_blocks, starts)
    else:
        cum_blocks = log_f_cum.reshape(B, nb, Q_BLOCK, H).swapaxes(0, 1)
        cum_keys = log_f_cum.transpose(0, 2, 1)[:, :, None, :]
        xs = (q_blocks, starts, cum_blocks)

    def block(args):
        q_blk, start = args[0], args[1]
        s = jnp.einsum('bqhd,bkhd->bhqk', q_blk, k).astype(jnp.float32) * scale
        if log_f_cum is not None:
            s = s + (args[2].transpose(0, 2, 1)[..., None] - cum_keys)
        qpos = start + jnp.arange(Q_BLOCK, dtype=jnp.int32)
        causal = key_pos[None, :] <= qpos[:, None]
        s = jnp.where(causal, s, -jnp.inf)
        p = jax.nn.softmax(s, axis=-1).astype(v.dtype)
        return jnp.einsum('bhqk,bkhd->bqhd', p, v)

    out = lax.map(block, xs)
    return out.swapaxes(0, 1).reshape(B, S, H, dv)

def sliding_window_attention(q, k, v, sinks, scale):
    B, S, H, d = q.shape
    Hk = k.shape[2]
    G = H // Hk
    W = SWA_WINDOW
    nb = S // W
    qb = q.reshape(B, nb, W, Hk, G, d)

    def with_prev(t):
        tb = t.reshape(B, nb, W, Hk, d)
        prev = jnp.concatenate([jnp.zeros_like(tb[:, :1]), tb[:, :-1]], axis=1)
        return jnp.concatenate([prev, tb], axis=2)

    kb, vb = with_prev(k), with_prev(v)
    s = jnp.einsum('bnqkgd,bnjkd->bnkgqj', qb, kb).astype(jnp.float32) * scale
    blk = jnp.arange(nb, dtype=jnp.int32)[:, None, None]
    qi = jnp.arange(W, dtype=jnp.int32)[None, :, None]
    kj = jnp.arange(2 * W, dtype=jnp.int32)[None, None, :]
    qpos = blk * W + qi
    kpos = blk * W - W + kj
    mask = (kpos >= 0) & (kpos <= qpos) & (qpos - kpos < SWA_WINDOW)
    s = jnp.where(mask[None, :, None, None], s, -jnp.inf)
    sink = jnp.broadcast_to(sinks.astype(jnp.float32).reshape(1, 1, Hk, G, 1, 1),
                            s.shape[:-1] + (1,))
    p = jax.nn.softmax(jnp.concatenate([s, sink], axis=-1), axis=-1)[..., :-1]
    o = jnp.einsum('bnkgqj,bnjkd->bnqkgd', p.astype(v.dtype), vb)
    return o.reshape(B, S, H, d)

def dsa_attention(q, k, v, q_idx, k_idx, w_idx, top_k, scale):
    B, S, H, d = q.shape
    nb = S // Q_BLOCK

    def blocks(t):
        return t.reshape((B, nb, Q_BLOCK) + t.shape[2:]).swapaxes(0, 1)

    starts = jnp.arange(nb, dtype=jnp.int32) * Q_BLOCK
    key_pos = jnp.arange(S, dtype=jnp.int32)

    def block(args):
        q_blk, qi_blk, w_blk, start = args
        qpos = start + jnp.arange(Q_BLOCK, dtype=jnp.int32)
        rel = jax.nn.relu(jnp.einsum('bqhd,bkd->bqhk', qi_blk, k_idx).astype(jnp.float32))
        score = jnp.einsum('bqhk,bqh->bqk', rel, w_blk.astype(jnp.float32))
        score = jnp.where(key_pos[None, None, :] <= qpos[None, :, None], score, -jnp.inf)
        _, idx = lax.top_k(score, top_k)
        k_sel = jax.vmap(lambda kb, ib: kb[ib])(k, idx)
        v_sel = jax.vmap(lambda vb, ib: vb[ib])(v, idx)
        s = jnp.einsum('bqhd,bqkhd->bqhk', q_blk, k_sel).astype(jnp.float32) * scale
        valid = (idx <= qpos[None, :, None])[:, :, None, :]
        s = jnp.where(valid, s, -jnp.inf)
        p = jax.nn.softmax(s, axis=-1).astype(v.dtype)
        return jnp.einsum('bqhk,bqkhd->bqhd', p, v_sel)

    out = lax.map(block, (blocks(q), blocks(q_idx), blocks(w_idx), starts))
    return out.swapaxes(0, 1).reshape(B, S, H, d)

def first_inputs(seed: int = 0) -> dict:
    key = jax.random.key(seed)
    ks = jax.random.split(key, 16)
    H = N_GROUP_HEADS
    f32 = jnp.float32

    def nrm(k, shape, fan_in):
        return jax.random.normal(k, shape, f32) * (fan_in ** -0.5)

    def gain(k, shape):
        return 1.0 + 0.05 * jax.random.normal(k, shape, f32)

    return {
        "x": jax.random.normal(ks[0], (BATCH, SEQ, D_MODEL), f32),
        "norm1": gain(ks[1], (DEPTH, D_MODEL)),
        "w_in": nrm(ks[2], (DEPTH, D_MODEL, IN_WIDTH), D_MODEL),
        "mla_q_norm": gain(ks[3], (DEPTH, MLA_Q_RANK)),
        "mla_kv_norm": gain(ks[4], (DEPTH, MLA_KV_RANK)),
        "mla_w_uq": nrm(ks[5], (DEPTH, MLA_Q_RANK, H * (MLA_NOPE + MLA_ROPE)), MLA_Q_RANK),
        "mla_w_ukv": nrm(ks[6], (DEPTH, MLA_KV_RANK, H * (MLA_NOPE + MLA_V)), MLA_KV_RANK),
        "swa_sinks": 0.5 * jax.random.normal(ks[7], (DEPTH, H), f32),
        "fox_b_f": 0.1 * jax.random.normal(ks[8], (DEPTH, FOX_HEADS), f32),
        "w_out": nrm(ks[9], (DEPTH, MIX_WIDTH, D_MODEL), MIX_WIDTH),
        "norm2": gain(ks[10], (DEPTH, D_MODEL)),
        "w_up": nrm(ks[11], (DEPTH, D_MODEL, D_FF), D_MODEL),
        "w_down": nrm(ks[12], (DEPTH, D_FF, D_MODEL), D_FF),
        "final_norm": gain(ks[13], (D_MODEL,)),
    }

def first_block(x, norm1, w_in, mla_q_norm, mla_kv_norm, mla_w_uq, mla_w_ukv, swa_sinks,
              fox_b_f, w_out, norm2, w_up, w_down, final_norm):
    B, S, _ = x.shape
    H = N_GROUP_HEADS
    Dh = HEAD_DIM
    pos = jnp.arange(S, dtype=jnp.float32)
    top_k = min(DSA_TOPK, S // 4)
    for l in range(DEPTH):
        h = rms_norm(x, norm1[l])
        proj = h @ w_in[l]
        (a_cq, a_ckv, a_kr, b_q, b_k, b_v, c_q, c_k, c_v, c_qi, c_ki, c_w,
         d_q, d_k, d_v, d_f) = split_cols(proj)

        qa = (rms_norm(a_cq, mla_q_norm[l]) @ mla_w_uq[l]).reshape(B, S, H, MLA_NOPE + MLA_ROPE)
        q_a = jnp.concatenate([qa[..., :MLA_NOPE], rope(qa[..., MLA_NOPE:], pos)], axis=-1)
        kv = (rms_norm(a_ckv, mla_kv_norm[l]) @ mla_w_ukv[l]).reshape(B, S, H, MLA_NOPE + MLA_V)
        k_rope = rope(a_kr.reshape(B, S, 1, MLA_ROPE), pos)
        k_a = jnp.concatenate([kv[..., :MLA_NOPE],
                               jnp.broadcast_to(k_rope, (B, S, H, MLA_ROPE))], axis=-1)
        o_a = causal_block_attention(q_a, k_a, kv[..., MLA_NOPE:],
                                     (MLA_NOPE + MLA_ROPE) ** -0.5)

        q_b = rope(b_q.reshape(B, S, H, Dh), pos)
        k_b = rope(b_k.reshape(B, S, SWA_KV_HEADS, Dh), pos)
        v_b = b_v.reshape(B, S, SWA_KV_HEADS, Dh)
        o_b = sliding_window_attention(q_b, k_b, v_b, swa_sinks[l], Dh ** -0.5)

        q_c = rope(c_q.reshape(B, S, H, Dh), pos)
        k_c = rope(c_k.reshape(B, S, H, Dh), pos)
        v_c = c_v.reshape(B, S, H, Dh)
        qi = rope(c_qi.reshape(B, S, IDX_HEADS, IDX_DIM), pos)
        ki = rope(c_ki.reshape(B, S, 1, IDX_DIM), pos)[:, :, 0, :]
        o_c = dsa_attention(q_c, k_c, v_c, qi, ki, c_w, top_k, Dh ** -0.5)

        log_f = jax.nn.log_sigmoid((d_f + fox_b_f[l]).astype(jnp.float32))
        cum = lax.cumsum(log_f, axis=1)
        o_d = causal_block_attention(d_q.reshape(B, S, FOX_HEADS, Dh),
                                     d_k.reshape(B, S, FOX_HEADS, Dh),
                                     d_v.reshape(B, S, FOX_HEADS, Dh),
                                     Dh ** -0.5, log_f_cum=cum)

        mixed = jnp.concatenate([o_a.reshape(B, S, GROUP_WIDTH), o_b.reshape(B, S, GROUP_WIDTH),
                                 o_c.reshape(B, S, GROUP_WIDTH), o_d.reshape(B, S, GROUP_WIDTH)],
                                axis=-1)
        x = x + mixed @ w_out[l]

        h2 = rms_norm(x, norm2[l])
        x = x + jnp.square(jax.nn.relu(h2 @ w_up[l])) @ w_down[l]
    return rms_norm(x, final_norm)


DEPTH_2 = 1

HEADS_PER_GROUP = 8
ATTN_GROUPS = ((128, 1), (512, 4), (2048, 16))
N_GROUPS = len(ATTN_GROUPS)
N_ATTN_HEADS = N_GROUPS * HEADS_PER_GROUP
ATTN_WIDTH = HEADS_PER_GROUP * HEAD_DIM
QKV_WIDTH = N_GROUPS * 3 * ATTN_WIDTH
BLOCK = 128
POOL_WINDOWS = (2, 4, 8, 16)
POOL_GROUPS = len(POOL_WINDOWS)
POOL_WIDTH = D_MODEL // 2
PGW = POOL_WIDTH // POOL_GROUPS
NUM_BUCKETS = 32
MAX_DISTANCE = 2048
SPLIT_SIZES = (QKV_WIDTH, ATTN_WIDTH, POOL_WIDTH, POOL_WIDTH, D_MODEL, D_MODEL)
SPLIT_POINTS = (QKV_WIDTH,
                QKV_WIDTH + ATTN_WIDTH,
                QKV_WIDTH + ATTN_WIDTH + POOL_WIDTH,
                QKV_WIDTH + ATTN_WIDTH + 2 * POOL_WIDTH,
                QKV_WIDTH + ATTN_WIDTH + 2 * POOL_WIDTH + D_MODEL)
IN_WIDTH_2 = QKV_WIDTH + ATTN_WIDTH + 2 * POOL_WIDTH + 2 * D_MODEL


def rmsnorm(x, g):
    xf = x.astype(jnp.float32)
    y = xf * lax.rsqrt(jnp.mean(xf * xf, axis=-1, keepdims=True) + EPS)
    return (y * g.astype(jnp.float32)).astype(x.dtype)

def t5_bucket(n):
    max_exact = NUM_BUCKETS // 2
    nf = jnp.maximum(n, 1).astype(jnp.float32)
    large = max_exact + (jnp.log(nf / max_exact) / math.log(MAX_DISTANCE / max_exact)
                         * (NUM_BUCKETS - max_exact)).astype(jnp.int32)
    large = jnp.minimum(large, NUM_BUCKETS - 1)
    return jnp.where(n < max_exact, n, large)

def to_sub(t, dil):
    B, S = t.shape[:2]
    L = S // dil
    t = t.reshape((B, L, dil) + t.shape[2:])
    t = jnp.moveaxis(t, 2, 1)
    return t.reshape((B * dil, L) + t.shape[3:])

def from_sub(t, B, dil):
    L = t.shape[1]
    t = t.reshape((B, dil, L) + t.shape[2:])
    t = jnp.moveaxis(t, 1, 2)
    return t.reshape((B, L * dil) + t.shape[3:])

def dilated_window_attention(q, k, v, dil, n_back, bias_g):
    B, S, H, Dh = q.shape
    L = S // dil
    nb = -(-L // BLOCK)
    pad = nb * BLOCK - L
    Bd = B * dil

    def sub(t):
        return jnp.pad(to_sub(t, dil), ((0, 0), (0, pad), (0, 0), (0, 0)))

    def band(t):
        tp = jnp.pad(t, ((0, 0), (BLOCK, 0), (0, 0), (0, 0)))
        prev = tp[:, :-BLOCK].reshape(Bd, nb, BLOCK, H, Dh)
        cur = t.reshape(Bd, nb, BLOCK, H, Dh)
        return jnp.concatenate([prev, cur], axis=2)

    qb = sub(q).reshape(Bd, nb, BLOCK, H, Dh)
    kb = band(sub(k))
    vb = band(sub(v))

    i = jnp.arange(BLOCK)[:, None]
    j = jnp.arange(2 * BLOCK)[None, :]
    dist = BLOCK + i - j
    band_ok = (dist >= 0) & (dist <= n_back)
    key_ok = (jnp.arange(nb)[:, None, None] * BLOCK - BLOCK + j[None]) >= 0
    mask = band_ok[None] & key_ok
    bucket = t5_bucket(jnp.clip(dist, 0, n_back) * dil)
    bias = jnp.transpose(bias_g[bucket].astype(jnp.float32), (2, 0, 1))

    logits = jnp.einsum('znqhd,znkhd->znhqk', qb, kb).astype(jnp.float32) * (HEAD_DIM ** -0.5)
    logits = jnp.where(mask[None, :, None], logits + bias[None, None], -jnp.inf)
    m = jnp.max(logits, axis=-1, keepdims=True)
    p = jnp.exp(logits - m)
    denom = jnp.sum(p, axis=-1)
    o = jnp.einsum('znhqk,znkhd->znqhd', p.astype(vb.dtype), vb).astype(jnp.float32)
    o = o / jnp.moveaxis(denom, 2, 3)[..., None]
    lse = jnp.moveaxis(m[..., 0] + jnp.log(denom), 2, 3)

    o = o.reshape(Bd, nb * BLOCK, H, Dh)[:, :L]
    lse = lse.reshape(Bd, nb * BLOCK, H)[:, :L]
    return from_sub(o, B, dil), from_sub(lse, B, dil)

def multiscale_pool(u):
    B, S, C = u.shape
    uf = u.astype(jnp.float32)
    csp = jnp.pad(jnp.cumsum(uf, axis=1), ((0, 0), (1, 0), (0, 0)))
    t = jnp.arange(S)
    outs = []
    for g, win in enumerate(POOL_WINDOWS):
        cg = csp[:, :, g * PGW:(g + 1) * PGW]
        lo = jnp.maximum(t + 1 - win, 0)
        s = cg[:, 1:] - cg[:, lo]
        cnt = jnp.minimum(t + 1, win).astype(jnp.float32)
        outs.append(s / cnt[None, :, None])
    return jnp.concatenate(outs, axis=-1) - uf

def second_inputs(seed: int = 0) -> dict:
    key = jax.random.key(seed)
    ks = jax.random.split(key, 14)
    f32 = jnp.float32
    nrm = lambda k, shape, s: (jax.random.normal(k, shape, f32) * s).astype(f32)
    return {
        "x": nrm(ks[0], (BATCH, SEQ, D_MODEL), 1.0),
        "c": nrm(ks[1], (BATCH, D_MODEL), 1.0),
        "norm_g": 1.0 + nrm(ks[2], (DEPTH_2, D_MODEL), 0.05),
        "w_ada": nrm(ks[3], (DEPTH_2, D_MODEL, 3 * D_MODEL), 0.5 * D_MODEL ** -0.5),
        "b_ada": nrm(ks[4], (DEPTH_2, 3 * D_MODEL), 0.01),
        "w_in": nrm(ks[5], (DEPTH_2, D_MODEL, IN_WIDTH_2), D_MODEL ** -0.5),
        "pool_w": nrm(ks[6], (DEPTH_2, POOL_GROUPS, PGW, PGW), PGW ** -0.5),
        "pool_scale": 1.0 + nrm(ks[7], (DEPTH_2, POOL_WIDTH), 0.1),
        "w_attn_br": nrm(ks[8], (DEPTH_2, ATTN_WIDTH, D_MODEL), ATTN_WIDTH ** -0.5),
        "w_pool_br": nrm(ks[9], (DEPTH_2, POOL_WIDTH, D_MODEL), POOL_WIDTH ** -0.5),
        "w_out": nrm(ks[10], (DEPTH_2, D_MODEL, D_MODEL), D_MODEL ** -0.5),
        "rel_bias": nrm(ks[11], (NUM_BUCKETS, N_ATTN_HEADS), 0.5),
        "final_g": 1.0 + nrm(ks[12], (D_MODEL,), 0.05),
    }

def second_block(x, c, norm_g, w_ada, b_ada, w_in, pool_w, pool_scale, w_attn_br, w_pool_br, w_out, rel_bias, final_g):
    B, S, D = x.shape
    for l in range(DEPTH_2):
        mod = c @ w_ada[l] + b_ada[l]
        shift, scale, gate = jnp.split(mod, 3, axis=-1)
        h = rmsnorm(x, norm_g[l]) * (1.0 + scale[:, None]) + shift[:, None]

        proj = h @ w_in[l]
        qkv, z_attn, u_pool, z_pool, g_attn, g_pool = jnp.split(proj, SPLIT_POINTS, axis=-1)
        qkv = qkv.reshape(B, S, N_GROUPS, 3, HEADS_PER_GROUP, HEAD_DIM)

        outs, lses = [], []
        for gi, (win, dil) in enumerate(ATTN_GROUPS):
            bias_g = rel_bias[:, gi * HEADS_PER_GROUP:(gi + 1) * HEADS_PER_GROUP]
            o, lse = dilated_window_attention(qkv[:, :, gi, 0], qkv[:, :, gi, 1], qkv[:, :, gi, 2],
                                              dil, win // dil, bias_g)
            outs.append(o)
            lses.append(lse)
        wts = jax.nn.softmax(jnp.stack(lses, axis=0), axis=0)
        attn = jnp.sum(wts[..., None] * jnp.stack(outs, axis=0), axis=0)
        attn = attn.reshape(B, S, ATTN_WIDTH).astype(x.dtype)
        y_attn = (attn * jax.nn.silu(z_attn)) @ w_attn_br[l]

        pooled = multiscale_pool(u_pool).reshape(B, S, POOL_GROUPS, PGW)
        mixed = jnp.einsum('bsgc,gce->bsge', pooled, pool_w[l].astype(jnp.float32))
        mixed = (mixed.reshape(B, S, POOL_WIDTH) * pool_scale[l]).astype(x.dtype)
        y_pool = (mixed * jax.nn.silu(z_pool)) @ w_pool_br[l]

        merged = jax.nn.sigmoid(g_attn) * y_attn + jax.nn.sigmoid(g_pool) * y_pool
        x = x + gate[:, None] * (merged @ w_out[l])
    return rmsnorm(x, final_g)


def setup_inputs(seed=0):
    out = dict(first_inputs(seed))
    for name, value in second_inputs(seed + 1).items():
        if name != "x":
            out[name + "_2"] = value
    return out


def reference(
    x, norm1, w_in, mla_q_norm, mla_kv_norm, mla_w_uq, mla_w_ukv, swa_sinks, fox_b_f, w_out,
    norm2, w_up, w_down, final_norm, c_2, norm_g_2, w_ada_2, b_ada_2, w_in_2, pool_w_2,
    pool_scale_2, w_attn_br_2, w_pool_br_2, w_out_2, rel_bias_2, final_g_2,
):
    x = first_block(
        x, norm1, w_in, mla_q_norm, mla_kv_norm, mla_w_uq, mla_w_ukv, swa_sinks, fox_b_f, w_out,
        norm2, w_up, w_down, final_norm,
    )
    return second_block(
        x, c_2, norm_g_2, w_ada_2, b_ada_2, w_in_2, pool_w_2, pool_scale_2, w_attn_br_2,
        w_pool_br_2, w_out_2, rel_bias_2, final_g_2,
    )


_drawn_inputs = setup_inputs


def setup_inputs(seed=0):
    import zlib

    import numpy as np

    out = dict(_drawn_inputs(seed))
    spreads = {}
    factors = {'mla_q_norm': 8.0,
     'mla_kv_norm': 6.039,
     'swa_sinks': 8.0,
     'fox_b_f': 2.867,
     'norm_g_2': 3.683,
     'b_ada_2': 8.0,
     'pool_scale_2': 3.308}
    for name, (base, spread) in spreads.items():
        noise = np.random.default_rng([zlib.crc32(name.encode()), seed]).standard_normal(out[name].shape)
        drawn = base * np.exp(spread * noise) if base else spread * noise
        out[name] = __import__('jax').numpy.asarray(drawn.astype(out[name].dtype))
    for name, factor in factors.items():
        out[name] = (out[name] * factor).astype(out[name].dtype)
    return out
```

```python
from contextlib import ExitStack
import math

import numpy as np

import concourse.bass as bass
from concourse import mybir

F32 = mybir.dt.float32
F32R = mybir.dt.float32r
ALU = mybir.AluOpType
ACT = mybir.ActivationFunctionType
AX = mybir.AxisListType

P = 128
D_MODEL = 1024
SEQ = 512
DEPTH = 2
TT = SEQ // P
KT = D_MODEL // P
D_FF = 4 * D_MODEL
EPS = 1e-6
TOP_K = 128
HEADS = 4
HD = 64
MLA_ROPE = 32
MLA_QK = 96
FOX_K = HD + 2
NEG = -1e30
TAKEN = -3e38

A_COLS = (0, 416)
B_COLS = 416
C_COLS = (928, 1440)
CV_COLS = (1440, 1696)
IDX_COLS = (1696, 1992)
D_COLS = (1992, 2504)
DV_COLS = (2504, 2760)
DF_COLS = (2760, 2764)
IDX_W = IDX_COLS[1] - IDX_COLS[0]
A_W = A_COLS[1] - A_COLS[0] + 4

HALF_K = KT // 2
RAW_SLOTS = 4
SPLIT_SLOTS = 2

JOB_IDX, JOB_A, JOB_C, JOB_B, JOB_D, JOB_V = range(6)
PROJ_N = (IDX_W, A_W, 512, 512, 512, 512)
PROJ_JOBS = 6
OUT_JOB = PROJ_JOBS
FFN_JOB = OUT_JOB + 2
FFN_GROUPS = 4
GROUP_JOBS = 4
LAYER_JOBS = FFN_JOB + FFN_GROUPS * GROUP_JOBS
LAYER_UNITS = TT * LAYER_JOBS
LAYER_PIECES = 2 * LAYER_JOBS

TR_NORM1 = 0
TR_IDX = TR_NORM1 + KT
TR_MLA = TR_IDX + 3
TR_CUM = TR_MLA + 3
TR_ATT = TR_CUM + 2

PAIRS = [(g, hp) for g in "DBAC" for hp in range(2)]
ITEMS = [(p, qt) for p in range(len(PAIRS)) for qt in range(TT)]
NI = len(ITEMS)


def qk_units(p):
    return 4 if PAIRS[p][0] in "DA" else 2


def number_transposes():
    at, qk, pt = TR_ATT, {}, {}
    for n in range(qk_units(0)):
        qk[0, n] = at
        at += 1
    for i in range(NI):
        p = ITEMS[i][0]
        if i % TT == 1 and p + 1 < len(PAIRS):
            for n in range(qk_units(p + 1)):
                qk[p + 1, n] = at
                at += 1
        for e in range(2):
            pt[i, e] = at
            at += 1
    return qk, pt, at


QK_NO, PT_NO, TR_MIX = number_transposes()
TR_NORM2 = TR_MIX + KT
LAYER_TR = TR_NORM2 + KT
SM_IDX = 0
SM_EXP = 3 * 8
LAYER_SM = SM_EXP + 2 * TT
LAYER_SC = NI
LAYER_OV = NI
assert LAYER_TR % 2 == 0 and LAYER_SM % 2 == 0


def rope_tables(dim):
    half = dim // 2
    inv = (np.float32(1.0) / np.power(np.float32(10000.0), np.arange(half, dtype=np.float32) * np.float32(2.0)
                                      / np.float32(dim)).astype(np.float32)).astype(np.float32)
    ang = (np.arange(SEQ, dtype=np.float32)[:, None] * inv[None, :]).astype(np.float32).astype(np.float64)
    tab = np.stack([np.cos(ang), np.sin(ang)]).astype(np.float32)
    return np.ascontiguousarray(tab.reshape(2, TT, P, half).transpose(2, 0, 1, 3))


def mask_tables():
    i, j = np.arange(P)[:, None], np.arange(P)[None, :]
    before = np.where(j > i, 0.0, NEG)
    causal = np.where(j <= i, 0.0, NEG)
    upto = np.where(i <= j, 1.0, 0.0)
    return np.concatenate([before, causal, upto, np.ones((P, P)), np.eye(P)], axis=1).astype(np.float32)


B2_GROUPS = (1, 2, 0)
B2_WINDOW = ((128, 1), (512, 4), (2048, 16))
B2_H = 8
B2_HEADS = B2_H * len(B2_WINDOW)
STRIDE = 4
NUM_BUCKETS = 32
SKEW = 3 * P
PACK = B2_H * HD + 2 * B2_H
POOL_WINDOWS = (2, 4, 8, 16)
PAD = 16
D_ATTN = B2_H * HD
COL_QKV = 0
COL_Z = 3 * 3 * D_ATTN
COL_U = COL_Z + D_ATTN
COL_ZP = COL_U + 512
COL_GA = COL_ZP + 512
COL_GP = COL_GA + D_MODEL

ADA = 0
QKV = 6
Z_JOB, U_JOB, ZP_JOB = 15, 16, 17
GATE_JOBS = 18
BRANCH = 22
OUT2 = 24
UNIT0 = DEPTH * LAYER_UNITS
PIECE0 = DEPTH * LAYER_PIECES
TR0 = DEPTH * LAYER_TR

SM2_BIAS = DEPTH * LAYER_SM
SM2_POOL = SM2_BIAS + B2_HEADS
SC0 = DEPTH * LAYER_SC
OV0 = DEPTH * LAYER_OV
TOTAL_PIECES = PIECE0 + 2 * (OUT2 + 2)
assert TOTAL_PIECES % RAW_SLOTS == 0


def unit2(job):
    return UNIT0 + TT * job + TT * max(0, job - BRANCH if job < OUT2 else 2)


def piece2(job):
    return PIECE0 + 2 * job


def items2(g):
    if g:
        return [(g, m, 0, 4, 1) for m in range(TT)]
    return [(g, m, 2 * a, 2, 2 if m else 1) for m in range(TT) for a in range(2)]


ITEMS2 = {g: items2(g) for g in B2_GROUPS}


def item_base(g):
    return sum(len(ITEMS2[x]) for x in B2_GROUPS[:B2_GROUPS.index(g)])


TR2_NORM = TR0
TR2_ATT = TR2_NORM + KT
TR2_Z = TR2_ATT + 2 * sum(len(x) for x in ITEMS2.values())


def bucket_tables():
    hot = np.zeros((NUM_BUCKETS + 1, 3, SKEW), np.float32)
    for g, (win, dil) in enumerate(B2_WINDOW):
        step = dil if g < 2 else STRIDE
        for u in range(SKEW):
            n = (2 * P - 1 - u) * step
            if n < 0 or n % dil or n // dil > win // dil:
                hot[NUM_BUCKETS, g, u] = 1.0
                continue
            half = NUM_BUCKETS // 2
            ratio = np.log(np.float32(max(n, 1)) / np.float32(half)) / np.float32(math.log(2048 / half))
            large = min(half + int(np.float32(ratio) * np.float32(NUM_BUCKETS - half)), NUM_BUCKETS - 1)
            hot[n if n < half else large, g, u] = 1.0
    return hot


def count_table():
    t = np.arange(PAD)
    inv = np.stack([1.0 / np.minimum(t + 1, w) for w in POOL_WINDOWS])
    return np.broadcast_to(inv[None], (P, len(POOL_WINDOWS), PAD)).astype(np.float32).copy()


PROJ_PARTS = {JOB_IDX: (IDX_COLS,), JOB_A: (A_COLS, DF_COLS), JOB_C: (C_COLS,),
              JOB_B: ((416, 480), (544, 608), (480, 544), (608, 928)),
              JOB_D: (D_COLS,), JOB_V: (CV_COLS, DV_COLS)}


def loads_upto(c):
    parts = [len(PROJ_PARTS[x // 2]) if x // 2 < PROJ_JOBS else 1 for x in range(c + 1) if x % RAW_SLOTS == c % RAW_SLOTS]
    return 16 * sum(parts)


FIRST_GROUP_PIECE = 2 * FFN_JOB
LOADS_TO_GROUPS = [loads_upto(FIRST_GROUP_PIECE - RAW_SLOTS + s) for s in range(RAW_SLOTS)]
GROUP_LOADS = 16 * 2 * GROUP_JOBS // RAW_SLOTS
LAYER_LOADS = [x + FFN_GROUPS * GROUP_LOADS for x in LOADS_TO_GROUPS]
assert FIRST_GROUP_PIECE % RAW_SLOTS == 0
HI_PER_LAYER = 3 * KT
HIDDEN_UNITS = 2 * TT
LAYER_HIDDEN = FFN_GROUPS * HIDDEN_UNITS
UNITS_CREDIT, PAIR_CREDIT = TT, 2


class Steps:

    def __init__(self, eng, sem):
        self.eng, self.sem, self.n = eng, sem, 0

    def done(self, ins):
        self.n += 1
        ins.then_inc(self.sem, 1)
        self.eng.wait_ge(self.sem, self.n)

    def restart(self):
        self.eng.sem_clear(self.sem)
        self.n = 0


class Room:

    def __init__(self, nc, at):
        self.nc, self.at = nc, at

    def place(self, name, shape, dt=F32):
        t = self.nc.alloc_sbuf_tensor_at(name, shape, dt, offset=self.at)
        self.at += -(-4 * math.prod(shape[1:]) // 32) * 32
        return t


def build(nc, A, out):
    ctx = ExitStack()
    with ctx:
        def sem(name):
            return ctx.enter_context(nc.semaphore(name))

        c_rope64 = nc.inline_tensor(rope_tables(HD), "rope64_table")
        c_rope32 = nc.inline_tensor(rope_tables(MLA_ROPE), "rope32_table")
        c_mask = nc.inline_tensor(mask_tables(), "mask_table")
        c_hot = nc.inline_tensor(bucket_tables(), "bucket_table")
        c_count = nc.inline_tensor(count_table(), "count_table")
        skew_dram = nc.dram_tensor("skew_scratch", [B2_HEADS, P, SKEW], F32, kind="Internal").ap()
        merge_dram = nc.dram_tensor("merge_scratch", [SEQ, PACK], F32, kind="Internal").ap()

        base = Room(nc, -(-nc.sbuf_base // 64) * 64)
        X = base.place("X", [P, TT, D_MODEL])
        raw = base.place("raw", [P, RAW_SLOTS, HALF_K, 512])
        w_hi = base.place("w_hi", [P, SPLIT_SLOTS, HALF_K, 512], F32R)
        w_lo = base.place("w_lo", [P, SPLIT_SLOTS, HALF_K, 512], F32R)
        masks = base.place("masks", [P, 5 * P])
        window, causal, upto = masks[:, 0:2 * P], masks[:, P:2 * P], masks[:, 2 * P:3 * P]
        ones, ident = masks[:, 3 * P:4 * P], masks[:, 4 * P:5 * P]
        rope64 = base.place("rope64", [P, 2, TT, HD // 2])
        rope32 = base.place("rope32", [P, 2, TT, MLA_ROPE // 2])
        gain1, gain2 = base.place("gain1", [P, KT]), base.place("gain2", [P, KT])
        q_gain, kv_gain = base.place("q_gain", [P, 2]), base.place("kv_gain", [P, 1])
        sinks, gate_bias = base.place("sinks", [P, HEADS]), base.place("gate_bias", [P, HEADS])
        sumsq, var, std = (base.place(n, [P, TT]) for n in ("sumsq", "var", "std"))
        rstd, newton = (base.place(n, [P, TT]) for n in ("rstd", "newton"))
        m_sumsq, m_var, m_std, m_rstd, m_newton = (
            base.place(n, [P, 2 * TT]) for n in ("m_sumsq", "m_var", "m_std", "m_rstd", "m_newton"))
        top8 = base.place("top8", [P, 8])
        row_max, neg_max = base.place("row_max", [P, 2, 2]), base.place("neg_max", [P, 2, 2])
        row_sum, sink_term = base.place("row_sum", [P, 4, 2]), base.place("sink_term", [P, 4, 2])
        inv_sum = base.place("inv_sum", [P, 4, 2])
        hT_at = base.at
        room = Room(nc, hT_at)
        h_hi, h_lo = room.place("h_hi", [P, KT, SEQ], F32R), room.place("h_lo", [P, KT, SEQ], F32R)
        free_at = room.at
        room = Room(nc, hT_at)
        qkT = room.place("qkT", [P, 2, 4, SEQ])
        prob = room.place("prob", [P, 2, 2, SEQ])
        probT = room.place("probT", [P, 2, 2, SEQ])
        assert room.at <= free_at

        room = Room(nc, free_at)
        rows_idx = room.place("rows_idx", [P, TT, IDX_W])
        rows_a = room.place("rows_a", [P, TT, A_W])
        xn_at = room.at
        rows_b, rows_c = room.place("rows_b", [P, TT, 512]), room.place("rows_c", [P, TT, 512])
        early = Room(nc, room.at)
        cqT, ckvT = early.place("cqT", [P, 2, SEQ]), early.place("ckvT", [P, SEQ])
        rows_v = room.place("rows_v", [P, TT, 512])
        assert early.at <= room.at
        fox_q, fox_k = (room.place(n, [P, TT, HEADS, FOX_K]) for n in ("fox_q", "fox_k"))
        mla_q, mla_k = (room.place(n, [P, TT, HEADS, MLA_QK]) for n in ("mla_q", "mla_k"))
        mla_v = room.place("mla_v", [P, TT, HEADS * HD])
        w_uq, w_ukv = room.place("w_uq", [P, 2, HEADS * MLA_QK]), room.place("w_ukv", [P, HEADS * 2 * HD])
        k_idx4 = room.place("k_idx4", [P, TT, 4 * 32])
        qiT, kiT = room.place("qiT", [P, 2, SEQ]), room.place("kiT", [P, SEQ])
        select = room.place("select", [P, (2 + 3 + 4) * P])
        work, rel = room.place("work", [P, SEQ]), room.place("rel", [P, 2, SEQ])
        turn = room.place("turn", [P, 4, 8 * HD // 2])
        gate_z, gate_a, gate_e, log_f = (
            room.place(n, [P, TT, HEADS]) for n in ("gate_z", "gate_a", "gate_e", "log_f"))
        room = Room(nc, xn_at)
        xn = room.place("xn", [P, TT, D_MODEL])
        u_hi, u_lo = room.place("u_hi", [P, KT, SEQ], F32R), room.place("u_lo", [P, KT, SEQ], F32R)
        relu, square = room.place("relu", [P, 2, SEQ]), room.place("square", [P, SEQ])
        room = Room(nc, free_at)
        xn2 = room.place("xn2", [P, TT, D_MODEL])
        cb_hi, cb_lo = room.place("cb_hi", [P, KT, P], F32R), room.place("cb_lo", [P, KT, P], F32R)
        h_full = room.place("h_full", [P, 2, SEQ])
        hot = room.place("hot", [P, 3, SKEW])
        stage_at = room.at
        stage = room.place("stage", [P, B2_HEADS, SKEW])
        rel_wide = room.place("rel_wide", [P, B2_HEADS, P])
        last_at = room.at
        room = Room(nc, free_at)
        qkv = room.place("qkv", [P, 16, SEQ])
        assert room.at <= stage_at
        room = Room(nc, stage_at)
        bias_far = room.place("bias_far", [P, 2, B2_H, P])
        bias_near = room.place("bias_near", [P, B2_H, 2 * P])
        prob2, probT2 = room.place("prob2", [P, 2, 2, SEQ]), room.place("probT2", [P, 2, 2, SEQ])
        sum_a, sum_b = room.place("sum_a", [P, TT, PACK]), room.place("sum_b", [P, TT, PACK])
        last_at = max(last_at, room.at)
        room = Room(nc, stage_at)
        at_hi, at_lo = room.place("at_hi", [P, 4, SEQ], F32R), room.place("at_lo", [P, 4, SEQ], F32R)
        pt_hi, pt_lo = room.place("pt_hi", [P, 4, SEQ], F32R), room.place("pt_lo", [P, 4, SEQ], F32R)
        win = room.place("win", [P, 3, PAD + SEQ])
        pool_w = room.place("pool_w", [P, 4, P])
        assert room.at <= last_at
        room = Room(nc, last_at)
        gate_row, gain_row = room.place("gate_row", [P, D_MODEL]), room.place("gain_row", [P, D_MODEL])
        rel_row = room.place("rel_row", [P, B2_HEADS])
        mod_b, mod = room.place("mod_b", [P, 2 * KT]), room.place("mod", [P, 2 * KT])
        norm_col, c_col, pool_gain = (
            room.place(n, [P, k]) for n, k in (("norm_col", KT), ("c_col", KT), ("pool_gain", 4)))
        inv_count = room.place("inv_count", [P, len(POOL_WINDOWS), PAD])
        head_max, head_neg, head_sum = (
            room.place(n, [P, 3, TT, B2_H]) for n in ("head_max", "head_neg", "head_sum"))
        best, part_a, part_b = (room.place(n, [P, TT, B2_H]) for n in ("best", "part_a", "part_b"))

        G = ctx.enter_context(nc.psum_tensor("G", [P, 4, 512], F32))
        S = ctx.enter_context(nc.psum_tensor("S", [P, 4, 512], F32))

        x_loaded, const_loaded = sem("x_loaded"), sem("const_loaded")
        slots_cleared = sem("slots_cleared")
        params_loaded, mla_w_loaded = sem("params_loaded"), sem("mla_w_loaded")
        raw_loaded = [sem(f"raw_loaded{i}") for i in range(RAW_SLOTS)]
        high_ready, low_ready = sem("high_ready"), sem("low_ready")
        pieces_asked = sem("pieces_asked")
        half_used = sem("half_used")
        bank_filled, bank_drained = sem("bank_filled"), sem("bank_drained")
        tr_filled, tr_drained = sem("tr_filled"), sem("tr_drained")
        small_filled, small_drained = sem("small_filled"), sem("small_drained")
        score_filled, score_drained = sem("score_filled"), sem("score_drained")
        o_filled, o_drained = sem("o_filled"), sem("o_drained")
        sumsq_ready, var_ready, std_ready, xn_ready = (
            sem(n) for n in ("sumsq_ready", "var_ready", "std_ready", "xn_ready"))
        m_sumsq_ready, m_var_ready, m_std_ready, m_rows_ready = (
            sem(n) for n in ("m_sumsq_ready", "m_var_ready", "m_std_ready", "m_rows_ready"))
        hi_ready = sem("hi_ready")
        idx_rows_ready, gate_abs_ready, gate_exp_ready, log_f_ready = (
            sem(n) for n in ("idx_rows_ready", "gate_abs_ready", "gate_exp_ready", "log_f_ready"))
        fox_ready, mla_ready, heads_ready = sem("fox_ready"), sem("mla_ready"), sem("heads_ready")
        rel_used, neg_max_ready, hidden_split = sem("rel_used"), sem("neg_max_ready"), sem("hidden_split")
        act_step, dve_step = sem("act_step"), sem("dve_step")
        b2_loaded, gain2_loaded, c_ready = sem("b2_loaded"), sem("gain2_loaded"), sem("c_ready")
        rel_ready, stage_ready, skew_saved, bias_loaded = (
            sem(n) for n in ("rel_ready", "stage_ready", "skew_saved", "bias_loaded"))
        x_scaled, hot_loaded, pool_w_loaded = sem("x_scaled"), sem("hot_loaded"), sem("pool_w_loaded")
        mod_ready, full_ready, neg2_ready, prob2_ready = (
            sem(n) for n in ("mod_ready", "full_ready", "neg2_ready", "prob2_ready"))
        combine_max, combine_exp = sem("combine_max"), sem("combine_exp")
        pack_ready, pack_saved, pack_loaded = sem("pack_ready"), sem("pack_saved"), sem("pack_loaded")
        z_rows_ready, sigma_ready, pooled_ready = sem("z_rows_ready"), sem("sigma_ready"), sem("pooled_ready")
        split_ready, out_ready, out_saved = sem("split_ready"), sem("out_ready"), sem("out_saved")

        block = ctx.enter_context(nc.Block())

        def weights2(job, half):
            if job < QKV:
                w, c0, k0 = A["w_ada_2"], 512 * job, half * HALF_K
            elif job < Z_JOB:
                g, s = B2_GROUPS[(job - QKV) // 3], (job - QKV) % 3
                w, c0, k0 = A["w_in_2"], COL_QKV + (3 * g + s) * D_ATTN, half * HALF_K
            elif job < BRANCH:
                c0 = {Z_JOB: COL_Z, U_JOB: COL_U, ZP_JOB: COL_ZP, GATE_JOBS: COL_GA, GATE_JOBS + 1: COL_GA + 512,
                      GATE_JOBS + 2: COL_GP, GATE_JOBS + 3: COL_GP + 512}[job]
                w, k0 = A["w_in_2"], half * HALF_K
            elif job < OUT2:
                w, c0, k0 = A["w_pool_br_2"] if half else A["w_attn_br_2"], 512 * (job - BRANCH), 0
            else:
                w, c0, k0 = A["w_out_2"], 512 * (job - OUT2), half * HALF_K
            return w[0, k0 * P:(k0 + HALF_K) * P, c0:c0 + 512].rearrange("(k p) n -> p k n", p=P)

        def skewed(h0, heads, first, width):
            return bass.AP(tensor=skew_dram.tensor, offset=h0 * P * SKEW + P - 1 + first,
                           ap=[[SKEW - 1, P], [P * SKEW, heads], [1, width]])

        def second_loads(sp):
            sp.wait_ge(tr_drained, TR0 + PAIR_CREDIT)
            column = lambda v: v.rearrange("(k p) -> p k", p=P)
            for dst, src in (
                (c_col[:], column(A["c_2"][0, :])),
                (rel_row[0:NUM_BUCKETS, :], A["rel_bias_2"]),
                (gain_row[:], A["final_norm"].unsqueeze(0).broadcast_to([P, D_MODEL])),
                (norm_col[:], column(A["norm_g_2"][0, :])),
                (mod_b[:], column(A["b_ada_2"][0, 0:2 * D_MODEL])),
                (gate_row[:], A["b_ada_2"][0:1, 2 * D_MODEL:3 * D_MODEL].broadcast_to([P, D_MODEL])),
                (pool_gain[:], column(A["pool_scale_2"][0, :])),
                (inv_count[:], c_count[:, :, :]),
            ):
                sp.dma_start(dst, src, allow_slow_non_contiguous=True).then_inc(b2_loaded, 16)
            for job in range(OUT2 + 2):
                for half in range(2):
                    c = 2 * job + half
                    sp.wait_ge(low_ready, PIECE0 + c + 1)
                    sp.dma_start(raw[:, c % RAW_SLOTS], weights2(job, half)).then_inc(raw_loaded[c % RAW_SLOTS], 16)
                if job == 1:
                    sp.wait_ge(bank_drained, UNIT0 + UNITS_CREDIT)
                    sp.dma_start(hot[0:NUM_BUCKETS + 1], c_hot[:, :, :]).then_inc(hot_loaded, 16)
                if job == QKV:
                    sp.wait_ge(small_drained, SM2_BIAS + B2_HEADS + PAIR_CREDIT)
                    sp.dma_start(skew_dram.rearrange("h p u -> p h u"), stage[:]).then_inc(skew_saved, 16)
                    sp.wait_ge(x_scaled, 1)
                    sp.dma_start(gain_row[:], A["final_g_2"].unsqueeze(0).broadcast_to([P, D_MODEL])
                                 ).then_inc(gain2_loaded, 16)
                    sp.wait_ge(skew_saved, 16)
                    for g in (1, 2):
                        sp.dma_start(bias_far[:, g - 1], skewed(g * B2_H, B2_H, P, P)).then_inc(bias_loaded, 16)
                    sp.dma_start(bias_near[:], skewed(0, B2_H, 0, 2 * P)).then_inc(bias_loaded, 16)
                if job == QKV + 7:
                    sp.wait_ge(pack_ready, 1)
                    sp.dma_start(merge_dram.rearrange("(p m) c -> p m c", m=STRIDE), sum_a[:]).then_inc(pack_saved, 16)
                    sp.wait_ge(pack_saved, 16)
                    sp.dma_start(sum_b[:], merge_dram.rearrange("(t p) c -> p t c", p=P)).then_inc(pack_loaded, 16)
                if job == ZP_JOB:
                    sp.wait_ge(z_rows_ready, 1)
                    sp.dma_start(pool_w[:], A["pool_w_2"][0].rearrange("g c e -> c g e")).then_inc(pool_w_loaded, 16)
            for t in range(TT):
                sp.wait_ge(out_ready, t + 1)
                sp.dma_start(out[0, P * t:P * t + P, :], X[:, t, :]).then_inc(out_saved, 16)
            sp.wait_ge(out_saved, 16 * TT)

        def own(g, v, blocks):
            return v[:, :, P:2 * P] if not g and blocks == 1 else v

        def by_tile(g, v):
            return v.rearrange("p (n w) -> p n w", w=P if g else 2 * P)

        def second_scalar(act, split_high, square_sums):
            def ahead(job, half):
                c = 2 * (job + 1) + half
                s = c % RAW_SLOTS
                act.wait_ge(raw_loaded[s], DEPTH * LAYER_LOADS[s] + 16 * (c // RAW_SLOTS + 1))
                if half:
                    act.wait_ge(bank_filled, unit2(job + 1))
                elif BRANCH <= job < OUT2:
                    act.wait_ge(bank_filled, unit2(job) + TT)
                else:
                    act.wait_ge(half_used, DEPTH * LAYER_JOBS + job + 1 - (2 if job >= OUT2 else 0))
                act.activation(w_hi[:, c % SPLIT_SLOTS], raw[:, c % RAW_SLOTS], ACT.Copy).then_inc(high_ready, 1)

            def columns_out(job, place, func=ACT.Copy, scale=1.0):
                for t in range(TT):
                    act.wait_ge(bank_filled, unit2(job) + t + 1)
                    act.activation(qkv[:, place + t, :], G[:, t, :], func, scale=scale).then_inc(bank_drained, 1)

            def bias_rows(job):
                for h in range(4 * job, 4 * job + 4):
                    act.wait_ge(small_filled, SM2_BIAS + h + 1)
                    act.activation(stage[:, h, :], S[:, h % 2, 0:SKEW], ACT.Copy).then_inc(small_drained, 1)

            act.wait_ge(bank_drained, UNIT0 + UNITS_CREDIT)
            ahead(ADA, 0)
            square_sums(2 * DEPTH, xn2)
            ahead(ADA, 1)
            bias_rows(0)
            ahead(ADA + 1, 0)
            act.wait_ge(x_scaled, 1)
            square_sums(2 * DEPTH + 1, xn2)
            ahead(ADA + 1, 1)
            bias_rows(1)
            for job in range(2, QKV):
                ahead(job, 0)
                ahead(job, 1)
                bias_rows(job)
            act.wait_ge(mod_ready, 1)
            for k in range(KT):
                act.wait_ge(tr_filled, TR2_NORM + k + 1)
                act.activation(h_full[:, k % 2, :], S[:, 2 + k % 2, :], ACT.Identity, scale=mod[:, KT + k:KT + k + 1],
                               bias=mod[:, k:k + 1]).then_inc(full_ready, 1)
            for gn, g in enumerate(B2_GROUPS):
                for s in range(3):
                    job = QKV + 3 * gn + s
                    ahead(job, 0)
                    if gn == 0 and s == 0:
                        act.wait_ge(skew_saved, 16)
                    columns_out(job, 4 * s)
                    ahead(job, 1)
                for i, (_, m, tile0, tiles, blocks) in enumerate(ITEMS2[g]):
                    it = item_base(g) + i
                    act.wait_ge(neg2_ready, it + 1)
                    for e in range(2):
                        part = own(g, by_tile(g, prob2[:, it % 2, e, :]), blocks)
                        for n in range(tiles):
                            h = 2 * (tile0 + n) + e
                            ins = act.activation(part[:, n, :], part[:, n, :], ACT.Exp,
                                                 bias=head_neg[:, g, m, h:h + 1],
                                                 accum_out=head_sum[:, g, m, h:h + 1])
                    ins.then_inc(prob2_ready, 1)
                if g != B2_GROUPS[0]:
                    n = gn
                    act.wait_ge(combine_max, n)
                    act.activation(part_a[:], part_a[:], ACT.Exp)
                    act.activation(part_b[:], part_b[:], ACT.Exp).then_inc(combine_exp, 1)

            def negative_exps(job, place, first):
                for t in range(TT):
                    act.wait_ge(bank_filled, unit2(job) + t + 1)
                    act.activation(qkv[:, place + t, :], G[:, t, :], ACT.Exp, scale=-1.0).then_inc(sigma_ready, 1)

            ahead(Z_JOB, 0)
            negative_exps(Z_JOB, 0, 0)
            ahead(Z_JOB, 1)
            ahead(U_JOB, 0)
            columns_out(U_JOB, 4)
            ahead(U_JOB, 1)
            ahead(ZP_JOB, 0)
            negative_exps(ZP_JOB, 8, TT)
            ahead(ZP_JOB, 1)
            for n in range(4):
                ahead(GATE_JOBS + n, 0)
                if n == 0:
                    act.wait_ge(split_ready, 1)
                columns_out(GATE_JOBS + n, 4 * n, ACT.Exp, -1.0)
                ahead(GATE_JOBS + n, 1)
            for job in range(BRANCH, OUT2 + 1):
                ahead(job, 0)
                ahead(job, 1)
            act.wait_ge(x_scaled, 2)
            square_sums(2 * DEPTH + 2, xn2)

        def second_vector(dve, step, root, normal_rows):
            dve.wait_ge(b2_loaded, 8 * 16)
            wide = c_col[:].unsqueeze(2).broadcast_to([P, KT, P])
            step.done(dve.tensor_copy(cb_hi[:], wide))
            dve.tensor_tensor(cb_lo[:], wide, cb_hi[:].bitcast(F32), ALU.subtract).then_inc(c_ready, 1)
            step.done(dve.memset(rel_row[NUM_BUCKETS:NUM_BUCKETS + 1, :], NEG))
            dve.tensor_copy(rel_wide[0:NUM_BUCKETS + 1], rel_row[0:NUM_BUCKETS + 1, :].unsqueeze(2).broadcast_to(
                [NUM_BUCKETS + 1, B2_HEADS, P])).then_inc(rel_ready, 1)

            def scaled_rows(norm_no):
                dve.wait_ge(sumsq_ready, norm_no + 1)
                dve.tensor_scalar(var[:], sumsq[:], 1.0 / D_MODEL, EPS, ALU.mult, ALU.add).then_inc(var_ready, 1)
                dve.wait_ge(std_ready, norm_no + 1)
                root(var[:], std[:], rstd[:], newton[:])
                for t in range(TT):
                    yield dve.scalar_tensor_tensor(X[:, t, :], X[:, t, :], rstd[:, t:t + 1], gain_row[:], ALU.mult, ALU.mult)

            def modulation(job):
                for t in range(TT):
                    dve.wait_ge(bank_filled, unit2(job) + t + 1)
                    if job < 4:
                        at = slice(4 * job + t, 4 * job + t + 1)
                        ins = dve.tensor_tensor(mod[:, at], G[:, t, 0:1], mod_b[:, at], ALU.add)
                    else:
                        at = slice(512 * (job - 4) + P * t, 512 * (job - 4) + P * t + P)
                        ins = dve.tensor_tensor(gate_row[:, at], G[:, t, 0:P], gate_row[:, at], ALU.add)
                    ins.then_inc(bank_drained, 1)

            for ins in scaled_rows(2 * DEPTH):
                pass
            ins.then_inc(x_scaled, 1)
            dve.wait_ge(x_scaled, 1)
            modulation(0)
            normal_rows(2 * DEPTH + 1, xn2).then_inc(xn_ready, 1)
            for job in range(1, 4):
                modulation(job)
            dve.wait_ge(bank_drained, unit2(4) + UNITS_CREDIT)
            dve.scalar_tensor_tensor(mod[:, KT:2 * KT], mod[:, KT:2 * KT], 1.0, norm_col[:], ALU.add,
                                     ALU.mult).then_inc(mod_ready, 1)
            for job in range(4, QKV):
                modulation(job)
            for k in range(KT):
                dve.wait_ge(full_ready, k + 1)
                step.done(dve.tensor_copy(h_hi[:, k, :], h_full[:, k % 2, :]))
                dve.tensor_tensor(h_lo[:, k, :], h_full[:, k % 2, :], h_hi[:, k, :].bitcast(F32),
                                  ALU.subtract).then_inc(tr_drained, 1)

            def row_maxima(g, i):
                it = item_base(g) + i
                _, m, tile0, tiles, blocks = ITEMS2[g][i]
                dve.wait_ge(score_filled, SC0 + it + 1)
                for e in range(2):
                    table = bias_far[:, g - 1] if g else bias_near[:]
                    heads = slice(2 * tile0 + e, 2 * (tile0 + tiles) + e - 1, 2)
                    ins = dve.scalar_tensor_tensor(
                        own(g, by_tile(g, prob2[:, it % 2, e, :]), blocks),
                        own(g, by_tile(g, S[:, 2 * (it % 2) + e, :]), blocks), HD ** -0.5,
                        own(g, table[:, heads, :], blocks), ALU.mult, ALU.add)
                ins.then_inc(score_drained, 1)
                dve.wait_ge(score_drained, SC0 + it + 1 + PAIR_CREDIT)
                for e in range(2):
                    heads = slice(2 * tile0 + e, 2 * (tile0 + tiles) + e - 1, 2)
                    ins = dve.tensor_reduce(head_max[:, g, m, heads], own(g, by_tile(g, prob2[:, it % 2, e, :]), blocks),
                                            AX.X, ALU.max)
                step.done(ins)
                heads = slice(2 * tile0, 2 * (tile0 + tiles))
                dve.tensor_scalar(head_neg[:, g, m, heads], head_max[:, g, m, heads], -1.0, None,
                                  ALU.mult).then_inc(neg2_ready, 1)

            def take_probs(g, i):
                it = item_base(g) + i
                blocks = ITEMS2[g][i][4]
                if it >= 2:
                    dve.wait_ge(o_filled, OV0 + it - 1)
                for e in range(2):
                    dve.wait_ge(tr_filled, TR2_ATT + 2 * it + e + 1)
                    dve.tensor_copy(own(g, by_tile(g, probT2[:, it % 2, e, :]), blocks),
                                    own(g, by_tile(g, G[:, e, :]), blocks)).then_inc(tr_drained, 1)

            def take_output(g, i):
                it = item_base(g) + i
                _, m, tile0, tiles, _ = ITEMS2[g][i]
                dve.wait_ge(o_filled, OV0 + it + 1)
                n = 2 * HD * tiles
                rows = sum_b if g == 2 else sum_a
                dve.tensor_copy(rows[:, m, 2 * HD * tile0:2 * HD * tile0 + n], G[:, 2 + it % 2, 0:n]).then_inc(o_drained, 1)

            ov, om, od = slice(0, D_ATTN), slice(D_ATTN, D_ATTN + B2_H), slice(D_ATTN + B2_H, PACK)

            def heads_of(v):
                return v.rearrange("p (h d) -> p h d", h=B2_H)

            def combine(no, m_a, d_a, m_b, d_b, last):
                step.done(dve.tensor_tensor(best[:], m_a, m_b, ALU.max))
                dve.tensor_tensor(part_a[:], m_a, best[:], ALU.subtract)
                dve.tensor_tensor(part_b[:], m_b, best[:], ALU.subtract).then_inc(combine_max, 1)
                dve.wait_ge(combine_exp, no)
                dve.tensor_tensor(d_a, d_a, part_a[:], ALU.mult)
                step.done(dve.tensor_tensor(d_b, d_b, part_b[:], ALU.mult))
                total = head_sum[:, 0] if last else sum_a[:, :, od]
                step.done(dve.tensor_tensor(total, d_a, d_b, ALU.add))
                if last:
                    step.done(dve.reciprocal(best[:], total))
                    dve.tensor_tensor(part_a[:], part_a[:], best[:], ALU.mult)
                    step.done(dve.tensor_tensor(part_b[:], part_b[:], best[:], ALU.mult))
                else:
                    dve.tensor_copy(sum_a[:, :, om], best[:])
                for rows, part in ((sum_a, part_a), (sum_b, part_b)):
                    for t in range(TT):
                        ins = dve.tensor_tensor(heads_of(rows[:, t, ov]), heads_of(rows[:, t, ov]),
                                                part[:, t, :].unsqueeze(2).broadcast_to([P, B2_H, HD]), ALU.mult)
                step.done(ins)
                for t in range(TT):
                    dst = qkv[:, 12 + t, :] if last else sum_a[:, t, ov]
                    ins = dve.tensor_tensor(dst, sum_a[:, t, ov], sum_b[:, t, ov], ALU.add)
                return ins

            dve.wait_ge(bias_loaded, 3 * 16)
            for gn, g in enumerate(B2_GROUPS):
                row_maxima(g, 0)
                n = len(ITEMS2[g])
                for i in range(n):
                    if i + 1 < n:
                        row_maxima(g, i + 1)
                    take_probs(g, i)
                    if i:
                        if g == 0 and i == 1:
                            dve.wait_ge(pack_saved, 16)
                        take_output(g, i - 1)
                take_output(g, n - 1)
                dve.wait_ge(o_drained, OV0 + item_base(g) + n + PAIR_CREDIT)
                if gn == 1:
                    combine(1, head_max[:, 1], head_sum[:, 1], head_max[:, 2], head_sum[:, 2], False
                            ).then_inc(pack_ready, 1)
            dve.wait_ge(pack_loaded, 16)
            step.done(combine(2, head_max[:, 0], head_sum[:, 0], sum_b[:, :, om], sum_b[:, :, od], True))

            def gated(job, place, first):
                for t in range(TT):
                    dve.wait_ge(sigma_ready, first + t + 1)
                    e = qkv[:, place + t, :]
                    step.done(dve.tensor_scalar(e, e, 1.0, None, ALU.add))
                    step.done(dve.reciprocal(e, e))
                    dve.tensor_tensor(e, e, G[:, t, :], ALU.mult).then_inc(bank_drained, 1)
                dve.wait_ge(bank_drained, unit2(job + 1) + UNITS_CREDIT)

            def two_parts(hi, lo, src):
                step.done(dve.tensor_copy(hi, src))
                return dve.tensor_tensor(lo, src, hi.bitcast(F32), ALU.subtract)

            gated(Z_JOB, 0, 0)
            for t in range(TT):
                ins = dve.tensor_tensor(qkv[:, 12 + t, :], qkv[:, 12 + t, :], qkv[:, t, :], ALU.mult)
            ins.then_inc(z_rows_ready, 1)
            for k in range(4):
                dve.wait_ge(tr_filled, TR2_Z + k + 1)
                two_parts(at_hi[:, k, :], at_lo[:, k, :], S[:, 2 + k % 2, :]).then_inc(tr_drained, 1)
            step.done(dve.memset(win[:, :, 0:PAD], 0.0))
            dve.wait_ge(bank_drained, unit2(U_JOB + 1) + UNITS_CREDIT)
            dve.wait_ge(tr_drained, TR2_Z + 4 + PAIR_CREDIT)
            for g, w in enumerate(POOL_WINDOWS):
                u, pooled = qkv[:, 4 + g, :], qkv[:, 12 + g, :]
                step.done(dve.tensor_copy(win[:, 0, PAD:], u))
                at = 0
                for n in range(g + 1):
                    step.done(dve.tensor_tensor(win[:, 1 + n % 2, PAD:], win[:, at, PAD:],
                                                win[:, at, PAD - 2 ** n:PAD + SEQ - 2 ** n], ALU.add))
                    at = 1 + n % 2
                step.done(dve.scalar_tensor_tensor(pooled, win[:, at, PAD:], 1.0 / w, u, ALU.mult, ALU.subtract))
                step.done(dve.tensor_tensor(win[:, at, PAD:2 * PAD], win[:, at, PAD:2 * PAD], inv_count[:, g, :], ALU.mult))
                ins = dve.tensor_tensor(pooled[:, 0:PAD], win[:, at, PAD:2 * PAD], u[:, 0:PAD], ALU.subtract)
                ins.then_inc(pooled_ready, 1)
                dve.wait_ge(pooled_ready, g + 1)
            gated(ZP_JOB, 8, TT)
            for g in range(4):
                dve.wait_ge(small_filled, SM2_POOL + g + 1)
                full = win[:, g % 2, PAD:]
                dve.scalar_tensor_tensor(full, S[:, g % 2, :], pool_gain[:, g:g + 1], qkv[:, 8 + g, :], ALU.mult,
                                         ALU.mult).then_inc(small_drained, 1)
                dve.wait_ge(small_drained, SM2_POOL + g + 1 + PAIR_CREDIT)
                step.done(two_parts(pt_hi[:, g, :], pt_lo[:, g, :], full))
            dve.engine_nop().then_inc(split_ready, 1)
            for n in range(4):
                for t in range(TT):
                    dve.wait_ge(bank_drained, unit2(GATE_JOBS + n) + t + 1 + UNITS_CREDIT)
                    e = qkv[:, 4 * n + t, :]
                    step.done(dve.tensor_scalar(e, e, 1.0, None, ALU.add))
                    step.done(dve.reciprocal(e, e))
            for e in range(2):
                for t in range(TT):
                    a = qkv[:, 4 * e + t, :]
                    dve.wait_ge(bank_filled, unit2(BRANCH + e) + t + 1)
                    dve.tensor_tensor(a, a, G[:, t, :], ALU.mult).then_inc(bank_drained, 1)
                for t in range(TT):
                    a, b = qkv[:, 4 * e + t, :], qkv[:, 8 + 4 * e + t, :]
                    dve.wait_ge(bank_filled, unit2(BRANCH + e) + TT + t + 1)
                    dve.tensor_tensor(b, b, G[:, t, :], ALU.mult).then_inc(bank_drained, 1)
                    dve.wait_ge(bank_drained, unit2(BRANCH + e) + TT + t + 1 + UNITS_CREDIT)
                    step.done(dve.tensor_tensor(a, a, b, ALU.add))
                    two_parts(h_hi[:, 4 * e + t, :], h_lo[:, 4 * e + t, :], a).then_inc(split_ready, 1)
            for j in range(2):
                for t in range(TT):
                    dve.wait_ge(bank_filled, unit2(OUT2 + j) + t + 1)
                    n, at = t % 2, slice(512 * j, 512 * j + 512)
                    tmp = win[:, n, PAD:]
                    dve.tensor_tensor(tmp, G[:, t, :], gate_row[:, at], ALU.mult).then_inc(bank_drained, 1)
                    dve.wait_ge(bank_drained, unit2(OUT2 + j) + t + 1 + UNITS_CREDIT)
                    step.done(dve.tensor_tensor(X[:, t, at], X[:, t, at], tmp, ALU.add))
            dve.engine_nop().then_inc(x_scaled, 1)
            dve.wait_ge(gain2_loaded, 16)
            for ins in scaled_rows(2 * DEPTH + 2):
                ins.then_inc(out_ready, 1)

        def second_tensor(pe, three, product, in_rows, in_columns, turn_rows, turn_unit):
            def all_drained(job):
                pe.wait_ge(bank_drained, unit2(job) + UNITS_CREDIT)

            def every_fourth(hi, lo):
                return lambda t, k, s, kk: (hi[:, k, t::STRIDE], lo[:, k, t::STRIDE], w_hi[:, s, kk, :], w_lo[:, s, kk, :])

            pe.wait_ge(c_ready, 1)
            all_drained(ADA)
            for job in range(QKV):
                if job < 4:
                    product(unit2(job), piece2(job), lambda t, k, s, kk: (
                        w_hi[:, s, kk, P * t:P * t + P], w_lo[:, s, kk, P * t:P * t + P],
                        cb_hi[:, k, 0:2], cb_lo[:, k, 0:2]), 2)
                else:
                    product(unit2(job), piece2(job), lambda t, k, s, kk: (
                        cb_hi[:, k, :], cb_lo[:, k, :],
                        w_hi[:, s, kk, P * t:P * t + P], w_lo[:, s, kk, P * t:P * t + P]), P)
                if job == 0:
                    pe.wait_ge(hot_loaded, 16)
                    pe.wait_ge(rel_ready, 1)
                for h in range(4 * job, 4 * job + 4):
                    pe.wait_ge(small_drained, SM2_BIAS + h + 1)
                    pe.matmul(S[:, h % 2, 0:SKEW], rel_wide[0:NUM_BUCKETS + 1, h, :], hot[0:NUM_BUCKETS + 1, h // B2_H, :],
                              start=True, stop=True).then_inc(small_filled, 1)
            pe.wait_ge(xn_ready, 2 * DEPTH + 1)
            turn_rows(TR2_NORM, lambda k, t: xn2[:, t, P * k:P * k + P])
            pe.wait_ge(tr_drained, TR2_NORM + KT + PAIR_CREDIT)

            def give_scores(g, i):
                it = item_base(g) + i
                _, m, tile0, tiles, blocks = ITEMS2[g][i]
                pe.wait_ge(score_drained, SC0 + it + 1)
                q = slice(m, None, STRIDE) if g else slice(P * m, P * m + P)
                k = q if g else slice(P * (m + 1 - blocks), P * m + P)
                for n in range(tiles):
                    for e in range(2):
                        at = slice(HD * e, HD * e + HD)
                        dst = own(g, by_tile(g, S[:, 2 * (it % 2) + e, :]), blocks)[:, n, :]
                        ins = pe.matmul(dst, qkv[at, tile0 + n, q], qkv[at, 4 + tile0 + n, k], start=True, stop=True)
                ins.then_inc(score_filled, 1)

            def give_probs(g, i):
                it = item_base(g) + i
                blocks = ITEMS2[g][i][4]
                pe.wait_ge(prob2_ready, it + 1)
                for e in range(2):
                    pe.wait_ge(tr_drained, TR2_ATT + 2 * it + e + 1)
                    for b in range(4):
                        if not g and blocks == 1 and b % 2 == 0:
                            continue
                        ins = pe.transpose(G[:, e, P * b:P * b + P], prob2[:, it % 2, e, P * b:P * b + P], ident)
                    ins.then_inc(tr_filled, 1)

            def give_output(g, i):
                it = item_base(g) + i
                _, m, tile0, tiles, blocks = ITEMS2[g][i]
                pe.wait_ge(tr_drained, TR2_ATT + 2 * it + 2 + PAIR_CREDIT)
                pe.wait_ge(o_drained, OV0 + it + 1)
                for n in range(tiles):
                    for e in range(2):
                        h = 2 * (tile0 + n) + e
                        dst = G[:, 2 + it % 2, HD * (2 * n + e):HD * (2 * n + e) + HD]
                        for b in range(blocks):
                            place = n if g else 2 * n + 2 - blocks + b
                            ins = pe.matmul(dst, probT2[:, it % 2, e, P * place:P * place + P],
                                            qkv[:, 8 + m + 1 - blocks + b, HD * h:HD * h + HD],
                                            start=b == 0, stop=b == blocks - 1)
                ins.then_inc(o_filled, 1)

            for gn, g in enumerate(B2_GROUPS):
                all_drained(QKV + 3 * gn)
                for s in range(3):
                    job = QKV + 3 * gn + s
                    rows = every_fourth(h_hi, h_lo) if g else in_rows(h_hi, h_lo)
                    product(unit2(job), piece2(job), rows if s == 2 else in_columns(h_hi, h_lo))
                all_drained(QKV + 3 * gn + 3)
                pe.wait_ge(small_drained, SM2_BIAS + B2_HEADS + PAIR_CREDIT)
                n = len(ITEMS2[g])
                give_scores(g, 0)
                for i in range(n):
                    if i + 1 < n:
                        give_scores(g, i + 1)
                    give_probs(g, i)
                    if i:
                        give_output(g, i - 1)
                give_output(g, n - 1)
                pe.wait_ge(o_drained, OV0 + item_base(g) + n + PAIR_CREDIT)
            pe.wait_ge(score_drained, SC0 + len(ITEMS2[1]) + len(ITEMS2[2]) + len(ITEMS2[0]) + PAIR_CREDIT)

            product(unit2(Z_JOB), piece2(Z_JOB), in_rows(h_hi, h_lo))
            all_drained(U_JOB)
            product(unit2(U_JOB), piece2(U_JOB), in_columns(h_hi, h_lo))
            pe.wait_ge(z_rows_ready, 1)
            for k in range(4):
                turn_unit(TR2_Z + k, S[:, 2 + k % 2, :], lambda t: qkv[:, 12 + t, P * k:P * k + P])
            all_drained(ZP_JOB)
            product(unit2(ZP_JOB), piece2(ZP_JOB), in_columns(h_hi, h_lo))
            pe.wait_ge(pool_w_loaded, 16)
            for g in range(4):
                pe.wait_ge(pooled_ready, g + 1)
                pe.wait_ge(small_drained, SM2_POOL + g + 1)
                pe.matmul(S[:, g % 2, :], pool_w[:, g, :], qkv[:, 12 + g, :], start=True, stop=True).then_inc(small_filled, 1)
            all_drained(GATE_JOBS)
            for n in range(4):
                product(unit2(GATE_JOBS + n), piece2(GATE_JOBS + n), in_columns(h_hi, h_lo))
            all_drained(BRANCH)
            pe.wait_ge(split_ready, 1)
            for e in range(2):
                for half, (hi, lo) in enumerate(((at_hi, at_lo), (pt_hi, pt_lo))):
                    pe.wait_ge(low_ready, piece2(BRANCH + e) + half + 1 + RAW_SLOTS)
                    for t in range(TT):
                        unit = unit2(BRANCH + e) + TT * half + t
                        pe.wait_ge(bank_drained, unit + 1)
                        for k in range(4):
                            ins = three(G[:, t, :], w_hi[:, half, k, P * t:P * t + P], w_lo[:, half, k, P * t:P * t + P],
                                        hi[:, k, :], lo[:, k, :], k == 0, k == 3)
                        ins.then_inc(bank_filled, 1)
            pe.wait_ge(split_ready, 1 + 2 * TT)
            for j in range(2):
                product(unit2(OUT2 + j), piece2(OUT2 + j), in_rows(h_hi, h_lo))

        def pair_columns(p, e):
            g, hp = PAIRS[p]
            return HD * (hp + 2 * e if g == "B" else 2 * hp + e)

        def head_rows(p, what, e, t):
            g, hp = PAIRS[p]
            if g == "D":
                return (fox_q if what == "q" else fox_k)[:, t, 2 * hp + e, :]
            if g == "A":
                return (mla_q if what == "q" else mla_k)[:, t, 2 * hp + e, :]
            if g == "B":
                at = P * hp if what == "q" else 2 * P
                return rows_b[:, t, at:at + P]
            at = P * hp + (0 if what == "q" else 2 * P)
            return rows_c[:, t, at:at + P]

        def head_width(p):
            return {"D": FOX_K, "A": MLA_QK, "B": P, "C": P}[PAIRS[p][0]]

        def qk_places(p):
            if PAIRS[p][0] in "DA":
                return [("q", 0, 0), ("q", 1, 1), ("k", 0, 2), ("k", 1, 3)]
            return [("q", 0, 0), ("k", 0, 2)]

        def score_scale(p):
            return (MLA_QK if PAIRS[p][0] == "A" else HD) ** -0.5

        def key_tiles(i):
            p, qt = ITEMS[i]
            return list(range(max(qt - 1, 0), qt + 1)) if PAIRS[p][0] == "B" else list(range(qt + 1))

        def mixed_rows(g):
            return {"A": rows_a, "B": rows_b, "C": rows_c, "D": rows_idx}[g]

        def select_at(qt):
            at = sum(n + 1 for n in range(1, qt)) * P
            return select[:, at:at + (qt + 1) * P]

        @block.sync
        def _(sp):
            def cols(w, l, half, c0, c1, k0=0):
                rows = slice((k0 + half * HALF_K) * P, (k0 + (half + 1) * HALF_K) * P)
                return w[bass.ds(l, 1), rows, c0:c1].rearrange("l (k p) n -> p (l k) n", p=P)

            def slot_free(value):
                sp.wait_ge(low_ready, value)
                sp.sem_inc(pieces_asked, 1)

            sp.dma_start(X[:], A["x"].rearrange("b (t p) d -> p (b t) d", p=P)).then_inc(x_loaded, 16)
            sp.dma_start(masks[:], c_mask[:, :]).then_inc(const_loaded, 16)
            sp.dma_start(rope64[:], c_rope64[:, :, :, :]).then_inc(const_loaded, 16)
            sp.dma_start(rope32[:], c_rope32[:, :, :, :]).then_inc(const_loaded, 16)
            with sp.Fori(0, DEPTH) as l:
                number = l * LAYER_PIECES
                sp.wait_ge(tr_drained, l * LAYER_TR + PAIR_CREDIT)
                sp.sem_inc(pieces_asked, 1)
                for dst, src in (
                    (gain1[:], A["norm1"][bass.ds(l, 1), :].rearrange("l (k p) -> p (l k)", p=P)),
                    (gain2[:], A["norm2"][bass.ds(l, 1), :].rearrange("l (k p) -> p (l k)", p=P)),
                    (q_gain[:], A["mla_q_norm"][bass.ds(l, 1), :].rearrange("l (k p) -> p (l k)", p=P)),
                    (kv_gain[:], A["mla_kv_norm"][bass.ds(l, 1), :].rearrange("l (k p) -> p (l k)", p=P)),
                    (sinks[:], A["swa_sinks"][bass.ds(l, 1), :].broadcast_to([P, HEADS])),
                    (gate_bias[:], A["fox_b_f"][bass.ds(l, 1), :].broadcast_to([P, HEADS])),
                ):
                    sp.dma_start(dst, src, allow_slow_non_contiguous=True).then_inc(params_loaded, 16)
                for c in range(FIRST_GROUP_PIECE):
                    job, half, slot = c // 2, c % 2, c % RAW_SLOTS
                    slot_free(number + (c + 1))
                    if job < PROJ_JOBS:
                        at = 0
                        for c0, c1 in PROJ_PARTS[job]:
                            sp.dma_start(raw[:, slot, :, at:at + c1 - c0], cols(A["w_in"], l, half, c0, c1)
                                         ).then_inc(raw_loaded[slot], 16)
                            at += c1 - c0
                    else:
                        n0 = 512 * (job - OUT_JOB)
                        sp.dma_start(raw[:, slot], cols(A["w_out"], l, half, n0, n0 + 512)
                                     ).then_inc(raw_loaded[slot], 16)
                    if c == 7:
                        sp.dma_start(w_uq[:], A["mla_w_uq"][bass.ds(l, 1), :, :].rearrange("l (k p) n -> p (l k) n", p=P)
                                     ).then_inc(mla_w_loaded, 16)
                        sp.dma_start(w_ukv[:], A["mla_w_ukv"][bass.ds(l, 1), :, :].rearrange("l p n -> p (l n)")
                                     ).then_inc(mla_w_loaded, 16)
                with sp.Fori(0, FFN_GROUPS) as g:
                    for c in range(2 * GROUP_JOBS):
                        job, half, slot = c // 2, c % 2, c % RAW_SLOTS
                        slot_free(number + (g * (2 * GROUP_JOBS) + (FIRST_GROUP_PIECE + c + 1)))
                        n0, kh = 512 * (job % 2), slice(half * HALF_K, (half + 1) * HALF_K)
                        if job < 2:
                            src = A["w_up"].rearrange("l (k p) n -> l p k n", p=P)[
                                bass.ds(l, 1), :, kh, bass.ds(g * D_MODEL + n0, 512)].rearrange("l p k n -> p (l k) n")
                        else:
                            src = A["w_down"].rearrange("l (g k p) n -> l g p k n", p=P, g=FFN_GROUPS)[
                                bass.ds(l, 1), bass.ds(g, 1), :, kh, n0:n0 + 512].rearrange("l g p k n -> p (l g k) n")
                        sp.dma_start(raw[:, slot], src).then_inc(raw_loaded[slot], 16)
            second_loads(sp)

        @block.gpsimd
        def _(pool):
            pool.memset(raw[:, 0:2, :, IDX_W:512], 0.0)
            pool.memset(raw[:, 2:4, :, A_W:512], 0.0).then_inc(slots_cleared, 1)
            pool.sem_inc(low_ready, RAW_SLOTS)

            def split_low(number, c):
                pool.wait_ge(high_ready, number + 1)
                pool.tensor_tensor(w_lo[:, c % SPLIT_SLOTS], raw[:, c % RAW_SLOTS],
                                   w_hi[:, c % SPLIT_SLOTS].bitcast(F32), ALU.subtract).then_inc(low_ready, 1)

            with pool.Fori(0, TOTAL_PIECES // RAW_SLOTS) as i:
                for c in range(RAW_SLOTS):
                    split_low(i * RAW_SLOTS + c, c)

        @block.scalar
        def _(act):
            def split_high(c, loads, jobs_before):
                act.wait_ge(raw_loaded[c % RAW_SLOTS], loads)
                if c % 2 == 0:
                    act.wait_ge(half_used, jobs_before)
                else:
                    act.wait_ge(bank_filled, jobs_before * TT)
                act.activation(w_hi[:, c % SPLIT_SLOTS], raw[:, c % RAW_SLOTS], ACT.Copy).then_inc(high_ready, 1)

            def square_sums(norm_no, rows):
                for t in range(TT):
                    ins = act.activation(rows[:, t, :], X[:, t, :], ACT.Square, accum_out=sumsq[:, t:t + 1])
                ins.then_inc(sumsq_ready, 1)
                act.wait_ge(var_ready, norm_no + 1)
                act.activation(std[:], var[:], ACT.Sqrt).then_inc(std_ready, 1)

            def high_T(gain, tr):
                for k in range(KT):
                    act.wait_ge(tr_filled, tr + (k + 1))
                    scale = 1.0 if gain is None else gain[:, k:k + 1]
                    act.activation(h_hi[:, k, :], S[:, 2 + k % 2, :], ACT.Copy, scale=scale).then_inc(hi_ready, 1)

            act.wait_ge(slots_cleared, 1)
            for c in range(2):
                act.wait_ge(raw_loaded[c], 16)
                act.activation(w_hi[:, c], raw[:, c], ACT.Copy).then_inc(high_ready, 1)
            act.wait_ge(x_loaded, 16)

            with act.Fori(0, DEPTH) as l:
                unit, tr, small, jobs = l * LAYER_UNITS, l * LAYER_TR, l * LAYER_SM, l * LAYER_JOBS
                item0 = l * NI

                def ahead(job, half):
                    c = 2 * (job + 1) + half
                    s = c % RAW_SLOTS
                    upto = loads_upto(c) if job + 1 < FFN_JOB else LOADS_TO_GROUPS[s] + 16
                    split_high(c, l * LAYER_LOADS[s] + upto, jobs + (job + 1))

                def rows_out(job, parts):
                    for t in range(TT):
                        act.wait_ge(bank_filled, unit + (TT * job + t + 1))
                        for dst, src in parts(t):
                            ins = act.activation(dst, src, ACT.Copy)
                        ins.then_inc(bank_drained, 1)

                act.wait_ge(params_loaded, l * 96 + 96)
                act.wait_ge(bank_drained, unit + UNITS_CREDIT)
                square_sums(l * 2, xn)
                high_T(gain1, tr + TR_NORM1)

                ahead(JOB_IDX, 0)
                rows_out(JOB_IDX, lambda t: [(rows_idx[:, t, :], G[:, t, 0:IDX_W])])
                ahead(JOB_IDX, 1)
                ahead(JOB_A, 0)
                rows_out(JOB_A, lambda t: [(rows_a[:, t, :], G[:, t, 0:A_W])])
                ahead(JOB_A, 1)
                act.wait_ge(bank_drained, unit + (TT * (JOB_A + 1) + UNITS_CREDIT))
                for t in range(TT):
                    act.activation(select[:, 256 * t:256 * t + 256], rows_a[:, t, 0:256], ACT.Square,
                                   accum_out=m_sumsq[:, t:t + 1])
                for t in range(TT):
                    ins = act.activation(work[:, P * t:P * t + P], rows_a[:, t, 256:384], ACT.Square,
                                         accum_out=m_sumsq[:, TT + t:TT + t + 1])
                ins.then_inc(m_sumsq_ready, 1)
                act.wait_ge(m_var_ready, l + 1)
                act.activation(m_std[:], m_var[:], ACT.Sqrt).then_inc(m_std_ready, 1)
                act.wait_ge(gate_abs_ready, l + 1)
                act.activation(gate_e[:], gate_a[:], ACT.Exp, scale=-1.0).then_inc(gate_exp_ready, 1)
                act.wait_ge(gate_exp_ready, l * 2 + 1)
                act.activation(gate_a[:], gate_e[:], ACT.Ln, bias=1.0).then_inc(gate_exp_ready, 1)

                ahead(JOB_C, 0)
                rows_out(JOB_C, lambda t: [(rows_c[:, t, :], G[:, t, :])])
                ahead(JOB_C, 1)

                def relu_scores(qt):
                    for h in range(8):
                        n = SM_IDX + 8 * (qt - 1) + h
                        act.wait_ge(small_filled, small + (n + 1))
                        act.wait_ge(rel_used, l * 24 + (n + 1))
                        act.activation(rel[:, h % 2, 0:P * (qt + 1)], S[:, n % 2, 0:P * (qt + 1)],
                                       ACT.Relu).then_inc(small_drained, 1)

                relu_scores(1)
                relu_scores(2)
                ahead(JOB_B, 0)
                rows_out(JOB_B, lambda t: [(rows_b[:, t, :], G[:, t, :])])
                ahead(JOB_B, 1)
                relu_scores(3)
                for t in range(TT):
                    n = SM_EXP + 2 * t
                    act.wait_ge(small_filled, small + (n + 1))
                    act.activation(mla_q[:, t].rearrange("p h d -> p (h d)"), S[:, 0, 0:HEADS * MLA_QK],
                                   ACT.Copy).then_inc(small_drained, 1)
                    act.wait_ge(small_filled, small + (n + 2))
                    kv = S[:, 1, :].rearrange("p (h d) -> p h d", h=HEADS)
                    act.activation(mla_k[:, t, :, 0:HD], kv[:, :, 0:HD], ACT.Copy)
                    act.activation(mla_v[:, t, :].rearrange("p (h d) -> p h d", h=HEADS), kv[:, :, HD:2 * HD],
                                   ACT.Copy).then_inc(small_drained, 1)
                ahead(JOB_D, 0)
                rows_out(JOB_D, lambda t: [
                    (fox_q[:, t, :, 0:HD], G[:, t, 0:256].rearrange("p (h d) -> p h d", h=HEADS)),
                    (fox_k[:, t, :, 0:HD], G[:, t, 256:512].rearrange("p (h d) -> p h d", h=HEADS))])
                ahead(JOB_D, 1)
                ahead(JOB_V, 0)
                rows_out(JOB_V, lambda t: [(rows_v[:, t, :], G[:, t, :])])
                ahead(JOB_V, 1)

                for i, (p, qt) in enumerate(ITEMS):
                    width = P * len(key_tiles(i))
                    act.wait_ge(neg_max_ready, item0 + (i + 1))
                    if i >= 2:
                        act.wait_ge(tr_filled, tr + (PT_NO[i - 2, 1] + 1))
                    for e in range(2):
                        if PAIRS[p][0] == "B":
                            h = PAIRS[p][1] + 2 * e
                            act.activation(sink_term[:, i % 4, e:e + 1], sinks[:, h:h + 1], ACT.Exp,
                                           bias=neg_max[:, i % 2, e:e + 1])
                        ins = act.activation(prob[:, i % 2, e, 0:width], S[:, 2 * (i % 2) + e, 0:width], ACT.Exp,
                                             bias=neg_max[:, i % 2, e:e + 1], scale=score_scale(p),
                                             accum_out=row_sum[:, i % 4, e:e + 1])
                    ins.then_inc(score_drained, 1)

                high_T(None, tr + TR_MIX)
                for job in (OUT_JOB, OUT_JOB + 1):
                    for half in range(2):
                        ahead(job, half)
                act.wait_ge(bank_drained, unit + (TT * FFN_JOB + UNITS_CREDIT))
                square_sums(l * 2 + 1, xn)
                high_T(gain2, tr + TR_NORM2)

                with act.Fori(0, FFN_GROUPS) as g:
                    unit_g = unit + g * (TT * GROUP_JOBS)
                    hidden = l * LAYER_HIDDEN + g * HIDDEN_UNITS
                    jobs_g = jobs + g * GROUP_JOBS

                    def ahead_g(job, half):
                        c = 2 * (job + 1) + half
                        s = c % RAW_SLOTS
                        if job + 1 < GROUP_JOBS:
                            upto = LOADS_TO_GROUPS[s] + 16 * (c // RAW_SLOTS + 1)
                            split_high(c, l * LAYER_LOADS[s] + (g * GROUP_LOADS + upto), jobs_g + (FFN_JOB + job + 1))
                        else:
                            upto = LOADS_TO_GROUPS[s] + GROUP_LOADS + 16
                            split_high(c, l * LAYER_LOADS[s] + (g * GROUP_LOADS + upto), jobs_g + (FFN_JOB + job + 1))

                    for job in range(2):
                        ahead_g(job, 0)
                        for t in range(TT):
                            n = TT * job + t
                            act.wait_ge(bank_filled, unit_g + (TT * (FFN_JOB + job) + t + 1))
                            act.wait_ge(hidden_split, hidden + (n + 1))
                            act.activation(relu[:, n % 2, :], G[:, t, :], ACT.Relu).then_inc(bank_drained, 1)
                        ahead_g(job, 1)
                    for job in range(2, GROUP_JOBS):
                        ahead_g(job, 0)
                        ahead_g(job, 1)
            second_scalar(act, split_high, square_sums)

        @block.vector
        def _(dve):
            step = Steps(dve, dve_step)
            dve.sem_inc(bank_drained, UNITS_CREDIT)
            for s in (tr_drained, small_drained, score_drained, o_drained, rel_used, hidden_split):
                dve.sem_inc(s, PAIR_CREDIT)

            def inverse_root(v, root, r, y):
                step.done(dve.reciprocal(r, root))
                step.done(dve.tensor_tensor(y, r, r, ALU.mult))
                step.done(dve.tensor_tensor(y, y, v, ALU.mult))
                step.done(dve.tensor_scalar(y, y, -0.5, 1.5, ALU.mult, ALU.add))
                step.done(dve.tensor_tensor(r, r, y, ALU.mult))

            def normal_rows(norm_no, rows):
                dve.wait_ge(sumsq_ready, norm_no + 1)
                dve.tensor_scalar(var[:], sumsq[:], 1.0 / D_MODEL, EPS, ALU.mult, ALU.add).then_inc(var_ready, 1)
                dve.wait_ge(std_ready, norm_no + 1)
                inverse_root(var[:], std[:], rstd[:], newton[:])
                for t in range(TT):
                    ins = dve.tensor_scalar(rows[:, t, :], X[:, t, :], rstd[:, t:t + 1], None, ALU.mult)
                return ins

            def low_T(gain, hi_no):
                for k in range(KT):
                    dve.wait_ge(hi_ready, hi_no + (k + 1))
                    scale = 1.0 if gain is None else gain[:, k:k + 1]
                    dve.scalar_tensor_tensor(h_lo[:, k, :], S[:, 2 + k % 2, :], scale, h_hi[:, k, :].bitcast(F32),
                                             ALU.mult, ALU.subtract).then_inc(tr_drained, 1)

            def rotate(v, table, heads, half):
                for t in range(TT):
                    x1, x2 = v(t)[:, :, 0:half], v(t)[:, :, half:2 * half]
                    cos = table[:, 0, t, :].unsqueeze(1).broadcast_to([P, heads, half])
                    sin = table[:, 1, t, :].unsqueeze(1).broadcast_to([P, heads, half])
                    a, b, c, d = (turn[:, n, 0:heads * half].rearrange("p (h d) -> p h d", h=heads) for n in range(4))
                    dve.tensor_tensor(a, x1, cos, ALU.mult)
                    dve.tensor_tensor(b, x2, sin, ALU.mult)
                    dve.tensor_tensor(c, x2, cos, ALU.mult)
                    step.done(dve.tensor_tensor(d, x1, sin, ALU.mult))
                    dve.tensor_tensor(x1, a, b, ALU.subtract)
                    step.done(dve.tensor_tensor(x2, c, d, ALU.add))

            dve.wait_ge(x_loaded, 16)
            dve.wait_ge(const_loaded, 48)

            with dve.Fori(0, DEPTH) as l:
                unit, tr, small, item0 = l * LAYER_UNITS, l * LAYER_TR, l * LAYER_SM, l * NI

                def stored(job):
                    dve.wait_ge(bank_drained, unit + (TT * (job + 1) + UNITS_CREDIT))

                dve.wait_ge(params_loaded, l * 96 + 96)
                normal_rows(l * 2, xn).then_inc(xn_ready, 1)
                low_T(gain1, l * HI_PER_LAYER)

                stored(JOB_IDX)
                rotate(lambda t: rows_idx[:, t, 0:288].rearrange("p (h d) -> p h d", h=9), rope32, 9, 16)
                key = rows_idx[:, :, 256:288].unsqueeze(2).broadcast_to([P, TT, 4, 32])
                dve.tensor_copy(k_idx4[:].rearrange("p t (c d) -> p t c d", c=4), key).then_inc(idx_rows_ready, 1)

                stored(JOB_A)
                dve.wait_ge(m_sumsq_ready, l + 1)
                dve.tensor_scalar(m_var[:, 0:TT], m_sumsq[:, 0:TT], 1.0 / 256, EPS, ALU.mult, ALU.add)
                dve.tensor_scalar(m_var[:, TT:2 * TT], m_sumsq[:, TT:2 * TT], 1.0 / 128, EPS, ALU.mult,
                                  ALU.add).then_inc(m_var_ready, 1)
                z = rows_a[:, :, 416:420]
                step.done(dve.tensor_tensor(gate_z[:], z, gate_bias[:].unsqueeze(1).broadcast_to([P, TT, HEADS]), ALU.add))
                dve.scalar_tensor_tensor(gate_a[:], gate_z[:], -1.0, gate_z[:], ALU.mult, ALU.max).then_inc(gate_abs_ready, 1)
                dve.wait_ge(m_std_ready, l + 1)
                inverse_root(m_var[:], m_std[:], m_rstd[:], m_newton[:])
                for t in range(TT):
                    dve.tensor_scalar(rows_a[:, t, 0:256], rows_a[:, t, 0:256], m_rstd[:, t:t + 1], None, ALU.mult)
                    ins = dve.tensor_scalar(rows_a[:, t, 256:384], rows_a[:, t, 256:384],
                                            m_rstd[:, TT + t:TT + t + 1], None, ALU.mult)
                ins.then_inc(m_rows_ready, 1)
                for n in range(3):
                    dve.wait_ge(tr_filled, tr + (TR_IDX + n + 1))
                    dst = qiT[:, n, :] if n < 2 else kiT[:]
                    dve.tensor_copy(dst, S[:, 2 + (TR_IDX + n) % 2, :]).then_inc(tr_drained, 1)
                rotate(lambda t: rows_a[:, t, 384:416].rearrange("p (h d) -> p h d", h=1), rope32, 1, 16)
                dve.wait_ge(gate_exp_ready, l * 2 + 2)
                dve.scalar_tensor_tensor(log_f[:], gate_z[:], 0.0, gate_a[:], ALU.min, ALU.subtract).then_inc(log_f_ready, 1)

                def index_scores(qt):
                    acc = select_at(qt)
                    for h in range(8):
                        n = SM_IDX + 8 * (qt - 1) + h
                        dve.wait_ge(small_drained, small + (n + 1 + PAIR_CREDIT))
                        w = rows_idx[:, qt, 288 + h:289 + h]
                        part = rel[:, h % 2, 0:P * (qt + 1)]
                        if h == 0:
                            dve.tensor_scalar(acc, part, w, None, ALU.mult).then_inc(rel_used, 1)
                        else:
                            dve.wait_ge(rel_used, l * 24 + (n + PAIR_CREDIT))
                            dve.scalar_tensor_tensor(acc, part, w, acc, ALU.mult, ALU.add).then_inc(rel_used, 1)
                    dve.wait_ge(rel_used, l * 24 + (8 * qt + PAIR_CREDIT))
                    diag = acc[:, P * qt:P * qt + P]
                    step.done(dve.tensor_tensor(diag, diag, causal, ALU.add))

                index_scores(1)
                index_scores(2)
                for n in range(3):
                    dve.wait_ge(tr_filled, tr + (TR_MLA + n + 1))
                    src = S[:, 2 + (TR_MLA + n) % 2, :]
                    if n < 2:
                        dve.tensor_scalar(cqT[:, n, :], src, q_gain[:, n:n + 1], None, ALU.mult).then_inc(tr_drained, 1)
                    else:
                        dve.tensor_scalar(ckvT[:], src, kv_gain[:, 0:1], None, ALU.mult).then_inc(tr_drained, 1)
                stored(JOB_C)
                rotate(lambda t: rows_c[:, t, :].rearrange("p (h d) -> p h d", h=8), rope64, 8, 32)
                index_scores(3)

                def top_keys(qt):
                    acc, left = select_at(qt), work[:, 0:P * (qt + 1)]
                    for n in range(TOP_K // 8):
                        src = acc if n == 0 else left
                        step.done(dve.max(top8[:], src))
                        step.done(dve.match_replace(left, top8[:], src, TAKEN))
                    step.done(dve.tensor_scalar(acc, left, TAKEN * 0.9, NEG, ALU.is_gt, ALU.mult))

                top_keys(1)
                top_keys(2)
                dve.wait_ge(small_drained, small + (LAYER_SM + PAIR_CREDIT))
                rotate(lambda t: mla_q[:, t, :, HD:MLA_QK], rope32, HEADS, 16)
                for t in range(TT):
                    key = rows_a[:, t, 384:416].unsqueeze(1).broadcast_to([P, HEADS, MLA_ROPE])
                    ins = dve.tensor_copy(mla_k[:, t, :, HD:MLA_QK], key)
                step.done(ins)
                for n in range(2):
                    dve.wait_ge(tr_filled, tr + (TR_CUM + n + 1))
                    cum = S[:, 2 + n, 0:2 * HEADS].rearrange("p (t h) -> p t h", t=2)
                    tt = slice(2 * n, 2 * n + 2)
                    dve.memset(fox_q[:, tt, :, HD + 1:HD + 2], 1.0)
                    dve.memset(fox_k[:, tt, :, HD:HD + 1], 1.0)
                    dve.tensor_scalar(fox_q[:, tt, :, HD:HD + 1], cum.unsqueeze(3), HD ** 0.5, None, ALU.mult)
                    dve.tensor_scalar(fox_k[:, tt, :, HD + 1:HD + 2], cum.unsqueeze(3), -(HD ** 0.5), None,
                                      ALU.mult).then_inc(tr_drained, 1)
                stored(JOB_B)
                rotate(lambda t: rows_b[:, t, 0:384].rearrange("p (h d) -> p h d", h=6), rope64, 6, 32)
                top_keys(3)
                dve.engine_nop().then_inc(heads_ready, 1)

                def take_qk(p):
                    m = head_width(p)
                    for n, (_, _, at) in enumerate(qk_places(p)):
                        no = QK_NO[p, n]
                        dve.wait_ge(tr_filled, tr + (no + 1))
                        dve.tensor_copy(qkT[0:m, p % 2, at, :], G[0:m, no % 2, :]).then_inc(tr_drained, 1)

                def row_maxima(i):
                    p, qt = ITEMS[i]
                    g, hp = PAIRS[p]
                    tiles = key_tiles(i)
                    width, half = P * len(tiles), i % 2
                    s = S[:, 2 * half:2 * half + 2, :]
                    dve.wait_ge(score_filled, item0 + (i + 1))
                    if g == "C" and qt:
                        part, mask = s[:, :, 0:width], select_at(qt)
                    elif g == "B" and qt:
                        part, mask = s[:, :, 0:width], window
                    else:
                        part, mask = s[:, :, width - P:width], causal
                    m = part.shape[2]
                    step.done(dve.tensor_tensor(part, part, mask.unsqueeze(1).broadcast_to([P, 2, m]), ALU.add))
                    step.done(dve.tensor_reduce(row_max[:, half, :], s[:, :, 0:width], AX.X, ALU.max))
                    if g == "B":
                        scaled = dve.tensor_scalar(row_max[:, half, :], row_max[:, half, :], score_scale(p), None, ALU.mult)
                        step.done(scaled)
                        step.done(dve.tensor_tensor(row_max[:, half, :], row_max[:, half, :],
                                                    sinks[:, hp:hp + 3:2], ALU.max))
                        ins = dve.tensor_scalar(neg_max[:, half, :], row_max[:, half, :], -1.0, None, ALU.mult)
                    else:
                        ins = dve.tensor_scalar(neg_max[:, half, :], row_max[:, half, :], -score_scale(p), None, ALU.mult)
                    ins.then_inc(neg_max_ready, 1)

                def take_probs(i):
                    p, qt = ITEMS[i]
                    width = P * len(key_tiles(i))
                    for e in range(2):
                        no = PT_NO[i, e]
                        dve.wait_ge(tr_filled, tr + (no + 1))
                        if e == 0 and i >= 2:
                            dve.wait_ge(o_filled, item0 + (i - 1))
                        dve.tensor_copy(probT[:, i % 2, e, 0:width], G[:, no % 2, 0:width]).then_inc(tr_drained, 1)
                    dve.wait_ge(score_drained, item0 + (i + 1 + PAIR_CREDIT))
                    total = row_sum[:, i % 4, :]
                    if PAIRS[p][0] == "B":
                        step.done(dve.tensor_tensor(total, total, sink_term[:, i % 4, :], ALU.add))
                    step.done(dve.reciprocal(inv_sum[:, i % 4, :], total))

                def take_output(i):
                    p, qt = ITEMS[i]
                    dve.wait_ge(o_filled, item0 + (i + 1))
                    o = G[:, 2 + i % 2, 0:2 * HD].rearrange("p (e d) -> p e d", e=2)
                    rows = mixed_rows(PAIRS[p][0])
                    c0, c1 = pair_columns(p, 0), pair_columns(p, 1)
                    if c1 - c0 == HD:
                        dst = rows[:, qt, c0:c0 + 2 * HD].rearrange("p (e d) -> p e d", e=2)
                    else:
                        dst = rows[:, qt, 0:256].rearrange("p (e a d) -> p e a d", e=2, a=2)[:, :, c0 // HD, :]
                    dve.tensor_tensor(dst, o, inv_sum[:, i % 4, :].unsqueeze(2).broadcast_to([P, 2, HD]),
                                      ALU.mult).then_inc(o_drained, 1)

                take_qk(0)
                row_maxima(0)
                for i in range(NI):
                    p = ITEMS[i][0]
                    if i % TT == 1 and p + 1 < len(PAIRS):
                        take_qk(p + 1)
                    if i + 1 < NI:
                        row_maxima(i + 1)
                    take_probs(i)
                    if i:
                        take_output(i - 1)
                take_output(NI - 1)

                low_T(None, l * HI_PER_LAYER + KT)

                def add_to_x(first_unit, col):
                    for t in range(TT):
                        dve.wait_ge(bank_filled, first_unit + (t + 1))
                        dst = X[:, t, 512 * col:512 * col + 512]
                        dve.tensor_tensor(dst, G[:, t, :], dst, ALU.add).then_inc(bank_drained, 1)

                for j in range(2):
                    add_to_x(unit + TT * (OUT_JOB + j), j)
                normal_rows(l * 2 + 1, xn).then_inc(xn_ready, 1)
                low_T(gain2, l * HI_PER_LAYER + 2 * KT)
                step.restart()

                with dve.Fori(0, FFN_GROUPS) as g:
                    unit_g = unit + g * (TT * GROUP_JOBS)
                    hidden = l * LAYER_HIDDEN + g * HIDDEN_UNITS
                    for n in range(HIDDEN_UNITS):
                        dve.wait_ge(bank_drained, unit_g + (TT * FFN_JOB + n + 1 + UNITS_CREDIT))
                        dve.wait_ge(hidden_split, hidden + (n + PAIR_CREDIT))
                        step.done(dve.tensor_tensor(square[:], relu[:, n % 2, :], relu[:, n % 2, :], ALU.mult))
                        step.done(dve.tensor_copy(u_hi[:, n, :], square[:]))
                        dve.tensor_tensor(u_lo[:, n, :], square[:], u_hi[:, n, :].bitcast(F32),
                                          ALU.subtract).then_inc(hidden_split, 1)
                    for j in range(2):
                        first = unit_g + TT * (FFN_JOB + 2 + j)
                        dve.wait_ge(bank_drained, first + UNITS_CREDIT)
                        add_to_x(first, j)
                    step.restart()
            second_vector(dve, step, inverse_root, normal_rows)

        @block.tensor
        def _(pe):
            def three(dst, a_hi, a_lo, b_hi, b_lo, first, last):
                pe.matmul(dst, a_hi, b_hi, start=first, stop=False)
                pe.matmul(dst, a_hi, b_lo, start=False, stop=False)
                return pe.matmul(dst, a_lo, b_hi, start=False, stop=last)

            def product(unit, number, operands, n=512):
                for half in range(2):
                    pe.wait_ge(low_ready, number + (half + 1 + RAW_SLOTS))
                    for t in range(TT):
                        if half == 0:
                            pe.wait_ge(bank_drained, unit + (t + 1))
                        for kk in range(HALF_K):
                            ins = three(G[:, t, 0:n], *operands(t, half * HALF_K + kk, half, kk),
                                        half == 0 and kk == 0, half == 1 and kk == HALF_K - 1)
                        if half:
                            ins.then_inc(bank_filled, 1)
                    if half == 0:
                        ins.then_inc(half_used, 1)

            def in_rows(hi, lo, n=512):
                return lambda t, k, s, kk: (hi[:, k, P * t:P * t + P], lo[:, k, P * t:P * t + P],
                                            w_hi[:, s, kk, 0:n], w_lo[:, s, kk, 0:n])

            def in_columns(hi, lo):
                return lambda t, k, s, kk: (w_hi[:, s, kk, P * t:P * t + P], w_lo[:, s, kk, P * t:P * t + P],
                                            hi[:, k, :], lo[:, k, :])

            def turn_unit(tr, bank, parts):
                pe.wait_ge(tr_drained, tr + 1)
                for t in range(TT):
                    src = parts(t)
                    ins = pe.transpose(bank[0:src.shape[1], P * t:P * t + P], src, ident)
                ins.then_inc(tr_filled, 1)

            def turn_rows(tr, rows_of):
                for k in range(KT):
                    turn_unit(tr + k, S[:, 2 + k % 2, :], lambda t: rows_of(k, t))

            pe.wait_ge(const_loaded, 48)
            with pe.Fori(0, DEPTH) as l:
                unit, tr, small, item0 = l * LAYER_UNITS, l * LAYER_TR, l * LAYER_SM, l * NI
                number = l * LAYER_PIECES

                def project(job):
                    n = PROJ_N[job]
                    product(unit + TT * job, number + 2 * job, in_rows(h_hi, h_lo, n), n)

                pe.wait_ge(xn_ready, l * 2 + 1)
                turn_rows(tr + TR_NORM1, lambda k, t: xn[:, t, P * k:P * k + P])
                pe.wait_ge(tr_drained, tr + (TR_NORM1 + KT + PAIR_CREDIT))
                project(JOB_IDX)
                project(JOB_A)
                pe.wait_ge(idx_rows_ready, l + 1)
                for n in range(3):
                    turn_unit(tr + (TR_IDX + n), S[:, 2 + (TR_IDX + n) % 2, :],
                              lambda t: rows_idx[:, t, P * n:P * n + P] if n < 2 else k_idx4[:, t, :])
                project(JOB_C)

                def index_products(qt):
                    for h in range(8):
                        n = SM_IDX + 8 * (qt - 1) + h
                        at = slice(32 * (h % 4), 32 * (h % 4) + 32)
                        pe.wait_ge(small_drained, small + (n + 1))
                        pe.matmul(S[:, n % 2, 0:P * (qt + 1)], qiT[at, h // 4, P * qt:P * qt + P],
                                  kiT[at, 0:P * (qt + 1)], start=True, stop=True).then_inc(small_filled, 1)

                pe.wait_ge(tr_drained, tr + (TR_IDX + 3 + PAIR_CREDIT))
                index_products(1)
                index_products(2)
                pe.wait_ge(m_rows_ready, l + 1)
                for n in range(3):
                    turn_unit(tr + (TR_MLA + n), S[:, 2 + (TR_MLA + n) % 2, :],
                              lambda t: rows_a[:, t, P * n:P * n + P])
                project(JOB_B)
                index_products(3)
                pe.wait_ge(tr_drained, tr + (TR_MLA + 3 + PAIR_CREDIT))
                pe.wait_ge(mla_w_loaded, l * 32 + 32)
                for t in range(TT):
                    n = SM_EXP + 2 * t
                    pe.wait_ge(small_drained, small + (n + 1))
                    for k in range(2):
                        ins = pe.matmul(S[:, 0, 0:HEADS * MLA_QK], cqT[:, k, P * t:P * t + P], w_uq[:, k, :],
                                        start=k == 0, stop=k == 1)
                    ins.then_inc(small_filled, 1)
                    pe.wait_ge(small_drained, small + (n + 2))
                    pe.matmul(S[:, 1, :], ckvT[:, P * t:P * t + P], w_ukv[:], start=True, stop=True
                              ).then_inc(small_filled, 1)
                project(JOB_D)
                pe.wait_ge(log_f_ready, l + 1)
                for n in range(2):
                    pe.wait_ge(tr_drained, tr + (TR_CUM + n + 1))
                    for t in (2 * n, 2 * n + 1):
                        dst = S[:, 2 + n, HEADS * (t % 2):HEADS * (t % 2) + HEADS]
                        for s in range(t + 1):
                            ins = pe.matmul(dst, upto if s == t else ones, log_f[:, s, :], start=s == 0, stop=s == t)
                    ins.then_inc(tr_filled, 1)
                project(JOB_V)

                pe.wait_ge(bank_drained, unit + (TT * PROJ_JOBS + UNITS_CREDIT))
                pe.wait_ge(small_drained, small + (LAYER_SM + PAIR_CREDIT))
                pe.wait_ge(tr_drained, tr + (TR_ATT + PAIR_CREDIT))
                pe.wait_ge(heads_ready, l + 1)

                def give_qk(p):
                    for n, (what, e, _) in enumerate(qk_places(p)):
                        no = QK_NO[p, n]
                        turn_unit(tr + no, G[:, no % 2, :], lambda t: head_rows(p, what, e, t))

                def give_scores(i):
                    p, qt = ITEMS[i]
                    tiles = key_tiles(i)
                    if qt == 0:
                        pe.wait_ge(tr_drained, tr + (QK_NO[p, qk_units(p) - 1] + 1 + PAIR_CREDIT))
                    pe.wait_ge(score_drained, item0 + (i + 1))
                    for e in range(2):
                        if PAIRS[p][0] in "DA":
                            at, q, k = slice(0, head_width(p)), e, 2 + e
                        else:
                            at, q, k = slice(HD * e, HD * e + HD), 0, 2
                        ins = pe.matmul(S[:, 2 * (i % 2) + e, 0:P * len(tiles)], qkT[at, p % 2, q, P * qt:P * qt + P],
                                        qkT[at, p % 2, k, P * tiles[0]:P * (qt + 1)], start=True, stop=True)
                    ins.then_inc(score_filled, 1)

                def give_probs(i):
                    pe.wait_ge(score_drained, item0 + (i + 1 + PAIR_CREDIT))
                    for e in range(2):
                        no = PT_NO[i, e]
                        pe.wait_ge(tr_drained, tr + (no + 1))
                        for b in range(len(key_tiles(i))):
                            ins = pe.transpose(G[:, no % 2, P * b:P * b + P], prob[:, i % 2, e, P * b:P * b + P], ident)
                        ins.then_inc(tr_filled, 1)

                def values(p, e, kb):
                    g, hp = PAIRS[p]
                    if g == "A":
                        return mla_v[:, kb, HD * (2 * hp + e):HD * (2 * hp + e) + HD]
                    if g == "B":
                        return rows_b[:, kb, 384 + HD * e:384 + HD * e + HD]
                    at = HD * (2 * hp + e) + (256 if g == "D" else 0)
                    return rows_v[:, kb, at:at + HD]

                def give_output(i):
                    p = ITEMS[i][0]
                    tiles = key_tiles(i)
                    pe.wait_ge(tr_drained, tr + (PT_NO[i, 1] + 1 + PAIR_CREDIT))
                    pe.wait_ge(o_drained, item0 + (i + 1))
                    for e in range(2):
                        for b, kb in enumerate(tiles):
                            ins = pe.matmul(G[:, 2 + i % 2, HD * e:HD * e + HD], probT[:, i % 2, e, P * b:P * b + P],
                                            values(p, e, kb), start=b == 0, stop=b == len(tiles) - 1)
                    ins.then_inc(o_filled, 1)

                give_qk(0)
                give_scores(0)
                for i in range(NI):
                    p = ITEMS[i][0]
                    if i % TT == 1 and p + 1 < len(PAIRS):
                        give_qk(p + 1)
                    if i + 1 < NI:
                        give_scores(i + 1)
                    give_probs(i)
                    if i:
                        give_output(i - 1)
                give_output(NI - 1)

                pe.wait_ge(o_drained, item0 + (NI + PAIR_CREDIT))
                pe.wait_ge(score_drained, item0 + (NI + PAIR_CREDIT))
                turn_rows(tr + TR_MIX, lambda k, t: mixed_rows("ABCD"[k // 2])[:, t, P * (k % 2):P * (k % 2) + P])
                pe.wait_ge(tr_drained, tr + (TR_MIX + KT + PAIR_CREDIT))
                for j in range(2):
                    product(unit + TT * (OUT_JOB + j), number + 2 * (OUT_JOB + j), in_rows(h_hi, h_lo))

                pe.wait_ge(xn_ready, l * 2 + 2)
                turn_rows(tr + TR_NORM2, lambda k, t: xn[:, t, P * k:P * k + P])
                with pe.Fori(0, FFN_GROUPS) as g:
                    pe.wait_ge(tr_drained, tr + (TR_NORM2 + KT + PAIR_CREDIT))
                    unit_g = unit + (g * (TT * GROUP_JOBS) + TT * FFN_JOB)
                    number_g = number + (g * (2 * GROUP_JOBS) + FIRST_GROUP_PIECE)
                    pe.wait_ge(bank_drained, unit_g + UNITS_CREDIT)
                    for j in range(2):
                        product(unit_g + TT * j, number_g + 2 * j, in_columns(h_hi, h_lo))
                    pe.wait_ge(hidden_split, l * LAYER_HIDDEN + (g * HIDDEN_UNITS + (HIDDEN_UNITS + PAIR_CREDIT)))
                    for j in range(2, GROUP_JOBS):
                        product(unit_g + TT * j, number_g + 2 * j, in_rows(u_hi, u_lo))
            second_tensor(pe, three, product, in_rows, in_columns, turn_rows, turn_unit)


_INS = ['x', 'norm1', 'w_in', 'mla_q_norm', 'mla_kv_norm', 'mla_w_uq', 'mla_w_ukv', 'swa_sinks', 'fox_b_f', 'w_out',
        'norm2', 'w_up', 'w_down', 'final_norm', 'c_2', 'norm_g_2', 'w_ada_2', 'b_ada_2', 'w_in_2', 'pool_w_2',
        'pool_scale_2', 'w_attn_br_2', 'w_pool_br_2', 'w_out_2', 'rel_bias_2', 'final_g_2']
_OUTS = [((1, 512, 1024), 'float32')]


def kernel(**inputs):
    import numpy as _np
    import concourse.bacc as _bacc
    from concourse import mybir as _mybir
    from concourse.bass_utils import run_bass_kernel_spmd as _run

    nc = _bacc.Bacc("TRN2", target_bir_lowering=False, num_devices=1)
    arrays, ins, outs = {}, {}, []
    for name in _INS:
        a = _np.ascontiguousarray(inputs[name])
        arrays[f"in_{name}_dram"] = a
        ins[name] = nc.dram_tensor(f"in_{name}_dram", a.shape, _mybir.dt.from_np(a.dtype), kind="ExternalInput").ap()
    for i, (shape, dtype) in enumerate(_OUTS):
        dt = _mybir.dt.from_np(_np.dtype(dtype))
        outs.append(nc.dram_tensor(f"out_{i}_dram", shape, dt, kind="ExternalOutput").ap())
    build(nc, ins, outs[0])
    r = _run(nc, [arrays], core_ids=[0])
    got = tuple(r.results[0][f"out_{i}_dram"] for i in range(len(_OUTS)))
    return got[0]
```

```python
from contextlib import ExitStack
import math

import numpy as np

import concourse.bass as bass
from concourse import mybir

F32 = mybir.dt.float32
F32R = mybir.dt.float32r
BF16 = mybir.dt.bfloat16
ALU = mybir.AluOpType
ACT = mybir.ActivationFunctionType
AX = mybir.AxisListType

P = 128
D_MODEL = 1024
SEQ = 512
DEPTH = 2
TT = SEQ // P
KT = D_MODEL // P
D_FF = 4 * D_MODEL
EPS = 1e-6
TOP_K = 128
HEADS = 4
HD = 64
MLA_ROPE = 32
MLA_QK = 96
ROUNDS = TOP_K // 8
FOX_K = HD + 2
NEG = -1e30
TAKEN = -3e38

A_COLS = (0, 416)
B_COLS = 416
C_COLS = (928, 1440)
CV_COLS = (1440, 1696)
IDX_COLS = (1696, 1992)
D_COLS = (1992, 2504)
DV_COLS = (2504, 2760)
DF_COLS = (2760, 2764)
IDX_W = IDX_COLS[1] - IDX_COLS[0]
A_W = A_COLS[1] - A_COLS[0] + 4

HALF_K = KT // 2
RAW_SLOTS = 4
SPLIT_SLOTS = 2

JOB_IDX, JOB_A, JOB_C, JOB_B, JOB_D, JOB_V = range(6)
PROJ_N = (IDX_W, A_W, 512, 512, 512, 512)
PROJ_JOBS = 6
OUT_JOB = PROJ_JOBS
FFN_JOB = OUT_JOB + 2
FFN_GROUPS = 4
GROUP_JOBS = 4
LAYER_JOBS = FFN_JOB + FFN_GROUPS * GROUP_JOBS
LAYER_UNITS = TT * LAYER_JOBS
LAYER_PIECES = 2 * LAYER_JOBS

TR_NORM1 = 0
TR_IDX = TR_NORM1 + KT
TR_MLA = TR_IDX + 3
TR_CUM = TR_MLA + 3
TR_NORM2 = TR_CUM + 2
LAYER_TR = TR_NORM2 + KT

PAIRS = [(g, hp) for g in "DBAC" for hp in range(2)]
ITEMS = [(p, qt) for p in range(len(PAIRS)) for qt in range(TT)]
NI = len(ITEMS)


def qk_units(p):
    return 4 if PAIRS[p][0] in "DA" else 2


def number_turns():
    qk = {(0, n): n for n in range(qk_units(0))}
    at, pt = qk_units(0), {}
    for i in range(NI + 1):
        p = ITEMS[min(i, NI - 1)][0]
        if i % TT == 1 and p + 1 < len(PAIRS):
            for n in range(qk_units(p + 1)):
                qk[p + 1, n] = at
                at += 1
        if i:
            for e in range(2):
                pt[i - 1, e] = at
                at += 1
    return qk, pt, at


QK_NO, PT_NO, LAYER_TURNS = number_turns()
HALF_TURNS = LAYER_TURNS // 2
SM_IDX = 0
SM_EXP = 3 * 8
LAYER_SM = SM_EXP + 2 * TT
LAYER_SC = NI
LAYER_OV = NI
assert LAYER_TR % 2 == 0 and LAYER_TURNS % 2 == 0 and LAYER_SM % 2 == 0


def rope_tables(dim):
    half = dim // 2
    inv = (np.float32(1.0) / np.power(np.float32(10000.0), np.arange(half, dtype=np.float32) * np.float32(2.0)
                                      / np.float32(dim)).astype(np.float32)).astype(np.float32)
    ang = (np.arange(SEQ, dtype=np.float32)[:, None] * inv[None, :]).astype(np.float32).astype(np.float64)
    tab = np.stack([np.cos(ang), np.sin(ang)]).astype(np.float32)
    return np.ascontiguousarray(tab.reshape(2, TT, P, half).transpose(2, 0, 1, 3))


def mask_tables():
    i, j = np.arange(P)[:, None], np.arange(P)[None, :]
    before = np.where(j > i, 0.0, NEG)
    causal = np.where(j <= i, 0.0, NEG)
    upto = np.where(i <= j, 1.0, 0.0)
    return np.concatenate([before, causal, upto, np.ones((P, P)), np.eye(P)], axis=1).astype(np.float32)


B2_GROUPS = (1, 2, 0)
B2_WINDOW = ((128, 1), (512, 4), (2048, 16))
B2_H = 8
B2_HEADS = B2_H * len(B2_WINDOW)
STRIDE = 4
NUM_BUCKETS = 32
SKEW = 3 * P
PACK = B2_H * HD + 2 * B2_H
POOL_WINDOWS = (2, 4, 8, 16)
PAD = 16
D_ATTN = B2_H * HD
COL_QKV = 0
COL_Z = 3 * 3 * D_ATTN
COL_U = COL_Z + D_ATTN
COL_ZP = COL_U + 512
COL_GA = COL_ZP + 512
COL_GP = COL_GA + D_MODEL

ADA = 0
QKV = 6
Z_JOB, U_JOB, ZP_JOB = 15, 16, 17
GATE_JOBS = 18
BRANCH = 22
OUT2 = 24
UNIT0 = DEPTH * LAYER_UNITS
PIECE0 = DEPTH * LAYER_PIECES
TR0 = DEPTH * LAYER_TR

SM2_BIAS = DEPTH * LAYER_SM
SM2_POOL = SM2_BIAS + B2_HEADS
SC0 = DEPTH * LAYER_SC
OV0 = DEPTH * LAYER_OV
TOTAL_PIECES = PIECE0 + 2 * (OUT2 + 2)
assert TOTAL_PIECES % RAW_SLOTS == 0


def unit2(job):
    return UNIT0 + TT * job + TT * max(0, job - BRANCH if job < OUT2 else 2)


def piece2(job):
    return PIECE0 + 2 * job


def items2(g):
    if g:
        return [(g, m, 0, 4, 1) for m in range(TT)]
    return [(g, m, 2 * a, 2, 2 if m else 1) for m in range(TT) for a in range(2)]


ITEMS2 = {g: items2(g) for g in B2_GROUPS}


def item_base(g):
    return sum(len(ITEMS2[x]) for x in B2_GROUPS[:B2_GROUPS.index(g)])


TR2_MOD = TR0
TR2_NORM = TR2_MOD + 4
TR2_ATT = TR2_NORM + KT
TR2_Z = TR2_ATT + 2 * sum(len(x) for x in ITEMS2.values())


def bucket_tables():
    hot = np.zeros((NUM_BUCKETS + 1, 3, SKEW), np.float32)
    for g, (win, dil) in enumerate(B2_WINDOW):
        step = dil if g < 2 else STRIDE
        for u in range(SKEW):
            n = (2 * P - 1 - u) * step
            if n < 0 or n % dil or n // dil > win // dil:
                hot[NUM_BUCKETS, g, u] = 1.0
                continue
            half = NUM_BUCKETS // 2
            ratio = np.log(np.float32(max(n, 1)) / np.float32(half)) / np.float32(math.log(2048 / half))
            large = min(half + int(np.float32(ratio) * np.float32(NUM_BUCKETS - half)), NUM_BUCKETS - 1)
            hot[n if n < half else large, g, u] = 1.0
    return hot


def count_table():
    t = np.arange(PAD)
    inv = np.stack([1.0 / np.minimum(t + 1, w) for w in POOL_WINDOWS])
    return np.broadcast_to(inv[None], (P, len(POOL_WINDOWS), PAD)).astype(np.float32).copy()


PROJ_PARTS = {JOB_IDX: (IDX_COLS,), JOB_A: (A_COLS, DF_COLS), JOB_C: (C_COLS,),
              JOB_B: ((416, 480), (544, 608), (480, 544), (608, 928)),
              JOB_D: (D_COLS,), JOB_V: (CV_COLS, DV_COLS)}


def loads_upto(c):
    parts = [len(PROJ_PARTS[x // 2]) if x // 2 < PROJ_JOBS else 1 for x in range(c + 1) if x % RAW_SLOTS == c % RAW_SLOTS]
    return 16 * sum(parts)


FIRST_GROUP_PIECE = 2 * FFN_JOB
LOADS_TO_GROUPS = [loads_upto(FIRST_GROUP_PIECE - RAW_SLOTS + s) for s in range(RAW_SLOTS)]
GROUP_LOADS = 16 * 2 * GROUP_JOBS // RAW_SLOTS
LAYER_LOADS = [x + FFN_GROUPS * GROUP_LOADS for x in LOADS_TO_GROUPS]
assert FIRST_GROUP_PIECE % RAW_SLOTS == 0
HI_PER_LAYER = 3 * KT
HIDDEN_UNITS = 2 * TT
LAYER_HIDDEN = FFN_GROUPS * HIDDEN_UNITS
UNITS_CREDIT, PAIR_CREDIT = TT, 2


class Steps:

    def __init__(self, eng, sem):
        self.eng, self.sem, self.n = eng, sem, 0

    def done(self, ins):
        self.n += 1
        ins.then_inc(self.sem, 1)
        self.eng.wait_ge(self.sem, self.n)

    def restart(self):
        self.eng.sem_clear(self.sem)
        self.n = 0


class Room:

    def __init__(self, nc, at):
        self.nc, self.at = nc, at

    def place(self, name, shape, dt=F32):
        t = self.nc.alloc_sbuf_tensor_at(name, shape, dt, offset=self.at)
        self.at += -(-(2 if dt == BF16 else 4) * math.prod(shape[1:]) // 32) * 32
        return t


def build(nc, A, out):
    ctx = ExitStack()
    with ctx:
        def sem(name):
            return ctx.enter_context(nc.semaphore(name))

        c_rope64 = nc.inline_tensor(rope_tables(HD), "rope64_table")
        c_rope32 = nc.inline_tensor(rope_tables(MLA_ROPE), "rope32_table")
        c_mask = nc.inline_tensor(mask_tables(), "mask_table")
        c_hot = nc.inline_tensor(bucket_tables(), "bucket_table")
        c_count = nc.inline_tensor(count_table(), "count_table")
        skew_dram = nc.dram_tensor("skew_scratch", [B2_HEADS, P, SKEW], F32, kind="Internal").ap()
        merge_dram = nc.dram_tensor("merge_scratch", [SEQ, PACK], F32, kind="Internal").ap()

        base = Room(nc, -(-nc.sbuf_base // 64) * 64)
        X = base.place("X", [P, TT, D_MODEL])
        raw = base.place("raw", [P, RAW_SLOTS, HALF_K, 512])
        w_hi = base.place("w_hi", [P, SPLIT_SLOTS, HALF_K, 512], F32R)
        w_lo = base.place("w_lo", [P, SPLIT_SLOTS, HALF_K, 512], F32R)
        masks = base.place("masks", [P, 5 * P])
        window, causal, upto = masks[:, 0:2 * P], masks[:, P:2 * P], masks[:, 2 * P:3 * P]
        ones, ident = masks[:, 3 * P:4 * P], masks[:, 4 * P:5 * P]
        rope64 = base.place("rope64", [P, 2, TT, HD // 2])
        rope32 = base.place("rope32", [P, 2, TT, MLA_ROPE // 2])
        gain1, gain2 = base.place("gain1", [P, KT]), base.place("gain2", [P, KT])
        q_gain, kv_gain = base.place("q_gain", [P, 2]), base.place("kv_gain", [P, 1])
        sinks, gate_bias = base.place("sinks", [P, HEADS]), base.place("gate_bias", [P, HEADS])
        sumsq, var, std = (base.place(n, [P, TT]) for n in ("sumsq", "var", "std"))
        rstd, newton = (base.place(n, [P, TT]) for n in ("rstd", "newton"))
        m_sumsq, m_var, m_std, m_rstd, m_newton = (
            base.place(n, [P, 2 * TT]) for n in ("m_sumsq", "m_var", "m_std", "m_rstd", "m_newton"))
        top8 = base.place("top8", [P, 8])
        neg_max = base.place("neg_max", [P, 2, 2])
        row_sum, sink_term = base.place("row_sum", [P, 4, 2]), base.place("sink_term", [P, 4, 2])
        inv_sum = base.place("inv_sum", [P, 4, 2])
        hT_at = base.at
        room = Room(nc, hT_at)
        h_hi, h_lo = room.place("h_hi", [P, KT, SEQ], F32R), room.place("h_lo", [P, KT, SEQ], F32R)
        free_at = room.at
        room = Room(nc, hT_at)
        qkT = room.place("qkT", [P, 2, 4, SEQ])
        prob = room.place("prob", [P, 2, 2, SEQ])
        probT = room.place("probT", [P, 2, 2, SEQ])
        assert room.at <= free_at

        room = Room(nc, free_at)
        rows_idx = room.place("rows_idx", [P, TT, IDX_W])
        rows_a = room.place("rows_a", [P, TT, A_W])
        xn_at = room.at
        rows_b, rows_c = room.place("rows_b", [P, TT, 512]), room.place("rows_c", [P, TT, 512])
        early = Room(nc, room.at)
        cqT, ckvT = early.place("cqT", [P, 2, SEQ]), early.place("ckvT", [P, SEQ])
        rows_v = room.place("rows_v", [P, TT, 512])
        assert early.at <= room.at
        fox_q, fox_k = (room.place(n, [P, TT, HEADS, FOX_K]) for n in ("fox_q", "fox_k"))
        mla_q, mla_k = (room.place(n, [P, TT, HEADS, MLA_QK]) for n in ("mla_q", "mla_k"))
        mla_v = room.place("mla_v", [P, TT, HEADS * HD])
        dead_at = room.at
        w_uq, w_ukv = room.place("w_uq", [P, 2, HEADS * MLA_QK]), room.place("w_ukv", [P, HEADS * 2 * HD])
        k_idx4 = room.place("k_idx4", [P, TT, 4 * 32])
        qiT, kiT = room.place("qiT", [P, 2, SEQ]), room.place("kiT", [P, SEQ])
        select = room.place("select", [P, (2 + 3 + 4) * P])
        work, rel = room.place("work", [P, SEQ]), room.place("rel", [P, 2, SEQ])
        turn = room.place("turn", [P, 4, 8 * HD // 2])
        gate_z, gate_a, gate_e, log_f = (
            room.place(n, [P, TT, HEADS]) for n in ("gate_z", "gate_a", "gate_e", "log_f"))
        mixT_da = Room(nc, free_at).place("mixT_da", [P, 4, SEQ])
        mixT_bc = Room(nc, dead_at).place("mixT_bc", [P, 4, SEQ])
        ident_few, window_few = room.place("ident_few", [P, P], BF16), room.place("window_few", [P, 2 * P], BF16)
        room = Room(nc, xn_at)
        xn = room.place("xn", [P, TT, D_MODEL])
        u_hi, u_lo = room.place("u_hi", [P, KT, SEQ], F32R), room.place("u_lo", [P, KT, SEQ], F32R)
        relu, square = room.place("relu", [P, 2, SEQ]), room.place("square", [P, SEQ])
        room = Room(nc, free_at)
        xn2 = room.place("xn2", [P, TT, D_MODEL])
        cb_hi, cb_lo = room.place("cb_hi", [P, KT, P], F32R), room.place("cb_lo", [P, KT, P], F32R)
        h_full = room.place("h_full", [P, 2, SEQ])
        hot = room.place("hot", [P, 3, SKEW])
        stage_at = room.at
        stage = room.place("stage", [P, B2_HEADS, SKEW])
        rel_wide = room.place("rel_wide", [P, B2_HEADS, P])
        last_at = room.at
        room = Room(nc, free_at)
        qkv = room.place("qkv", [P, 16, SEQ])
        assert room.at <= stage_at
        room = Room(nc, stage_at)
        bias_far = room.place("bias_far", [P, 2, B2_H, P])
        bias_near = room.place("bias_near", [P, B2_H, 2 * P])
        prob2, probT2 = room.place("prob2", [P, 2, 2, SEQ]), room.place("probT2", [P, 2, 2, SEQ])
        sum_a, sum_b = room.place("sum_a", [P, TT, PACK]), room.place("sum_b", [P, TT, PACK])
        last_at = max(last_at, room.at)
        room = Room(nc, stage_at)
        at_hi, at_lo = room.place("at_hi", [P, 4, SEQ], F32R), room.place("at_lo", [P, 4, SEQ], F32R)
        pt_hi, pt_lo = room.place("pt_hi", [P, 4, SEQ], F32R), room.place("pt_lo", [P, 4, SEQ], F32R)
        win = room.place("win", [P, 3, PAD + SEQ])
        pool_w = room.place("pool_w", [P, 4, P])
        assert room.at <= last_at
        room = Room(nc, last_at)
        gate_row, gain_row = room.place("gate_row", [P, D_MODEL]), room.place("gain_row", [P, D_MODEL])
        rel_row = room.place("rel_row", [P, B2_HEADS])
        mod_b, mod = room.place("mod_b", [P, 2 * KT]), room.place("mod", [P, 2 * KT])
        norm_col, c_col, pool_gain = (
            room.place(n, [P, k]) for n, k in (("norm_col", KT), ("c_col", KT), ("pool_gain", 4)))
        inv_count = room.place("inv_count", [P, len(POOL_WINDOWS), PAD])
        head_max, head_neg, head_sum = (
            room.place(n, [P, 3, TT, B2_H]) for n in ("head_max", "head_neg", "head_sum"))
        best, part_a, part_b = (room.place(n, [P, TT, B2_H]) for n in ("best", "part_a", "part_b"))

        G = ctx.enter_context(nc.psum_tensor("G", [P, 4, 512], F32))
        S = ctx.enter_context(nc.psum_tensor("S", [P, 4, 512], F32))

        x_loaded, const_loaded = sem("x_loaded"), sem("const_loaded")
        slots_cleared = sem("slots_cleared")
        params_loaded, mla_w_loaded = sem("params_loaded"), sem("mla_w_loaded")
        raw_loaded = [sem(f"raw_loaded{i}") for i in range(RAW_SLOTS)]
        high_ready, low_ready = sem("high_ready"), sem("low_ready")
        pieces_asked = sem("pieces_asked")
        half_used = sem("half_used")
        bank_filled, bank_drained = sem("bank_filled"), sem("bank_drained")
        tr_filled, tr_drained = sem("tr_filled"), sem("tr_drained")
        turn_filled, even_drained, odd_drained = (
            sem(n) for n in ("turn_filled", "even_drained", "odd_drained"))
        inv_ready, prob_scaled = sem("inv_ready"), sem("prob_scaled")
        small_filled, small_drained = sem("small_filled"), sem("small_drained")
        score_filled, score_drained = sem("score_filled"), sem("score_drained")
        o_filled, o_drained = sem("o_filled"), sem("o_drained")
        sumsq_ready, var_ready, std_ready, xn_ready = (
            sem(n) for n in ("sumsq_ready", "var_ready", "std_ready", "xn_ready"))
        m_sumsq_ready, m_var_ready, m_std_ready, m_rows_ready = (
            sem(n) for n in ("m_sumsq_ready", "m_var_ready", "m_std_ready", "m_rows_ready"))
        hi_ready = sem("hi_ready")
        mix_split = sem("mix_split")
        idx_rows_ready, gate_abs_ready, gate_exp_ready, log_f_ready = (
            sem(n) for n in ("idx_rows_ready", "gate_abs_ready", "gate_exp_ready", "log_f_ready"))
        heads_ready = sem("heads_ready")
        rel_used, neg_max_ready, hidden_split = sem("rel_used"), sem("neg_max_ready"), sem("hidden_split")
        dve_step = sem("dve_step")
        b2_loaded, gain2_loaded, c_ready = sem("b2_loaded"), sem("gain2_loaded"), sem("c_ready")
        rel_ready, skew_saved, bias_loaded = (
            sem(n) for n in ("rel_ready", "skew_saved", "bias_loaded"))
        x_scaled, hot_loaded, pool_w_loaded = sem("x_scaled"), sem("hot_loaded"), sem("pool_w_loaded")
        mod_ready, full_ready, neg2_ready, prob2_ready = (
            sem(n) for n in ("mod_ready", "full_ready", "neg2_ready", "prob2_ready"))
        combine_max, combine_exp = sem("combine_max"), sem("combine_exp")
        pack_ready, pack_saved, pack_loaded = sem("pack_ready"), sem("pack_saved"), sem("pack_loaded")
        z_rows_ready, sigma_ready, pooled_ready = sem("z_rows_ready"), sem("sigma_ready"), sem("pooled_ready")
        split_ready, out_ready, out_saved = sem("split_ready"), sem("out_ready"), sem("out_saved")

        block = ctx.enter_context(nc.Block())

        def weights2(job, half):
            if job < QKV:
                w, c0, k0 = A["w_ada_2"], 512 * job, half * HALF_K
            elif job < Z_JOB:
                g, s = B2_GROUPS[(job - QKV) // 3], (job - QKV) % 3
                w, c0, k0 = A["w_in_2"], COL_QKV + (3 * g + s) * D_ATTN, half * HALF_K
            elif job < BRANCH:
                c0 = {Z_JOB: COL_Z, U_JOB: COL_U, ZP_JOB: COL_ZP, GATE_JOBS: COL_GA, GATE_JOBS + 1: COL_GA + 512,
                      GATE_JOBS + 2: COL_GP, GATE_JOBS + 3: COL_GP + 512}[job]
                w, k0 = A["w_in_2"], half * HALF_K
            elif job < OUT2:
                w, c0, k0 = A["w_pool_br_2"] if half else A["w_attn_br_2"], 512 * (job - BRANCH), 0
            else:
                w, c0, k0 = A["w_out_2"], 512 * (job - OUT2), half * HALF_K
            return w[0, k0 * P:(k0 + HALF_K) * P, c0:c0 + 512].rearrange("(k p) n -> p k n", p=P)

        def skewed(h0, heads, first, width):
            return bass.AP(tensor=skew_dram.tensor, offset=h0 * P * SKEW + P - 1 + first,
                           ap=[[SKEW - 1, P], [P * SKEW, heads], [1, width]])

        def second_loads(sp):
            sp.wait_ge(tr_drained, TR0 + PAIR_CREDIT)
            column = lambda v: v.rearrange("(k p) -> p k", p=P)
            for dst, src in (
                (c_col[:], column(A["c_2"][0, :])),
                (rel_row[0:NUM_BUCKETS, :], A["rel_bias_2"]),
                (gain_row[:], A["final_norm"].unsqueeze(0).broadcast_to([P, D_MODEL])),
                (norm_col[:], column(A["norm_g_2"][0, :])),
                (mod_b[:], column(A["b_ada_2"][0, 0:2 * D_MODEL])),
                (gate_row[:], A["b_ada_2"][0:1, 2 * D_MODEL:3 * D_MODEL].broadcast_to([P, D_MODEL])),
                (pool_gain[:], column(A["pool_scale_2"][0, :])),
                (inv_count[:], c_count[:, :, :]),
            ):
                sp.dma_start(dst, src, allow_slow_non_contiguous=True).then_inc(b2_loaded, 16)
            for job in range(OUT2 + 2):
                for half in range(2):
                    c = 2 * job + half
                    sp.wait_ge(low_ready, PIECE0 + c + 1)
                    sp.dma_start(raw[:, c % RAW_SLOTS], weights2(job, half)).then_inc(raw_loaded[c % RAW_SLOTS], 16)
                if job == 1:
                    sp.wait_ge(bank_drained, UNIT0 + UNITS_CREDIT)
                    sp.dma_start(hot[0:NUM_BUCKETS + 1], c_hot[:, :, :]).then_inc(hot_loaded, 16)
                if job == QKV:
                    sp.wait_ge(small_drained, SM2_BIAS + B2_HEADS + PAIR_CREDIT)
                    sp.dma_start(skew_dram.rearrange("h p u -> p h u"), stage[:]).then_inc(skew_saved, 16)
                    sp.wait_ge(x_scaled, 1)
                    sp.dma_start(gain_row[:], A["final_g_2"].unsqueeze(0).broadcast_to([P, D_MODEL])
                                 ).then_inc(gain2_loaded, 16)
                    sp.wait_ge(skew_saved, 16)
                    for g in (1, 2):
                        sp.dma_start(bias_far[:, g - 1], skewed(g * B2_H, B2_H, P, P)).then_inc(bias_loaded, 16)
                    sp.dma_start(bias_near[:], skewed(0, B2_H, 0, 2 * P)).then_inc(bias_loaded, 16)
                if job == QKV + 7:
                    sp.wait_ge(pack_ready, 1)
                    sp.dma_start(merge_dram.rearrange("(p m) c -> p m c", m=STRIDE), sum_a[:]).then_inc(pack_saved, 16)
                    sp.wait_ge(pack_saved, 16)
                    sp.dma_start(sum_b[:], merge_dram.rearrange("(t p) c -> p t c", p=P)).then_inc(pack_loaded, 16)
                if job == ZP_JOB:
                    sp.wait_ge(z_rows_ready, 1)
                    sp.dma_start(pool_w[:], A["pool_w_2"][0].rearrange("g c e -> c g e")).then_inc(pool_w_loaded, 16)
            for t in range(TT):
                sp.wait_ge(out_ready, t + 1)
                sp.dma_start(out[0, P * t:P * t + P, :], X[:, t, :]).then_inc(out_saved, 16)
            sp.wait_ge(out_saved, 16 * TT)

        def own(g, v, blocks):
            return v[:, :, P:2 * P] if not g and blocks == 1 else v

        def by_tile(g, v):
            return v.rearrange("p (n w) -> p n w", w=P if g else 2 * P)

        def second_scalar(act, split_high, square_sums):
            def ahead(job, half):
                c = 2 * (job + 1) + half
                s = c % RAW_SLOTS
                act.wait_ge(raw_loaded[s], DEPTH * LAYER_LOADS[s] + 16 * (c // RAW_SLOTS + 1))
                if half:
                    act.wait_ge(bank_filled, unit2(job + 1))
                elif BRANCH <= job < OUT2:
                    act.wait_ge(bank_filled, unit2(job) + TT)
                else:
                    act.wait_ge(half_used, DEPTH * LAYER_JOBS + job + 1 - (2 if job >= OUT2 else 0))
                act.activation(w_hi[:, c % SPLIT_SLOTS], raw[:, c % RAW_SLOTS], ACT.Copy).then_inc(high_ready, 1)

            def columns_out(job, place, func=ACT.Copy, scale=1.0):
                for t in range(TT):
                    act.wait_ge(bank_filled, unit2(job) + t + 1)
                    act.activation(qkv[:, place + t, :], G[:, t, :], func, scale=scale).then_inc(bank_drained, 1)

            def bias_rows(job):
                for h in range(4 * job, 4 * job + 4):
                    act.wait_ge(small_filled, SM2_BIAS + h + 1)
                    act.activation(stage[:, h, :], S[:, h % 2, 0:SKEW], ACT.Copy).then_inc(small_drained, 1)

            square_sums(2 * DEPTH, xn2, lambda t: act.wait_ge(bank_drained, UNIT0 + t + 1))
            ahead(ADA, 0)
            ahead(ADA, 1)
            bias_rows(0)
            ahead(ADA + 1, 0)
            act.wait_ge(x_scaled, 1)
            square_sums(2 * DEPTH + 1, xn2)
            ahead(ADA + 1, 1)
            bias_rows(1)
            for job in range(2, QKV):
                ahead(job, 0)
                ahead(job, 1)
                bias_rows(job)
            act.wait_ge(mod_ready, 1)
            for k in range(KT):
                act.wait_ge(tr_filled, TR2_NORM + k + 1)
                if k >= 2:
                    act.wait_ge(tr_drained, TR2_NORM + k - 1 + PAIR_CREDIT)
                act.activation(h_full[:, k % 2, :], S[:, k % 4, :], ACT.Identity, scale=mod[:, KT + k:KT + k + 1],
                               bias=mod[:, k:k + 1]).then_inc(full_ready, 1)
            for gn, g in enumerate(B2_GROUPS):
                for s in range(3):
                    job = QKV + 3 * gn + s
                    ahead(job, 0)
                    if gn == 0 and s == 0:
                        act.wait_ge(skew_saved, 16)
                    columns_out(job, 4 * s)
                    ahead(job, 1)
                for i, (_, m, tile0, tiles, blocks) in enumerate(ITEMS2[g]):
                    it = item_base(g) + i
                    act.wait_ge(neg2_ready, it + 1)
                    for e in range(2):
                        part = own(g, by_tile(g, prob2[:, it % 2, e, :]), blocks)
                        for n in range(tiles):
                            h = 2 * (tile0 + n) + e
                            ins = act.activation(part[:, n, :], part[:, n, :], ACT.Exp,
                                                 bias=head_neg[:, g, m, h:h + 1],
                                                 accum_out=head_sum[:, g, m, h:h + 1])
                    ins.then_inc(prob2_ready, 1)
                if g != B2_GROUPS[0]:
                    n = gn
                    act.wait_ge(combine_max, n)
                    act.activation(part_a[:], part_a[:], ACT.Exp)
                    act.activation(part_b[:], part_b[:], ACT.Exp).then_inc(combine_exp, 1)

            def negative_exps(job, place):
                for t in range(TT):
                    act.wait_ge(bank_filled, unit2(job) + t + 1)
                    act.activation(qkv[:, place + t, :], G[:, t, :], ACT.Exp, scale=-1.0).then_inc(sigma_ready, 1)

            ahead(Z_JOB, 0)
            negative_exps(Z_JOB, 0)
            ahead(Z_JOB, 1)
            ahead(U_JOB, 0)
            columns_out(U_JOB, 4)
            ahead(U_JOB, 1)
            ahead(ZP_JOB, 0)
            negative_exps(ZP_JOB, 8)
            ahead(ZP_JOB, 1)
            for n in range(4):
                ahead(GATE_JOBS + n, 0)
                if n == 0:
                    act.wait_ge(split_ready, 1)
                columns_out(GATE_JOBS + n, 4 * n, ACT.Exp, -1.0)
                ahead(GATE_JOBS + n, 1)
            for job in range(BRANCH, OUT2 + 1):
                ahead(job, 0)
                ahead(job, 1)
            act.wait_ge(x_scaled, 2)
            square_sums(2 * DEPTH + 2, xn2)

        def second_vector(dve, step, root, normal_rows):
            dve.wait_ge(b2_loaded, 8 * 16)
            wide = c_col[:].unsqueeze(2).broadcast_to([P, KT, P])
            step.done(dve.tensor_copy(cb_hi[:], wide))
            dve.tensor_tensor(cb_lo[:], wide, cb_hi[:].bitcast(F32), ALU.subtract).then_inc(c_ready, 1)
            step.done(dve.memset(rel_row[NUM_BUCKETS:NUM_BUCKETS + 1, :], NEG))
            dve.tensor_copy(rel_wide[0:NUM_BUCKETS + 1], rel_row[0:NUM_BUCKETS + 1, :].unsqueeze(2).broadcast_to(
                [NUM_BUCKETS + 1, B2_HEADS, P])).then_inc(rel_ready, 1)

            def scaled_rows(norm_no):
                dve.wait_ge(sumsq_ready, norm_no + 1)
                dve.tensor_scalar(var[:], sumsq[:], 1.0 / D_MODEL, EPS, ALU.mult, ALU.add).then_inc(var_ready, 1)
                dve.wait_ge(std_ready, norm_no + 1)
                root(var[:], std[:], rstd[:], newton[:])
                for t in range(TT):
                    yield dve.scalar_tensor_tensor(X[:, t, :], X[:, t, :], rstd[:, t:t + 1], gain_row[:], ALU.mult, ALU.mult)

            def take_modulation(job):
                dve.wait_ge(bank_filled, unit2(job) + TT)
                if job < 4:
                    if job >= 2:
                        dve.wait_ge(tr_filled, TR2_MOD + job - 1)
                    ins = dve.tensor_copy(h_full[:, job % 2, :], G[:, job, :])
                else:
                    at = slice(512 * (job - 4), 512 * (job - 3))
                    ins = dve.tensor_tensor(gate_row[:, at], G[:, job - 4, :], gate_row[:, at], ALU.add)
                ins.then_inc(bank_drained, TT)

            def modulation_columns(job):
                at = slice(4 * job, 4 * job + 4)
                dve.wait_ge(tr_filled, TR2_MOD + job + 1)
                dve.tensor_tensor(mod[:, at], S[:, 2 + job % 2, 0::P], mod_b[:, at], ALU.add).then_inc(tr_drained, 1)

            for ins in scaled_rows(2 * DEPTH):
                pass
            ins.then_inc(x_scaled, 1)
            dve.wait_ge(x_scaled, 1)
            take_modulation(0)
            normal_rows(2 * DEPTH + 1, xn2).then_inc(xn_ready, 1)
            for job in range(1, QKV):
                take_modulation(job)
                if job <= 4:
                    modulation_columns(job - 1)
            dve.wait_ge(tr_drained, TR2_NORM + PAIR_CREDIT)
            dve.scalar_tensor_tensor(mod[:, KT:2 * KT], mod[:, KT:2 * KT], 1.0, norm_col[:], ALU.add,
                                     ALU.mult).then_inc(mod_ready, 1)
            for k in range(KT):
                dve.wait_ge(full_ready, k + 1)
                step.done(dve.tensor_copy(h_hi[:, k, :], h_full[:, k % 2, :]))
                dve.tensor_tensor(h_lo[:, k, :], h_full[:, k % 2, :], h_hi[:, k, :].bitcast(F32),
                                  ALU.subtract).then_inc(tr_drained, 1)

            def row_maxima(g, i):
                it = item_base(g) + i
                _, m, tile0, tiles, blocks = ITEMS2[g][i]
                dve.wait_ge(score_filled, SC0 + it + 1)
                for e in range(2):
                    table = bias_far[:, g - 1] if g else bias_near[:]
                    heads = slice(2 * tile0 + e, 2 * (tile0 + tiles) + e - 1, 2)
                    ins = dve.scalar_tensor_tensor(
                        own(g, by_tile(g, prob2[:, it % 2, e, :]), blocks),
                        own(g, by_tile(g, S[:, 2 * (it % 2) + e, :]), blocks), HD ** -0.5,
                        own(g, table[:, heads, :], blocks), ALU.mult, ALU.add)
                ins.then_inc(score_drained, 1)
                dve.wait_ge(score_drained, SC0 + it + 1 + PAIR_CREDIT)
                for e in range(2):
                    heads = slice(2 * tile0 + e, 2 * (tile0 + tiles) + e - 1, 2)
                    ins = dve.tensor_reduce(head_max[:, g, m, heads], own(g, by_tile(g, prob2[:, it % 2, e, :]), blocks),
                                            AX.X, ALU.max)
                step.done(ins)
                heads = slice(2 * tile0, 2 * (tile0 + tiles))
                dve.tensor_scalar(head_neg[:, g, m, heads], head_max[:, g, m, heads], -1.0, None,
                                  ALU.mult).then_inc(neg2_ready, 1)

            def take_probs(g, i):
                it = item_base(g) + i
                blocks = ITEMS2[g][i][4]
                if it >= 2:
                    dve.wait_ge(o_filled, OV0 + it - 1)
                for e in range(2):
                    dve.wait_ge(tr_filled, TR2_ATT + 2 * it + e + 1)
                    dve.tensor_copy(own(g, by_tile(g, probT2[:, it % 2, e, :]), blocks),
                                    own(g, by_tile(g, G[:, e, :]), blocks)).then_inc(tr_drained, 1)

            def take_output(g, i):
                it = item_base(g) + i
                _, m, tile0, tiles, _ = ITEMS2[g][i]
                dve.wait_ge(o_filled, OV0 + it + 1)
                n = 2 * HD * tiles
                rows = sum_b if g == 2 else sum_a
                dve.tensor_copy(rows[:, m, 2 * HD * tile0:2 * HD * tile0 + n], G[:, 2 + it % 2, 0:n]).then_inc(o_drained, 1)

            ov, om, od = slice(0, D_ATTN), slice(D_ATTN, D_ATTN + B2_H), slice(D_ATTN + B2_H, PACK)

            def heads_of(v):
                return v.rearrange("p (h d) -> p h d", h=B2_H)

            def combine(no, m_a, d_a, m_b, d_b, last):
                step.done(dve.tensor_tensor(best[:], m_a, m_b, ALU.max))
                dve.tensor_tensor(part_a[:], m_a, best[:], ALU.subtract)
                dve.tensor_tensor(part_b[:], m_b, best[:], ALU.subtract).then_inc(combine_max, 1)
                dve.wait_ge(combine_exp, no)
                dve.tensor_tensor(d_a, d_a, part_a[:], ALU.mult)
                step.done(dve.tensor_tensor(d_b, d_b, part_b[:], ALU.mult))
                total = head_sum[:, 0] if last else sum_a[:, :, od]
                step.done(dve.tensor_tensor(total, d_a, d_b, ALU.add))
                if last:
                    step.done(dve.reciprocal(best[:], total))
                    dve.tensor_tensor(part_a[:], part_a[:], best[:], ALU.mult)
                    step.done(dve.tensor_tensor(part_b[:], part_b[:], best[:], ALU.mult))
                else:
                    dve.tensor_copy(sum_a[:, :, om], best[:])
                for rows, part in ((sum_a, part_a), (sum_b, part_b)):
                    for t in range(TT):
                        ins = dve.tensor_tensor(heads_of(rows[:, t, ov]), heads_of(rows[:, t, ov]),
                                                part[:, t, :].unsqueeze(2).broadcast_to([P, B2_H, HD]), ALU.mult)
                step.done(ins)
                for t in range(TT):
                    dst = qkv[:, 12 + t, :] if last else sum_a[:, t, ov]
                    ins = dve.tensor_tensor(dst, sum_a[:, t, ov], sum_b[:, t, ov], ALU.add)
                return ins

            dve.wait_ge(bias_loaded, 3 * 16)
            for gn, g in enumerate(B2_GROUPS):
                row_maxima(g, 0)
                n = len(ITEMS2[g])
                for i in range(n):
                    if i + 1 < n:
                        row_maxima(g, i + 1)
                    take_probs(g, i)
                    if i:
                        if g == 0 and i == 1:
                            dve.wait_ge(pack_saved, 16)
                        take_output(g, i - 1)
                take_output(g, n - 1)
                dve.wait_ge(o_drained, OV0 + item_base(g) + n + PAIR_CREDIT)
                if gn == 1:
                    combine(1, head_max[:, 1], head_sum[:, 1], head_max[:, 2], head_sum[:, 2], False
                            ).then_inc(pack_ready, 1)
            dve.wait_ge(pack_loaded, 16)
            step.done(combine(2, head_max[:, 0], head_sum[:, 0], sum_b[:, :, om], sum_b[:, :, od], True))

            def gated(job, place, first):
                for t in range(TT):
                    dve.wait_ge(sigma_ready, first + t + 1)
                    e = qkv[:, place + t, :]
                    step.done(dve.tensor_scalar(e, e, 1.0, None, ALU.add))
                    step.done(dve.reciprocal(e, e))
                    dve.tensor_tensor(e, e, G[:, t, :], ALU.mult).then_inc(bank_drained, 1)
                dve.wait_ge(bank_drained, unit2(job + 1) + UNITS_CREDIT)

            def two_parts(hi, lo, src):
                step.done(dve.tensor_copy(hi, src))
                return dve.tensor_tensor(lo, src, hi.bitcast(F32), ALU.subtract)

            gated(Z_JOB, 0, 0)
            for t in range(TT):
                ins = dve.tensor_tensor(qkv[:, 12 + t, :], qkv[:, 12 + t, :], qkv[:, t, :], ALU.mult)
            ins.then_inc(z_rows_ready, 1)
            for k in range(4):
                dve.wait_ge(tr_filled, TR2_Z + k + 1)
                two_parts(at_hi[:, k, :], at_lo[:, k, :], S[:, 2 + k % 2, :]).then_inc(tr_drained, 1)
            step.done(dve.memset(win[:, :, 0:PAD], 0.0))
            dve.wait_ge(bank_drained, unit2(U_JOB + 1) + UNITS_CREDIT)
            dve.wait_ge(tr_drained, TR2_Z + 4 + PAIR_CREDIT)
            for g, w in enumerate(POOL_WINDOWS):
                u, pooled = qkv[:, 4 + g, :], qkv[:, 12 + g, :]
                step.done(dve.tensor_copy(win[:, 0, PAD:], u))
                at = 0
                for n in range(g + 1):
                    step.done(dve.tensor_tensor(win[:, 1 + n % 2, PAD:], win[:, at, PAD:],
                                                win[:, at, PAD - 2 ** n:PAD + SEQ - 2 ** n], ALU.add))
                    at = 1 + n % 2
                step.done(dve.scalar_tensor_tensor(pooled, win[:, at, PAD:], 1.0 / w, u, ALU.mult, ALU.subtract))
                step.done(dve.tensor_tensor(win[:, at, PAD:2 * PAD], win[:, at, PAD:2 * PAD], inv_count[:, g, :], ALU.mult))
                ins = dve.tensor_tensor(pooled[:, 0:PAD], win[:, at, PAD:2 * PAD], u[:, 0:PAD], ALU.subtract)
                ins.then_inc(pooled_ready, 1)
                dve.wait_ge(pooled_ready, g + 1)
            gated(ZP_JOB, 8, TT)
            for g in range(4):
                dve.wait_ge(small_filled, SM2_POOL + g + 1)
                full = win[:, g % 2, PAD:]
                dve.scalar_tensor_tensor(full, S[:, g % 2, :], pool_gain[:, g:g + 1], qkv[:, 8 + g, :], ALU.mult,
                                         ALU.mult).then_inc(small_drained, 1)
                dve.wait_ge(small_drained, SM2_POOL + g + 1 + PAIR_CREDIT)
                step.done(two_parts(pt_hi[:, g, :], pt_lo[:, g, :], full))
            dve.engine_nop().then_inc(split_ready, 1)
            for n in range(4):
                for t in range(TT):
                    dve.wait_ge(bank_drained, unit2(GATE_JOBS + n) + t + 1 + UNITS_CREDIT)
                    e = qkv[:, 4 * n + t, :]
                    step.done(dve.tensor_scalar(e, e, 1.0, None, ALU.add))
                    step.done(dve.reciprocal(e, e))
            for e in range(2):
                for t in range(TT):
                    a = qkv[:, 4 * e + t, :]
                    dve.wait_ge(bank_filled, unit2(BRANCH + e) + t + 1)
                    dve.tensor_tensor(a, a, G[:, t, :], ALU.mult).then_inc(bank_drained, 1)
                for t in range(TT):
                    a, b = qkv[:, 4 * e + t, :], qkv[:, 8 + 4 * e + t, :]
                    dve.wait_ge(bank_filled, unit2(BRANCH + e) + TT + t + 1)
                    dve.tensor_tensor(b, b, G[:, t, :], ALU.mult).then_inc(bank_drained, 1)
                    dve.wait_ge(bank_drained, unit2(BRANCH + e) + TT + t + 1 + UNITS_CREDIT)
                    step.done(dve.tensor_tensor(a, a, b, ALU.add))
                    two_parts(h_hi[:, 4 * e + t, :], h_lo[:, 4 * e + t, :], a).then_inc(split_ready, 1)
            for j in range(2):
                for t in range(TT):
                    dve.wait_ge(bank_filled, unit2(OUT2 + j) + t + 1)
                    n, at = t % 2, slice(512 * j, 512 * j + 512)
                    tmp = win[:, n, PAD:]
                    dve.tensor_tensor(tmp, G[:, t, :], gate_row[:, at], ALU.mult).then_inc(bank_drained, 1)
                    dve.wait_ge(bank_drained, unit2(OUT2 + j) + t + 1 + UNITS_CREDIT)
                    step.done(dve.tensor_tensor(X[:, t, at], X[:, t, at], tmp, ALU.add))
            dve.engine_nop().then_inc(x_scaled, 1)
            dve.wait_ge(gain2_loaded, 16)
            for ins in scaled_rows(2 * DEPTH + 2):
                ins.then_inc(out_ready, 1)

        def second_tensor(pe, three, product, in_rows, in_columns, turn_rows, turn_unit):
            def all_drained(job):
                pe.wait_ge(bank_drained, unit2(job) + UNITS_CREDIT)

            def every_fourth(hi, lo):
                return lambda t, k, s, kk: (hi[:, k, t::STRIDE], lo[:, k, t::STRIDE], w_hi[:, s, kk, :], w_lo[:, s, kk, :])

            pe.wait_ge(c_ready, 1)
            all_drained(ADA)
            for job in range(QKV):
                if job >= 4:
                    all_drained(job - 3)
                for half in range(2):
                    pe.wait_ge(low_ready, piece2(job) + half + 1 + RAW_SLOTS)
                    for kk in range(HALF_K):
                        k = half * HALF_K + kk
                        ins = three(G[:, job % 4, :], cb_hi[:, k, :], cb_lo[:, k, :], w_hi[:, half, kk, :],
                                    w_lo[:, half, kk, :], k == 0, k == KT - 1)
                    if half:
                        ins.then_inc(bank_filled, TT)
                    else:
                        ins.then_inc(half_used, 1)
                if job == 0:
                    pe.wait_ge(hot_loaded, 16)
                    pe.wait_ge(rel_ready, 1)
                for h in range(4 * job, 4 * job + 4):
                    pe.wait_ge(small_drained, SM2_BIAS + h + 1)
                    pe.matmul(S[:, h % 2, 0:SKEW], rel_wide[0:NUM_BUCKETS + 1, h, :], hot[0:NUM_BUCKETS + 1, h // B2_H, :],
                              start=True, stop=True).then_inc(small_filled, 1)
                if 1 <= job <= 4:
                    all_drained(job)
                    turn_unit(TR2_MOD + job - 1, S[:, 2 + (job - 1) % 2, :],
                              lambda t: h_full[:, (job - 1) % 2, P * t:P * t + P])
            pe.wait_ge(xn_ready, 2 * DEPTH + 1)
            pe.wait_ge(small_drained, SM2_BIAS + B2_HEADS + PAIR_CREDIT)
            turn_rows(TR2_NORM, lambda k, t: xn2[:, t, P * k:P * k + P])
            pe.wait_ge(tr_drained, TR2_NORM + KT + PAIR_CREDIT)

            def give_scores(g, i):
                it = item_base(g) + i
                _, m, tile0, tiles, blocks = ITEMS2[g][i]
                pe.wait_ge(score_drained, SC0 + it + 1)
                q = slice(m, None, STRIDE) if g else slice(P * m, P * m + P)
                k = q if g else slice(P * (m + 1 - blocks), P * m + P)
                for n in range(tiles):
                    for e in range(2):
                        at = slice(HD * e, HD * e + HD)
                        dst = own(g, by_tile(g, S[:, 2 * (it % 2) + e, :]), blocks)[:, n, :]
                        ins = pe.matmul(dst, qkv[at, tile0 + n, q], qkv[at, 4 + tile0 + n, k], start=True, stop=True)
                ins.then_inc(score_filled, 1)

            def give_probs(g, i):
                it = item_base(g) + i
                blocks = ITEMS2[g][i][4]
                pe.wait_ge(prob2_ready, it + 1)
                for e in range(2):
                    pe.wait_ge(tr_drained, TR2_ATT + 2 * it + e + 1)
                    for b in range(4):
                        if not g and blocks == 1 and b % 2 == 0:
                            continue
                        ins = pe.transpose(G[:, e, P * b:P * b + P], prob2[:, it % 2, e, P * b:P * b + P], ident)
                    ins.then_inc(tr_filled, 1)

            def give_output(g, i):
                it = item_base(g) + i
                _, m, tile0, tiles, blocks = ITEMS2[g][i]
                pe.wait_ge(tr_drained, TR2_ATT + 2 * it + 2 + PAIR_CREDIT)
                pe.wait_ge(o_drained, OV0 + it + 1)
                for n in range(tiles):
                    for e in range(2):
                        h = 2 * (tile0 + n) + e
                        dst = G[:, 2 + it % 2, HD * (2 * n + e):HD * (2 * n + e) + HD]
                        for b in range(blocks):
                            place = n if g else 2 * n + 2 - blocks + b
                            ins = pe.matmul(dst, probT2[:, it % 2, e, P * place:P * place + P],
                                            qkv[:, 8 + m + 1 - blocks + b, HD * h:HD * h + HD],
                                            start=b == 0, stop=b == blocks - 1)
                ins.then_inc(o_filled, 1)

            for gn, g in enumerate(B2_GROUPS):
                all_drained(QKV + 3 * gn)
                for s in range(3):
                    job = QKV + 3 * gn + s
                    rows = every_fourth(h_hi, h_lo) if g else in_rows(h_hi, h_lo)
                    product(unit2(job), piece2(job), rows if s == 2 else in_columns(h_hi, h_lo))
                all_drained(QKV + 3 * gn + 3)
                pe.wait_ge(small_drained, SM2_BIAS + B2_HEADS + PAIR_CREDIT)
                n = len(ITEMS2[g])
                give_scores(g, 0)
                for i in range(n):
                    if i + 1 < n:
                        give_scores(g, i + 1)
                    give_probs(g, i)
                    if i:
                        give_output(g, i - 1)
                give_output(g, n - 1)
                pe.wait_ge(o_drained, OV0 + item_base(g) + n + PAIR_CREDIT)
            pe.wait_ge(score_drained, SC0 + len(ITEMS2[1]) + len(ITEMS2[2]) + len(ITEMS2[0]) + PAIR_CREDIT)

            product(unit2(Z_JOB), piece2(Z_JOB), in_rows(h_hi, h_lo))
            all_drained(U_JOB)
            product(unit2(U_JOB), piece2(U_JOB), in_columns(h_hi, h_lo))
            pe.wait_ge(z_rows_ready, 1)
            for k in range(4):
                turn_unit(TR2_Z + k, S[:, 2 + k % 2, :], lambda t: qkv[:, 12 + t, P * k:P * k + P])
            all_drained(ZP_JOB)
            product(unit2(ZP_JOB), piece2(ZP_JOB), in_columns(h_hi, h_lo))
            pe.wait_ge(pool_w_loaded, 16)
            for g in range(4):
                pe.wait_ge(pooled_ready, g + 1)
                pe.wait_ge(small_drained, SM2_POOL + g + 1)
                pe.matmul(S[:, g % 2, :], pool_w[:, g, :], qkv[:, 12 + g, :], start=True, stop=True).then_inc(small_filled, 1)
            all_drained(GATE_JOBS)
            for n in range(4):
                product(unit2(GATE_JOBS + n), piece2(GATE_JOBS + n), in_columns(h_hi, h_lo))
            all_drained(BRANCH)
            pe.wait_ge(split_ready, 1)
            for e in range(2):
                for half, (hi, lo) in enumerate(((at_hi, at_lo), (pt_hi, pt_lo))):
                    pe.wait_ge(low_ready, piece2(BRANCH + e) + half + 1 + RAW_SLOTS)
                    for t in range(TT):
                        unit = unit2(BRANCH + e) + TT * half + t
                        pe.wait_ge(bank_drained, unit + 1)
                        for k in range(4):
                            ins = three(G[:, t, :], w_hi[:, half, k, P * t:P * t + P], w_lo[:, half, k, P * t:P * t + P],
                                        hi[:, k, :], lo[:, k, :], k == 0, k == 3)
                        ins.then_inc(bank_filled, 1)
            pe.wait_ge(split_ready, 1 + 2 * TT)
            for j in range(2):
                product(unit2(OUT2 + j), piece2(OUT2 + j), in_rows(h_hi, h_lo))

        def head_rows(p, what, e, t):
            g, hp = PAIRS[p]
            if g == "D":
                return (fox_q if what == "q" else fox_k)[:, t, 2 * hp + e, :]
            if g == "A":
                return (mla_q if what == "q" else mla_k)[:, t, 2 * hp + e, :]
            if g == "B":
                at = P * hp if what == "q" else 2 * P
                return rows_b[:, t, at:at + P]
            at = P * hp + (0 if what == "q" else 2 * P)
            return rows_c[:, t, at:at + P]

        def head_width(p):
            return {"D": FOX_K, "A": MLA_QK, "B": P, "C": P}[PAIRS[p][0]]

        def qk_places(p):
            if PAIRS[p][0] in "DA":
                return [("q", 0, 0), ("q", 1, 1), ("k", 0, 2), ("k", 1, 3)]
            return [("q", 0, 0), ("k", 0, 2)]

        def score_scale(p):
            return (MLA_QK if PAIRS[p][0] == "A" else HD) ** -0.5

        def key_tiles(i):
            p, qt = ITEMS[i]
            return list(range(max(qt - 1, 0), qt + 1)) if PAIRS[p][0] == "B" else list(range(qt + 1))

        def mixed(g, n):
            return {"D": mixT_da, "A": mixT_da, "B": mixT_bc, "C": mixT_bc}[g][:, n + (2 if g in "AC" else 0), :]

        def output_bank(i):
            g, hp = PAIRS[ITEMS[i][0]]
            if g == "B":
                return [G[HD * hp:HD * hp + HD, 2 + i % 2, P * e:P * e + P] for e in range(2)]
            return [G[HD * e:HD * e + HD, 2 + i % 2, 0:P] for e in range(2)]

        def select_at(qt):
            at = sum(n + 1 for n in range(1, qt)) * P
            return select[:, at:at + (qt + 1) * P]

        def chosen(qt):
            at = 2 * sum(n + 1 for n in range(1, qt)) * P
            return select[:].bitcast(BF16)[:, at:at + (qt + 1) * P]

        @block.sync
        def _(sp):
            def cols(w, l, half, c0, c1, k0=0):
                rows = slice((k0 + half * HALF_K) * P, (k0 + (half + 1) * HALF_K) * P)
                return w[bass.ds(l, 1), rows, c0:c1].rearrange("l (k p) n -> p (l k) n", p=P)

            def slot_free(value):
                sp.wait_ge(low_ready, value)
                sp.sem_inc(pieces_asked, 1)

            for t in range(TT):
                sp.dma_start(X[:, t, :], A["x"][0, P * t:P * t + P, :]).then_inc(x_loaded, 16)
            sp.dma_start(masks[:], c_mask[:, :]).then_inc(const_loaded, 16)
            sp.dma_start(rope64[:], c_rope64[:, :, :, :]).then_inc(const_loaded, 16)
            sp.dma_start(rope32[:], c_rope32[:, :, :, :]).then_inc(const_loaded, 16)
            with sp.Fori(0, DEPTH) as l:
                number = l * LAYER_PIECES
                sp.wait_ge(tr_drained, l * LAYER_TR + PAIR_CREDIT)
                sp.sem_inc(pieces_asked, 1)
                for dst, src in (
                    (gain1[:], A["norm1"][bass.ds(l, 1), :].rearrange("l (k p) -> p (l k)", p=P)),
                    (gain2[:], A["norm2"][bass.ds(l, 1), :].rearrange("l (k p) -> p (l k)", p=P)),
                    (q_gain[:], A["mla_q_norm"][bass.ds(l, 1), :].rearrange("l (k p) -> p (l k)", p=P)),
                    (kv_gain[:], A["mla_kv_norm"][bass.ds(l, 1), :].rearrange("l (k p) -> p (l k)", p=P)),
                    (sinks[:], A["swa_sinks"][bass.ds(l, 1), :].broadcast_to([P, HEADS])),
                    (gate_bias[:], A["fox_b_f"][bass.ds(l, 1), :].broadcast_to([P, HEADS])),
                ):
                    sp.dma_start(dst, src, allow_slow_non_contiguous=True).then_inc(params_loaded, 16)
                for c in range(FIRST_GROUP_PIECE):
                    job, half, slot = c // 2, c % 2, c % RAW_SLOTS
                    slot_free(number + (c + 1))
                    if job < PROJ_JOBS:
                        at = 0
                        for c0, c1 in PROJ_PARTS[job]:
                            sp.dma_start(raw[:, slot, :, at:at + c1 - c0], cols(A["w_in"], l, half, c0, c1)
                                         ).then_inc(raw_loaded[slot], 16)
                            at += c1 - c0
                    else:
                        n0 = 512 * (job - OUT_JOB)
                        sp.dma_start(raw[:, slot], cols(A["w_out"], l, half, n0, n0 + 512)
                                     ).then_inc(raw_loaded[slot], 16)
                    if c == 7:
                        sp.dma_start(w_uq[:], A["mla_w_uq"][bass.ds(l, 1), :, :].rearrange("l (k p) n -> p (l k) n", p=P)
                                     ).then_inc(mla_w_loaded, 16)
                        sp.dma_start(w_ukv[:], A["mla_w_ukv"][bass.ds(l, 1), :, :].rearrange("l p n -> p (l n)")
                                     ).then_inc(mla_w_loaded, 16)
                with sp.Fori(0, FFN_GROUPS) as g:
                    for c in range(2 * GROUP_JOBS):
                        job, half, slot = c // 2, c % 2, c % RAW_SLOTS
                        slot_free(number + (g * (2 * GROUP_JOBS) + (FIRST_GROUP_PIECE + c + 1)))
                        n0, kh = 512 * (job % 2), slice(half * HALF_K, (half + 1) * HALF_K)
                        if job < 2:
                            src = A["w_up"].rearrange("l (k p) n -> l p k n", p=P)[
                                bass.ds(l, 1), :, kh, bass.ds(g * D_MODEL + n0, 512)].rearrange("l p k n -> p (l k) n")
                        else:
                            src = A["w_down"].rearrange("l (g k p) n -> l g p k n", p=P, g=FFN_GROUPS)[
                                bass.ds(l, 1), bass.ds(g, 1), :, kh, n0:n0 + 512].rearrange("l g p k n -> p (l g k) n")
                        sp.dma_start(raw[:, slot], src).then_inc(raw_loaded[slot], 16)
            second_loads(sp)

        @block.gpsimd
        def _(pool):
            pool.memset(raw[:, 0:2, :, IDX_W:512], 0.0)
            pool.memset(raw[:, 2:4, :, A_W:512], 0.0).then_inc(slots_cleared, 1)
            pool.sem_inc(low_ready, RAW_SLOTS)

            def split_low(number, c):
                pool.wait_ge(high_ready, number + 1)
                pool.tensor_tensor(w_lo[:, c % SPLIT_SLOTS], raw[:, c % RAW_SLOTS],
                                   w_hi[:, c % SPLIT_SLOTS].bitcast(F32), ALU.subtract).then_inc(low_ready, 1)

            def scale_probs(i, done):
                pool.wait_ge(inv_ready, done + (i + 1))
                part = prob[:, i % 2, :, 0:P * len(key_tiles(i))]
                inverse = inv_sum[:, i % 4, :].unsqueeze(2).broadcast_to([P, 2, part.shape[2]])
                pool.tensor_tensor(part, part, inverse, ALU.mult).then_inc(prob_scaled, 1)

            with pool.Fori(0, DEPTH) as l:
                number = l * LAYER_PIECES
                for c in range(2 * OUT_JOB + 2):
                    split_low(number + c, c)
                for i in range(NI):
                    scale_probs(i, l * NI)
                for c in range(2 * OUT_JOB + 2, FIRST_GROUP_PIECE):
                    split_low(number + c, c)
                with pool.Fori(0, (LAYER_PIECES - FIRST_GROUP_PIECE) // RAW_SLOTS) as i:
                    for c in range(RAW_SLOTS):
                        split_low(number + (i * RAW_SLOTS + (FIRST_GROUP_PIECE + c)), c)
            with pool.Fori(0, (TOTAL_PIECES - PIECE0) // RAW_SLOTS) as i:
                for c in range(RAW_SLOTS):
                    split_low(i * RAW_SLOTS + (PIECE0 + c), c)

        @block.scalar
        def _(act):
            def split_high(c, loads, jobs_before):
                act.wait_ge(raw_loaded[c % RAW_SLOTS], loads)
                if c % 2 == 0:
                    act.wait_ge(half_used, jobs_before)
                else:
                    act.wait_ge(bank_filled, jobs_before * TT)
                act.activation(w_hi[:, c % SPLIT_SLOTS], raw[:, c % RAW_SLOTS], ACT.Copy).then_inc(high_ready, 1)

            def square_sums(norm_no, rows, tile_added=None):
                for t in range(TT):
                    if tile_added:
                        tile_added(t)
                    ins = act.activation(rows[:, t, :], X[:, t, :], ACT.Square, accum_out=sumsq[:, t:t + 1])
                ins.then_inc(sumsq_ready, 1)
                act.wait_ge(var_ready, norm_no + 1)
                act.activation(std[:], var[:], ACT.Sqrt).then_inc(std_ready, 1)

            def high_T(gain, tr):
                for k in range(KT):
                    act.wait_ge(tr_filled, tr + (k + 1))
                    scale = 1.0 if gain is None else gain[:, k:k + 1]
                    act.activation(h_hi[:, k, :], S[:, k % 4, :], ACT.Copy, scale=scale).then_inc(hi_ready, 1)

            act.wait_ge(slots_cleared, 1)
            for c in range(2):
                act.wait_ge(raw_loaded[c], 16)
                act.activation(w_hi[:, c], raw[:, c], ACT.Copy).then_inc(high_ready, 1)
            act.wait_ge(x_loaded, 16 * TT)

            with act.Fori(0, DEPTH) as l:
                unit, tr, small, jobs = l * LAYER_UNITS, l * LAYER_TR, l * LAYER_SM, l * LAYER_JOBS
                item0, turns = l * NI, l * LAYER_TURNS

                def ahead(job, half):
                    c = 2 * (job + 1) + half
                    s = c % RAW_SLOTS
                    upto = loads_upto(c) if job + 1 < FFN_JOB else LOADS_TO_GROUPS[s] + 16
                    split_high(c, l * LAYER_LOADS[s] + upto, jobs + (job + 1))

                def rows_out(job, parts):
                    for t in range(TT):
                        act.wait_ge(bank_filled, unit + (TT * job + t + 1))
                        for dst, src in parts(t):
                            ins = act.activation(dst, src, ACT.Copy)
                        ins.then_inc(bank_drained, 1)

                act.wait_ge(params_loaded, l * 96 + 96)
                square_sums(l * 2, xn, lambda t: act.wait_ge(bank_drained, unit + (UNITS_CREDIT + t + 1 - TT)))
                high_T(gain1, tr + TR_NORM1)

                ahead(JOB_IDX, 0)
                rows_out(JOB_IDX, lambda t: [(rows_idx[:, t, :], G[:, t, 0:IDX_W])])
                ahead(JOB_IDX, 1)
                ahead(JOB_A, 0)
                rows_out(JOB_A, lambda t: [(rows_a[:, t, :], G[:, t, 0:A_W])])
                ahead(JOB_A, 1)
                act.wait_ge(bank_drained, unit + (TT * (JOB_A + 1) + UNITS_CREDIT))
                for t in range(TT):
                    act.activation(select[:, 256 * t:256 * t + 256], rows_a[:, t, 0:256], ACT.Square,
                                   accum_out=m_sumsq[:, t:t + 1])
                for t in range(TT):
                    ins = act.activation(work[:, P * t:P * t + P], rows_a[:, t, 256:384], ACT.Square,
                                         accum_out=m_sumsq[:, TT + t:TT + t + 1])
                ins.then_inc(m_sumsq_ready, 1)
                act.wait_ge(m_var_ready, l + 1)
                act.activation(m_std[:], m_var[:], ACT.Sqrt).then_inc(m_std_ready, 1)
                act.wait_ge(gate_abs_ready, l + 1)
                act.activation(gate_e[:], gate_a[:], ACT.Exp, scale=-1.0).then_inc(gate_exp_ready, 1)
                act.wait_ge(gate_exp_ready, l * 2 + 1)
                act.activation(gate_a[:], gate_e[:], ACT.Ln, bias=1.0).then_inc(gate_exp_ready, 1)

                ahead(JOB_C, 0)
                rows_out(JOB_C, lambda t: [(rows_c[:, t, :], G[:, t, :])])
                ahead(JOB_C, 1)

                def relu_scores(qt):
                    for h in range(8):
                        n = SM_IDX + 8 * (qt - 1) + h
                        act.wait_ge(small_filled, small + (n + 1))
                        act.wait_ge(rel_used, l * 24 + (n + 1))
                        act.activation(rel[:, h % 2, 0:P * (qt + 1)], S[:, n % 2, 0:P * (qt + 1)],
                                       ACT.Relu).then_inc(small_drained, 1)

                relu_scores(1)
                relu_scores(2)
                ahead(JOB_B, 0)
                rows_out(JOB_B, lambda t: [(rows_b[:, t, :], G[:, t, :])])
                ahead(JOB_B, 1)
                relu_scores(3)
                for t in range(TT):
                    n = SM_EXP + 2 * t
                    act.wait_ge(small_filled, small + (n + 1))
                    act.activation(mla_q[:, t].rearrange("p h d -> p (h d)"), S[:, 0, 0:HEADS * MLA_QK],
                                   ACT.Copy).then_inc(small_drained, 1)
                    act.wait_ge(small_filled, small + (n + 2))
                    kv = S[:, 1, :].rearrange("p (h d) -> p h d", h=HEADS)
                    act.activation(mla_k[:, t, :, 0:HD], kv[:, :, 0:HD], ACT.Copy)
                    act.activation(mla_v[:, t, :].rearrange("p (h d) -> p h d", h=HEADS), kv[:, :, HD:2 * HD],
                                   ACT.Copy).then_inc(small_drained, 1)
                ahead(JOB_D, 0)
                rows_out(JOB_D, lambda t: [
                    (fox_q[:, t, :, 0:HD], G[:, t, 0:256].rearrange("p (h d) -> p h d", h=HEADS)),
                    (fox_k[:, t, :, 0:HD], G[:, t, 256:512].rearrange("p (h d) -> p h d", h=HEADS))])
                ahead(JOB_D, 1)
                ahead(JOB_V, 0)
                rows_out(JOB_V, lambda t: [(rows_v[:, t, :], G[:, t, :])])
                ahead(JOB_V, 1)

                def exponentials(i):
                    p, qt = ITEMS[i]
                    width = P * len(key_tiles(i))
                    act.wait_ge(neg_max_ready, item0 + (i + 1))
                    if i >= 2:
                        act.wait_ge(turn_filled, turns + (PT_NO[i - 2, 1] + 1))
                    for e in range(2):
                        if PAIRS[p][0] == "B":
                            h = PAIRS[p][1] + 2 * e
                            act.activation(sink_term[:, i % 4, e:e + 1], sinks[:, h:h + 1], ACT.Exp,
                                           bias=neg_max[:, i % 2, e:e + 1])
                        ins = act.activation(prob[:, i % 2, e, 0:width], S[:, 2 * (i % 2) + e, 0:width], ACT.Exp,
                                             bias=neg_max[:, i % 2, e:e + 1], accum_out=row_sum[:, i % 4, e:e + 1])
                    ins.then_inc(score_drained, 1)

                def take_qk(p):
                    m = head_width(p)
                    for n, (what, _, at) in enumerate(qk_places(p)):
                        no = QK_NO[p, n]
                        if no % 2:
                            act.wait_ge(turn_filled, turns + (no + 1))
                            act.activation(qkT[0:m, p % 2, at, :], G[0:m, 1, :], ACT.Copy,
                                           scale=score_scale(p) if what == "q" else 1.0).then_inc(odd_drained, 1)

                def take_probs(i):
                    width = P * len(key_tiles(i))
                    act.wait_ge(turn_filled, turns + (PT_NO[i, 1] + 1))
                    if i >= 2:
                        act.wait_ge(o_filled, item0 + (i - 1))
                    act.activation(probT[:, i % 2, 1, 0:width], G[:, 1, 0:width], ACT.Copy).then_inc(odd_drained, 1)

                take_qk(0)
                exponentials(0)
                for i in range(NI + 1):
                    p = ITEMS[min(i, NI - 1)][0]
                    if i % TT == 1 and p + 1 < len(PAIRS):
                        take_qk(p + 1)
                    if i + 1 < NI:
                        exponentials(i + 1)
                    if i:
                        take_probs(i - 1)

                act.wait_ge(o_drained, item0 + (NI + PAIR_CREDIT))
                for k in range(KT):
                    act.activation(h_hi[:, k, :], mixed("ABCD"[k // 2], k % 2), ACT.Copy).then_inc(hi_ready, 1)
                for job in (OUT_JOB, OUT_JOB + 1):
                    for half in range(2):
                        ahead(job, half)
                square_sums(l * 2 + 1, xn, lambda t: act.wait_ge(
                    bank_drained, unit + (TT * (OUT_JOB + 1) + t + 1 + UNITS_CREDIT)))
                high_T(gain2, tr + TR_NORM2)

                with act.Fori(0, FFN_GROUPS) as g:
                    unit_g = unit + g * (TT * GROUP_JOBS)
                    hidden = l * LAYER_HIDDEN + g * HIDDEN_UNITS
                    jobs_g = jobs + g * GROUP_JOBS

                    def ahead_g(job, half):
                        c = 2 * (job + 1) + half
                        s = c % RAW_SLOTS
                        if job + 1 < GROUP_JOBS:
                            upto = LOADS_TO_GROUPS[s] + 16 * (c // RAW_SLOTS + 1)
                            split_high(c, l * LAYER_LOADS[s] + (g * GROUP_LOADS + upto), jobs_g + (FFN_JOB + job + 1))
                        else:
                            upto = LOADS_TO_GROUPS[s] + GROUP_LOADS + 16
                            split_high(c, l * LAYER_LOADS[s] + (g * GROUP_LOADS + upto), jobs_g + (FFN_JOB + job + 1))

                    for job in range(2):
                        ahead_g(job, 0)
                        for t in range(TT):
                            n = TT * job + t
                            act.wait_ge(bank_filled, unit_g + (TT * (FFN_JOB + job) + t + 1))
                            act.wait_ge(hidden_split, hidden + (n + 1))
                            act.activation(relu[:, n % 2, :], G[:, t, :], ACT.Relu).then_inc(bank_drained, 1)
                        ahead_g(job, 1)
                    for job in range(2, GROUP_JOBS):
                        ahead_g(job, 0)
                        ahead_g(job, 1)
            second_scalar(act, split_high, square_sums)

        @block.vector
        def _(dve):
            step = Steps(dve, dve_step)
            dve.sem_inc(bank_drained, UNITS_CREDIT)
            for s in (tr_drained, even_drained, odd_drained, small_drained, score_drained, o_drained, rel_used, hidden_split):
                dve.sem_inc(s, PAIR_CREDIT)

            def inverse_root(v, root, r, y):
                step.done(dve.reciprocal(r, root))
                step.done(dve.tensor_tensor(y, r, r, ALU.mult))
                step.done(dve.tensor_tensor(y, y, v, ALU.mult))
                step.done(dve.tensor_scalar(y, y, -0.5, 1.5, ALU.mult, ALU.add))
                step.done(dve.tensor_tensor(r, r, y, ALU.mult))

            def normal_rows(norm_no, rows):
                dve.wait_ge(sumsq_ready, norm_no + 1)
                dve.tensor_scalar(var[:], sumsq[:], 1.0 / D_MODEL, EPS, ALU.mult, ALU.add).then_inc(var_ready, 1)
                dve.wait_ge(std_ready, norm_no + 1)
                inverse_root(var[:], std[:], rstd[:], newton[:])
                for t in range(TT):
                    ins = dve.tensor_scalar(rows[:, t, :], X[:, t, :], rstd[:, t:t + 1], None, ALU.mult)
                return ins

            def low_T(gain, hi_no):
                for k in range(KT):
                    dve.wait_ge(hi_ready, hi_no + (k + 1))
                    scale = 1.0 if gain is None else gain[:, k:k + 1]
                    dve.scalar_tensor_tensor(h_lo[:, k, :], S[:, k % 4, :], scale, h_hi[:, k, :].bitcast(F32),
                                             ALU.mult, ALU.subtract).then_inc(tr_drained, 1)

            def rotate(v, table, heads, half):
                for t in range(TT):
                    x1, x2 = v(t)[:, :, 0:half], v(t)[:, :, half:2 * half]
                    cos = table[:, 0, t, :].unsqueeze(1).broadcast_to([P, heads, half])
                    sin = table[:, 1, t, :].unsqueeze(1).broadcast_to([P, heads, half])
                    a, b, c, d = (turn[:, n, 0:heads * half].rearrange("p (h d) -> p h d", h=heads) for n in range(4))
                    dve.tensor_tensor(a, x1, cos, ALU.mult)
                    dve.tensor_tensor(b, x2, sin, ALU.mult)
                    dve.tensor_tensor(c, x2, cos, ALU.mult)
                    step.done(dve.tensor_tensor(d, x1, sin, ALU.mult))
                    dve.tensor_tensor(x1, a, b, ALU.subtract)
                    step.done(dve.tensor_tensor(x2, c, d, ALU.add))

            dve.wait_ge(x_loaded, 16 * TT)
            dve.wait_ge(const_loaded, 48)
            dve.tensor_copy(ident_few[:], ident)
            dve.tensor_copy(window_few[:], window)

            with dve.Fori(0, DEPTH) as l:
                unit, tr, small, item0 = l * LAYER_UNITS, l * LAYER_TR, l * LAYER_SM, l * NI
                turns, evens = l * LAYER_TURNS, l * HALF_TURNS

                def stored(job):
                    dve.wait_ge(bank_drained, unit + (TT * (job + 1) + UNITS_CREDIT))

                dve.wait_ge(params_loaded, l * 96 + 96)
                normal_rows(l * 2, xn).then_inc(xn_ready, 1)
                low_T(gain1, l * HI_PER_LAYER)

                stored(JOB_IDX)
                rotate(lambda t: rows_idx[:, t, 0:288].rearrange("p (h d) -> p h d", h=9), rope32, 9, 16)
                key = rows_idx[:, :, 256:288].unsqueeze(2).broadcast_to([P, TT, 4, 32])
                dve.tensor_copy(k_idx4[:].rearrange("p t (c d) -> p t c d", c=4), key).then_inc(idx_rows_ready, 1)

                for n in range(3):
                    dve.wait_ge(tr_filled, tr + (TR_IDX + n + 1))
                    dst = qiT[:, n, :] if n < 2 else kiT[:]
                    dve.tensor_copy(dst, S[:, 2 + (TR_IDX + n) % 2, :]).then_inc(tr_drained, 1)
                stored(JOB_A)
                dve.wait_ge(m_sumsq_ready, l + 1)
                dve.tensor_scalar(m_var[:, 0:TT], m_sumsq[:, 0:TT], 1.0 / 256, EPS, ALU.mult, ALU.add)
                dve.tensor_scalar(m_var[:, TT:2 * TT], m_sumsq[:, TT:2 * TT], 1.0 / 128, EPS, ALU.mult,
                                  ALU.add).then_inc(m_var_ready, 1)
                z = rows_a[:, :, 416:420]
                step.done(dve.tensor_tensor(gate_z[:], z, gate_bias[:].unsqueeze(1).broadcast_to([P, TT, HEADS]), ALU.add))
                dve.scalar_tensor_tensor(gate_a[:], gate_z[:], -1.0, gate_z[:], ALU.mult, ALU.max).then_inc(gate_abs_ready, 1)
                dve.wait_ge(m_std_ready, l + 1)
                inverse_root(m_var[:], m_std[:], m_rstd[:], m_newton[:])
                for t in range(TT):
                    dve.tensor_scalar(rows_a[:, t, 0:256], rows_a[:, t, 0:256], m_rstd[:, t:t + 1], None, ALU.mult)
                    ins = dve.tensor_scalar(rows_a[:, t, 256:384], rows_a[:, t, 256:384],
                                            m_rstd[:, TT + t:TT + t + 1], None, ALU.mult)
                ins.then_inc(m_rows_ready, 1)
                rotate(lambda t: rows_a[:, t, 384:416].rearrange("p (h d) -> p h d", h=1), rope32, 1, 16)
                dve.wait_ge(gate_exp_ready, l * 2 + 2)
                dve.scalar_tensor_tensor(log_f[:], gate_z[:], 0.0, gate_a[:], ALU.min, ALU.subtract).then_inc(log_f_ready, 1)

                def index_scores(qt):
                    acc = select_at(qt)
                    for h in range(8):
                        n = SM_IDX + 8 * (qt - 1) + h
                        dve.wait_ge(small_drained, small + (n + 1 + PAIR_CREDIT))
                        w = rows_idx[:, qt, 288 + h:289 + h]
                        part = rel[:, h % 2, 0:P * (qt + 1)]
                        if h == 0:
                            dve.tensor_scalar(acc, part, w, None, ALU.mult).then_inc(rel_used, 1)
                        else:
                            dve.wait_ge(rel_used, l * 24 + (n + PAIR_CREDIT))
                            dve.scalar_tensor_tensor(acc, part, w, acc, ALU.mult, ALU.add).then_inc(rel_used, 1)
                    dve.wait_ge(rel_used, l * 24 + (8 * qt + PAIR_CREDIT))
                    diag = acc[:, P * qt:P * qt + P]
                    step.done(dve.tensor_tensor(diag, diag, causal, ALU.add))

                index_scores(1)
                index_scores(2)
                for n in range(3):
                    dve.wait_ge(tr_filled, tr + (TR_MLA + n + 1))
                    src = S[:, 2 + (TR_MLA + n) % 2, :]
                    if n < 2:
                        dve.tensor_scalar(cqT[:, n, :], src, q_gain[:, n:n + 1], None, ALU.mult).then_inc(tr_drained, 1)
                    else:
                        dve.tensor_scalar(ckvT[:], src, kv_gain[:, 0:1], None, ALU.mult).then_inc(tr_drained, 1)
                stored(JOB_C)
                rotate(lambda t: rows_c[:, t, :].rearrange("p (h d) -> p h d", h=8), rope64, 8, 32)
                index_scores(3)

                def top_keys(qt):
                    for n in range(ROUNDS):
                        top_round(qt, n)
                    mark(qt)

                def top_round(qt, n):
                    left = work[:, 0:P * (qt + 1)]
                    src = left if n else select_at(qt)
                    step.done(dve.max(top8[:], src))
                    step.done(dve.match_replace(left, top8[:], src, TAKEN))

                def mark(qt):
                    left = work[:, 0:P * (qt + 1)]
                    step.done(dve.tensor_scalar(chosen(qt), left, TAKEN * 0.9, NEG, ALU.is_gt, ALU.mult))

                top_keys(1)
                top_keys(2)
                dve.wait_ge(small_drained, small + (LAYER_SM + PAIR_CREDIT))
                rotate(lambda t: mla_q[:, t, :, HD:MLA_QK], rope32, HEADS, 16)
                for t in range(TT):
                    key = rows_a[:, t, 384:416].unsqueeze(1).broadcast_to([P, HEADS, MLA_ROPE])
                    ins = dve.tensor_copy(mla_k[:, t, :, HD:MLA_QK], key)
                step.done(ins)
                for n in range(2):
                    dve.wait_ge(tr_filled, tr + (TR_CUM + n + 1))
                    cum = S[:, 2 + n, 0:2 * HEADS].rearrange("p (t h) -> p t h", t=2)
                    tt = slice(2 * n, 2 * n + 2)
                    dve.memset(fox_q[:, tt, :, HD + 1:HD + 2], 1.0)
                    dve.memset(fox_k[:, tt, :, HD:HD + 1], 1.0)
                    dve.tensor_scalar(fox_q[:, tt, :, HD:HD + 1], cum.unsqueeze(3), HD ** 0.5, None, ALU.mult)
                    dve.tensor_scalar(fox_k[:, tt, :, HD + 1:HD + 2], cum.unsqueeze(3), -(HD ** 0.5), None,
                                      ALU.mult).then_inc(tr_drained, 1)
                stored(JOB_B)
                rotate(lambda t: rows_b[:, t, 0:384].rearrange("p (h d) -> p h d", h=6), rope64, 6, 32)
                dve.engine_nop().then_inc(heads_ready, 1)

                def take_qk(p):
                    m = head_width(p)
                    for n, (what, _, at) in enumerate(qk_places(p)):
                        no = QK_NO[p, n]
                        if no % 2 == 0:
                            dve.wait_ge(turn_filled, turns + (no + 1))
                            dve.tensor_scalar(qkT[0:m, p % 2, at, :], G[0:m, 0, :], score_scale(p) if what == "q" else 1.0,
                                              None, ALU.mult).then_inc(even_drained, 1)

                def row_maxima(i):
                    g, hp = PAIRS[ITEMS[i][0]]
                    width, half = P * len(key_tiles(i)), i % 2
                    dve.wait_ge(score_filled, item0 + (i + 1))
                    ins = dve.tensor_reduce(neg_max[:, half, :], S[:, 2 * half:2 * half + 2, 0:width], AX.X, ALU.max,
                                            negate=True)
                    if g == "B":
                        step.done(ins)
                        ins = dve.scalar_tensor_tensor(neg_max[:, half, :], sinks[:, hp:hp + 3:2], -1.0,
                                                       neg_max[:, half, :], ALU.mult, ALU.min)
                    ins.then_inc(neg_max_ready, 1)

                def invert_sums(i):
                    dve.wait_ge(score_drained, item0 + (i + 1 + PAIR_CREDIT))
                    total = row_sum[:, i % 4, :]
                    if PAIRS[ITEMS[i][0]][0] == "B":
                        step.done(dve.tensor_tensor(total, total, sink_term[:, i % 4, :], ALU.add))
                    dve.reciprocal(inv_sum[:, i % 4, :], total).then_inc(inv_ready, 1)

                def take_probs(i):
                    width = P * len(key_tiles(i))
                    dve.wait_ge(turn_filled, turns + (PT_NO[i, 0] + 1))
                    if i >= 2:
                        dve.wait_ge(o_filled, item0 + (i - 1))
                    dve.tensor_copy(probT[:, i % 2, 0, 0:width], G[:, 0, 0:width]).then_inc(even_drained, 1)

                def take_output(i):
                    p, qt = ITEMS[i]
                    g, hp = PAIRS[p]
                    q = slice(P * qt, P * qt + P)
                    dve.wait_ge(o_filled, item0 + (i + 1))
                    if g == "B":
                        at = slice(HD * hp, HD * hp + HD)
                        dve.tensor_copy(mixT_bc[at, 0:2, q], G[at, 2 + i % 2, 0:2 * P].rearrange("p (e q) -> p e q", e=2)
                                        ).then_inc(o_drained, 1)
                    else:
                        dve.tensor_copy(mixed(g, hp)[:, q], G[:, 2 + i % 2, 0:P]).then_inc(o_drained, 1)

                take_qk(0)
                row_maxima(0)
                for i in range(NI + 2):
                    p = ITEMS[min(i, NI - 1)][0]
                    if i % TT == 1 and p + 1 < len(PAIRS):
                        take_qk(p + 1)
                    if i + 1 < NI:
                        row_maxima(i + 1)
                    if i < NI:
                        invert_sums(i)
                    if 0 < i <= NI:
                        take_probs(i - 1)
                    if i > 1:
                        take_output(i - 2)
                    if i < ROUNDS:
                        top_round(3, i)
                    if i == ROUNDS:
                        mark(3)
                        dve.engine_nop().then_inc(heads_ready, 1)

                for k in range(KT):
                    dve.wait_ge(hi_ready, l * HI_PER_LAYER + (KT + k + 1))
                    dve.tensor_tensor(h_lo[:, k, :], mixed("ABCD"[k // 2], k % 2), h_hi[:, k, :].bitcast(F32),
                                      ALU.subtract).then_inc(mix_split, 1)

                def add_to_x(first_unit, col):
                    for t in range(TT):
                        dve.wait_ge(bank_filled, first_unit + (t + 1))
                        dst = X[:, t, 512 * col:512 * col + 512]
                        dve.tensor_tensor(dst, G[:, t, :], dst, ALU.add).then_inc(bank_drained, 1)

                for j in range(2):
                    add_to_x(unit + TT * (OUT_JOB + j), j)
                normal_rows(l * 2 + 1, xn).then_inc(xn_ready, 1)
                low_T(gain2, l * HI_PER_LAYER + 2 * KT)
                step.restart()

                with dve.Fori(0, FFN_GROUPS) as g:
                    unit_g = unit + g * (TT * GROUP_JOBS)
                    hidden = l * LAYER_HIDDEN + g * HIDDEN_UNITS
                    for n in range(HIDDEN_UNITS):
                        dve.wait_ge(bank_drained, unit_g + (TT * FFN_JOB + n + 1 + UNITS_CREDIT))
                        dve.wait_ge(hidden_split, hidden + (n + PAIR_CREDIT))
                        step.done(dve.tensor_tensor(square[:], relu[:, n % 2, :], relu[:, n % 2, :], ALU.mult))
                        step.done(dve.tensor_copy(u_hi[:, n, :], square[:]))
                        dve.tensor_tensor(u_lo[:, n, :], square[:], u_hi[:, n, :].bitcast(F32),
                                          ALU.subtract).then_inc(hidden_split, 1)
                    for j in range(2):
                        first = unit_g + TT * (FFN_JOB + 2 + j)
                        dve.wait_ge(bank_drained, first + UNITS_CREDIT)
                        add_to_x(first, j)
                    step.restart()
            second_vector(dve, step, inverse_root, normal_rows)

        @block.tensor
        def _(pe):
            def three(dst, a_hi, a_lo, b_hi, b_lo, first, last):
                pe.matmul(dst, a_hi, b_hi, start=first, stop=False)
                pe.matmul(dst, a_hi, b_lo, start=False, stop=False)
                return pe.matmul(dst, a_lo, b_hi, start=False, stop=last)

            def product(unit, number, operands, n=512, inputs_ready=None):
                for half in range(2):
                    if inputs_ready:
                        inputs_ready(half)
                    pe.wait_ge(low_ready, number + (half + 1 + RAW_SLOTS))
                    for t in range(TT):
                        if half == 0:
                            pe.wait_ge(bank_drained, unit + (t + 1))
                        for kk in range(HALF_K):
                            ins = three(G[:, t, 0:n], *operands(t, half * HALF_K + kk, half, kk),
                                        half == 0 and kk == 0, half == 1 and kk == HALF_K - 1)
                        if half:
                            ins.then_inc(bank_filled, 1)
                    if half == 0:
                        ins.then_inc(half_used, 1)

            def in_rows(hi, lo, n=512):
                return lambda t, k, s, kk: (hi[:, k, P * t:P * t + P], lo[:, k, P * t:P * t + P],
                                            w_hi[:, s, kk, 0:n], w_lo[:, s, kk, 0:n])

            def in_columns(hi, lo):
                return lambda t, k, s, kk: (w_hi[:, s, kk, P * t:P * t + P], w_lo[:, s, kk, P * t:P * t + P],
                                            hi[:, k, :], lo[:, k, :])

            def turn_unit(tr, bank, parts):
                pe.wait_ge(tr_drained, tr + 1)
                turn(bank, parts)

            def turn(bank, parts):
                for t in range(TT):
                    src = parts(t)
                    ins = pe.transpose(bank[0:src.shape[1], P * t:P * t + P], src, ident)
                ins.then_inc(tr_filled, 1)

            def turn_rows(tr, rows_of):
                for k in range(KT):
                    pe.wait_ge(tr_drained, tr + (max(k - 3, 0) + PAIR_CREDIT))
                    turn(S[:, k % 4, :], lambda t: rows_of(k, t))

            pe.wait_ge(const_loaded, 48)
            with pe.Fori(0, DEPTH) as l:
                unit, tr, small, item0 = l * LAYER_UNITS, l * LAYER_TR, l * LAYER_SM, l * NI
                number, turns, halves = l * LAYER_PIECES, l * LAYER_TURNS, l * HALF_TURNS

                def project(job):
                    n = PROJ_N[job]
                    product(unit + TT * job, number + 2 * job, in_rows(h_hi, h_lo, n), n)

                pe.wait_ge(xn_ready, l * 2 + 1)
                turn_rows(tr + TR_NORM1, lambda k, t: xn[:, t, P * k:P * k + P])
                pe.wait_ge(tr_drained, tr + (TR_NORM1 + KT + PAIR_CREDIT))
                project(JOB_IDX)
                project(JOB_A)
                pe.wait_ge(idx_rows_ready, l + 1)
                for n in range(3):
                    turn_unit(tr + (TR_IDX + n), S[:, 2 + (TR_IDX + n) % 2, :],
                              lambda t: rows_idx[:, t, P * n:P * n + P] if n < 2 else k_idx4[:, t, :])
                project(JOB_C)

                def index_products(qt):
                    for h in range(8):
                        n = SM_IDX + 8 * (qt - 1) + h
                        at = slice(32 * (h % 4), 32 * (h % 4) + 32)
                        pe.wait_ge(small_drained, small + (n + 1))
                        pe.matmul(S[:, n % 2, 0:P * (qt + 1)], qiT[at, h // 4, P * qt:P * qt + P],
                                  kiT[at, 0:P * (qt + 1)], start=True, stop=True).then_inc(small_filled, 1)

                pe.wait_ge(tr_drained, tr + (TR_IDX + 3 + PAIR_CREDIT))
                index_products(1)
                index_products(2)
                pe.wait_ge(m_rows_ready, l + 1)
                for n in range(3):
                    turn_unit(tr + (TR_MLA + n), S[:, 2 + (TR_MLA + n) % 2, :],
                              lambda t: rows_a[:, t, P * n:P * n + P])
                project(JOB_B)
                index_products(3)
                pe.wait_ge(tr_drained, tr + (TR_MLA + 3 + PAIR_CREDIT))
                pe.wait_ge(mla_w_loaded, l * 32 + 32)
                for t in range(TT):
                    n = SM_EXP + 2 * t
                    pe.wait_ge(small_drained, small + (n + 1))
                    for k in range(2):
                        ins = pe.matmul(S[:, 0, 0:HEADS * MLA_QK], cqT[:, k, P * t:P * t + P], w_uq[:, k, :],
                                        start=k == 0, stop=k == 1)
                    ins.then_inc(small_filled, 1)
                    pe.wait_ge(small_drained, small + (n + 2))
                    pe.matmul(S[:, 1, :], ckvT[:, P * t:P * t + P], w_ukv[:], start=True, stop=True
                              ).then_inc(small_filled, 1)
                project(JOB_D)
                pe.wait_ge(log_f_ready, l + 1)
                for n in range(2):
                    pe.wait_ge(tr_drained, tr + (TR_CUM + n + 1))
                    for t in (2 * n, 2 * n + 1):
                        dst = S[:, 2 + n, HEADS * (t % 2):HEADS * (t % 2) + HEADS]
                        for s in range(t + 1):
                            ins = pe.matmul(dst, upto if s == t else ones, log_f[:, s, :], start=s == 0, stop=s == t)
                    ins.then_inc(tr_filled, 1)
                project(JOB_V)

                pe.wait_ge(bank_drained, unit + (TT * PROJ_JOBS + UNITS_CREDIT))
                pe.wait_ge(small_drained, small + (LAYER_SM + PAIR_CREDIT))
                pe.wait_ge(tr_drained, tr + (TR_NORM2 + PAIR_CREDIT))
                pe.wait_ge(heads_ready, l * 2 + 1)

                def turn_free(no):
                    pe.wait_ge(odd_drained if no % 2 else even_drained, halves + (no // 2 + 2))

                def turns_taken(no):
                    pe.wait_ge(even_drained, halves + (no // 2 + 1 + PAIR_CREDIT))
                    pe.wait_ge(odd_drained, halves + ((no + 1) // 2 + PAIR_CREDIT))

                def give_qk(p):
                    for n, (what, e, _) in enumerate(qk_places(p)):
                        no = QK_NO[p, n]
                        turn_free(no)
                        for t in range(TT):
                            src = head_rows(p, what, e, t)
                            ins = pe.transpose(G[0:src.shape[1], no % 2, P * t:P * t + P], src, ident)
                        ins.then_inc(turn_filled, 1)

                def give_scores(i):
                    p, qt = ITEMS[i]
                    g = PAIRS[p][0]
                    tiles = key_tiles(i)
                    if qt == 0:
                        turns_taken(QK_NO[p, qk_units(p) - 1])
                    pe.wait_ge(score_drained, item0 + (i + 1))
                    for e in range(2):
                        if g in "DA":
                            at, q, k = slice(0, head_width(p)), e, 2 + e
                        else:
                            at, q, k = slice(HD * e, HD * e + HD), 0, 2
                        bank = S[:, 2 * (i % 2) + e, 0:P * len(tiles)]
                        pe.matmul(bank, qkT[at, p % 2, q, P * qt:P * qt + P],
                                  qkT[at, p % 2, k, P * tiles[0]:P * (qt + 1)], start=True, stop=False)
                        if g == "C" and qt == TT - 1:
                            pe.wait_ge(heads_ready, l * 2 + 2)
                        mask = chosen(qt) if g == "C" and qt else window_few[:, 0 if g == "B" and qt else P:2 * P]
                        ins = pe.matmul(bank[:, P * len(tiles) - mask.shape[1]:], ident_few[:], mask,
                                        start=False, stop=True)
                    ins.then_inc(score_filled, 1)

                def give_probs(i):
                    pe.wait_ge(prob_scaled, item0 + (i + 1))
                    for e in range(2):
                        no = PT_NO[i, e]
                        turn_free(no)
                        for b in range(len(key_tiles(i))):
                            ins = pe.transpose(G[:, no % 2, P * b:P * b + P], prob[:, i % 2, e, P * b:P * b + P], ident)
                        ins.then_inc(turn_filled, 1)

                def values(p, e, kb):
                    g, hp = PAIRS[p]
                    if g == "A":
                        return mla_v[:, kb, HD * (2 * hp + e):HD * (2 * hp + e) + HD]
                    if g == "B":
                        return rows_b[:, kb, 384 + HD * e:384 + HD * e + HD]
                    at = HD * (2 * hp + e) + (256 if g == "D" else 0)
                    return rows_v[:, kb, at:at + HD]

                def give_output(i):
                    p = ITEMS[i][0]
                    tiles = key_tiles(i)
                    turns_taken(PT_NO[i, 1])
                    pe.wait_ge(o_drained, item0 + (i + 1))
                    for e, dst in enumerate(output_bank(i)):
                        for b, kb in enumerate(tiles):
                            ins = pe.matmul(dst, values(p, e, kb), probT[:, i % 2, e, P * b:P * b + P],
                                            start=b == 0, stop=b == len(tiles) - 1)
                    ins.then_inc(o_filled, 1)

                give_qk(0)
                give_scores(0)
                for i in range(NI + 2):
                    p = ITEMS[min(i, NI - 1)][0]
                    if i % TT == 1 and p + 1 < len(PAIRS):
                        give_qk(p + 1)
                    if i + 1 < NI:
                        give_scores(i + 1)
                    if 0 < i <= NI:
                        give_probs(i - 1)
                    if i > 1:
                        give_output(i - 2)

                pe.wait_ge(o_drained, item0 + (NI + PAIR_CREDIT))
                for j in range(2):
                    product(unit + TT * (OUT_JOB + j), number + 2 * (OUT_JOB + j), in_rows(h_hi, h_lo),
                            inputs_ready=lambda half: pe.wait_ge(mix_split, l * KT + HALF_K * (1 + (half or j))))

                pe.wait_ge(xn_ready, l * 2 + 2)
                turn_rows(tr + TR_NORM2, lambda k, t: xn[:, t, P * k:P * k + P])
                with pe.Fori(0, FFN_GROUPS) as g:
                    pe.wait_ge(tr_drained, tr + (TR_NORM2 + KT + PAIR_CREDIT))
                    unit_g = unit + (g * (TT * GROUP_JOBS) + TT * FFN_JOB)
                    number_g = number + (g * (2 * GROUP_JOBS) + FIRST_GROUP_PIECE)
                    pe.wait_ge(bank_drained, unit_g + UNITS_CREDIT)
                    for j in range(2):
                        product(unit_g + TT * j, number_g + 2 * j, in_columns(h_hi, h_lo))
                    hidden = l * LAYER_HIDDEN + g * HIDDEN_UNITS
                    for j in range(2, GROUP_JOBS):
                        product(unit_g + TT * j, number_g + 2 * j, in_rows(u_hi, u_lo), inputs_ready=lambda half:
                                pe.wait_ge(hidden_split, hidden + (HALF_K * (1 + half) + PAIR_CREDIT)))
            second_tensor(pe, three, product, in_rows, in_columns, turn_rows, turn_unit)


_INS = ['x', 'norm1', 'w_in', 'mla_q_norm', 'mla_kv_norm', 'mla_w_uq', 'mla_w_ukv', 'swa_sinks', 'fox_b_f', 'w_out',
        'norm2', 'w_up', 'w_down', 'final_norm', 'c_2', 'norm_g_2', 'w_ada_2', 'b_ada_2', 'w_in_2', 'pool_w_2',
        'pool_scale_2', 'w_attn_br_2', 'w_pool_br_2', 'w_out_2', 'rel_bias_2', 'final_g_2']
_OUTS = [((1, 512, 1024), 'float32')]


def kernel(**inputs):
    import numpy as _np
    import concourse.bacc as _bacc
    from concourse import mybir as _mybir
    from concourse.bass_utils import run_bass_kernel_spmd as _run

    nc = _bacc.Bacc("TRN2", target_bir_lowering=False, num_devices=1)
    arrays, ins, outs = {}, {}, []
    for name in _INS:
        a = _np.ascontiguousarray(inputs[name])
        arrays[f"in_{name}_dram"] = a
        ins[name] = nc.dram_tensor(f"in_{name}_dram", a.shape, _mybir.dt.from_np(a.dtype), kind="ExternalInput").ap()
    for i, (shape, dtype) in enumerate(_OUTS):
        dt = _mybir.dt.from_np(_np.dtype(dtype))
        outs.append(nc.dram_tensor(f"out_{i}_dram", shape, dt, kind="ExternalOutput").ap())
    build(nc, ins, outs[0])
    r = _run(nc, [arrays], core_ids=[0])
    got = tuple(r.results[0][f"out_{i}_dram"] for i in range(len(_OUTS)))
    return got[0]
```
